# Optimizing a Trainium2 kernel written in Bass

```python
import math
import jax, jax.numpy as jnp
from jax import lax
import numpy as np

D_MODEL = 1024
BATCH = 1
SEQ = 1024
DEPTH = 1

RMS_EPS = 1e-6
MASK_VALUE = -1e30

NSA_HEADS = 8
NSA_KV_GROUPS = 2
NSA_HEAD_DIM = 64
NSA_CMP_BLOCK = 32
NSA_CMP_STRIDE = 16
NSA_CMP_HIDDEN = 128
NSA_SEL_BLOCK = 64
NSA_TOP_N = 16
NSA_WINDOW = 512
NSA_Q_BLOCK = 64
NSA_FORCE_BONUS = 1e3
NSA_Q_W = NSA_HEADS * NSA_HEAD_DIM
NSA_KV_W = NSA_KV_GROUPS * NSA_HEAD_DIM
NSA_GATE_W = NSA_HEADS * 3

SSM_HEADS = 16
SSM_HEAD_DIM = 64
SSM_INNER = SSM_HEADS * SSM_HEAD_DIM
SSM_GROUPS = 2
SSM_STATE = 128
SSM_CONV = 4
SSM_CHUNK = 256
SSM_CONV_DIM = SSM_INNER + 2 * SSM_GROUPS * SSM_STATE
SSM_DT_MIN = 0.001
SSM_DT_MAX = 0.1

MOE_GROUPS = 4
MOE_EXPERTS_PER_GROUP = 8
MOE_EXPERTS = MOE_GROUPS * MOE_EXPERTS_PER_GROUP
MOE_TOP_K = 2
MOE_HIDDEN = 256
MOE_ROW_BLOCK = 256

PLE_DIM = 256

IN_SIZES = (NSA_Q_W, NSA_KV_W, NSA_KV_W, NSA_KV_W, NSA_KV_W, NSA_KV_W, NSA_KV_W, NSA_GATE_W,
            SSM_INNER, SSM_CONV_DIM, SSM_HEADS, 2 * D_MODEL)
IN_W = sum(IN_SIZES)

kernel_name = 'nsa_ssd_hier_moe_hybrid_block'

def rmsnorm(x, gain):
    xf = x.astype(jnp.float32)
    y = xf * lax.rsqrt(jnp.mean(xf * xf, axis=-1, keepdims=True) + RMS_EPS)
    return (y * gain.astype(jnp.float32)).astype(x.dtype)

def _compress(k, pos, w1, w2):
    b, s, g, hd = k.shape
    r = NSA_CMP_BLOCK // NSA_CMP_STRIDE
    n_cmp = s // NSA_CMP_STRIDE - r + 1
    chunks = k.reshape(b, s // NSA_CMP_STRIDE, NSA_CMP_STRIDE, g, hd)
    blocks = jnp.concatenate([chunks[:, j:j + n_cmp] for j in range(r)], axis=2)
    blocks = blocks + pos[None, None, :, None, :]
    flat = blocks.transpose(0, 3, 1, 2, 4).reshape(b, g, n_cmp, NSA_CMP_BLOCK * hd)
    return jax.nn.silu(flat @ w1) @ w2

def nsa_mixer(q, kc, vc, ks, vs, kw, vw, gate_logits, q_gain, kc_gain, ks_gain, kw_gain,
              pos_k, w1_k, w2_k, pos_v, w1_v, w2_v):
    b, s = q.shape[:2]
    G, E, hd = NSA_KV_GROUPS, NSA_HEADS // NSA_KV_GROUPS, NSA_HEAD_DIM
    QB, SB, W = NSA_Q_BLOCK, NSA_SEL_BLOCK, NSA_WINDOW
    nqb, n_sel = s // QB, s // SB
    n_top = min(NSA_TOP_N, n_sel)
    scale = hd ** -0.5

    q = rmsnorm(q.reshape(b, s, G, E, hd), q_gain)
    to_g = lambda t: t.transpose(0, 2, 1, 3)
    k_cmp = rmsnorm(_compress(kc, pos_k, w1_k, w2_k), kc_gain)
    v_cmp = _compress(vc, pos_v, w1_v, w2_v)
    n_cmp = k_cmp.shape[2]
    k_sel = to_g(rmsnorm(ks, ks_gain)).reshape(b, G, n_sel, SB, hd)
    v_sel = to_g(vs).reshape(b, G, n_sel, SB, hd)
    pad = ((0, 0), (0, 0), (W, 0), (0, 0))
    k_win = jnp.pad(to_g(rmsnorm(kw, kw_gain)), pad)
    v_win = jnp.pad(to_g(vw), pad)

    cmp_start = jnp.arange(n_cmp) * NSA_CMP_STRIDE
    cmp_end = cmp_start + NSA_CMP_BLOCK - 1
    sel_idx = jnp.arange(n_sel)
    overlap = ((cmp_start[:, None] <= sel_idx[None, :] * SB + SB - 1)
               & (cmp_end[:, None] >= sel_idx[None, :] * SB)).astype(jnp.float32)
    bi = jnp.arange(b)[:, None, None, None]
    gi = jnp.arange(G)[None, :, None, None]

    q_blk = q.reshape(b, nqb, QB, G, E, hd).transpose(1, 0, 3, 4, 2, 5)
    g_blk = jax.nn.sigmoid(gate_logits.reshape(b, nqb, QB, G, E, 3)).transpose(1, 0, 3, 4, 2, 5)

    def block(args):
        qq, gg, i = args
        t = i * QB + jnp.arange(QB)
        s_c = jnp.einsum('bgeqd,bgcd->bgeqc', qq, k_cmp).astype(jnp.float32) * scale
        m_c = cmp_end[None, :] <= t[:, None]
        p_c = jax.nn.softmax(jnp.where(m_c, s_c, MASK_VALUE), axis=-1) * jnp.any(m_c, axis=-1)[:, None]
        o_c = jnp.einsum('bgeqc,bgcd->bgeqd', p_c.astype(v_cmp.dtype), v_cmp)
        imp = jnp.einsum('bgeqc,cj->bgqj', p_c, overlap)
        cur = t // SB
        j = sel_idx[None, :]
        forced = (j == 0) | (j == cur[:, None]) | (j == cur[:, None] - 1)
        valid = j * SB <= t[:, None]
        imp = jnp.where(valid, imp + NSA_FORCE_BONUS * forced, -jnp.inf)
        _, top = lax.top_k(imp, n_top)
        top_ok = jnp.take_along_axis(jnp.broadcast_to(valid, imp.shape), top, axis=-1)
        kg = k_sel[bi, gi, top]
        vg = v_sel[bi, gi, top]
        kpos = top[..., None] * SB + jnp.arange(SB)
        m_s = (kpos <= t[:, None, None]) & top_ok[..., None]
        s_s = jnp.einsum('bgeqd,bgqnkd->bgeqnk', qq, kg).astype(jnp.float32) * scale
        s_s = jnp.where(m_s[:, :, None], s_s, MASK_VALUE).reshape(b, G, E, QB, n_top * SB)
        p_s = jax.nn.softmax(s_s, axis=-1).reshape(b, G, E, QB, n_top, SB)
        o_s = jnp.einsum('bgeqnk,bgqnkd->bgeqd', p_s.astype(vg.dtype), vg)
        kw_b = lax.dynamic_slice_in_dim(k_win, i * QB, QB + W, axis=2)
        vw_b = lax.dynamic_slice_in_dim(v_win, i * QB, QB + W, axis=2)
        wpos = i * QB - W + jnp.arange(QB + W)
        dist = t[:, None] - wpos[None, :]
        m_w = (wpos[None, :] >= 0) & (dist >= 0) & (dist < W)
        s_w = jnp.einsum('bgeqd,bgkd->bgeqk', qq, kw_b).astype(jnp.float32) * scale
        p_w = jax.nn.softmax(jnp.where(m_w, s_w, MASK_VALUE), axis=-1)
        o_w = jnp.einsum('bgeqk,bgkd->bgeqd', p_w.astype(vw_b.dtype), vw_b)
        return gg[..., 0:1] * o_c + gg[..., 1:2] * o_s + gg[..., 2:3] * o_w

    out = lax.map(block, (q_blk, g_blk, jnp.arange(nqb)))
    return out.transpose(1, 0, 4, 2, 3, 5).reshape(b, s, NSA_HEADS * hd)

def ssd_mixer(z, xbc, dt_raw, conv_w, conv_b, dt_bias, a_log, d_skip, norm_gain):
    b, s, cdim = xbc.shape
    G, E, P, N = SSM_GROUPS, SSM_HEADS // SSM_GROUPS, SSM_HEAD_DIM, SSM_STATE
    f32 = jnp.float32
    Lc = math.gcd(SSM_CHUNK, s)
    nc = s // Lc
    conv = lax.conv_general_dilated(xbc, conv_w[:, None, :], window_strides=(1,),
                                    padding=[(SSM_CONV - 1, 0)],
                                    dimension_numbers=('NWC', 'WIO', 'NWC'),
                                    feature_group_count=cdim)
    xbc = jax.nn.silu(conv + conv_b)
    xs, bm, cm = jnp.split(xbc, [SSM_INNER, SSM_INNER + G * N], axis=-1)
    x = xs.reshape(b, s, G, E, P)
    dt = jax.nn.softplus(dt_raw.astype(f32) + dt_bias.astype(f32)).reshape(b, s, G, E)
    a = -jnp.exp(a_log.astype(f32)).reshape(G, E)
    xd = (x.astype(f32) * dt[..., None]).reshape(b, nc, Lc, G, E, P)
    bc = bm.astype(f32).reshape(b, nc, Lc, G, N)
    cc = cm.astype(f32).reshape(b, nc, Lc, G, N)
    a_cs = jnp.cumsum((dt * a).reshape(b, nc, Lc, G, E).transpose(0, 3, 4, 1, 2), axis=-1)
    causal = jnp.tril(jnp.ones((Lc, Lc), dtype=bool))
    seg = jnp.exp(jnp.where(causal, a_cs[..., :, None] - a_cs[..., None, :], -jnp.inf))
    cb = jnp.einsum('bclgn,bcsgn->bgcls', cc, bc)
    y_diag = jnp.einsum('bgecls,bcsgep->bclgep', cb[:, :, None] * seg, xd)
    to_cl = lambda t: t.transpose(0, 3, 4, 1, 2)
    decay_in = to_cl(jnp.exp(a_cs[..., -1:] - a_cs))
    states = jnp.einsum('bclgn,bclgep->bcgepn', bc, xd * decay_in[..., None])
    chunk_decay = jnp.exp(a_cs[..., -1])

    def step(h, inp):
        st, dec = inp
        return h * dec[..., None, None] + st, h

    _, prev = lax.scan(step, jnp.zeros((b, G, E, P, N), f32),
                       (jnp.moveaxis(states, 1, 0), jnp.moveaxis(chunk_decay, -1, 0)))
    prev = jnp.moveaxis(prev, 0, 1)
    y_off = jnp.einsum('bclgn,bcgepn->bclgep', cc, prev) * to_cl(jnp.exp(a_cs))[..., None]
    y = (y_diag + y_off).reshape(b, s, G, E, P) + x.astype(f32) * d_skip.astype(f32).reshape(G, E, 1)
    gw = SSM_INNER // G
    y = y.reshape(b, s, G, gw) * jax.nn.silu(z.astype(f32)).reshape(b, s, G, gw)
    y = rmsnorm(y, norm_gain.reshape(G, gw))
    return y.reshape(b, s, SSM_INNER).astype(z.dtype)

def hier_moe(h, w_group, b_group, w_expert, b_expert, w_gate, w_up, w_down):
    b, s, d = h.shape
    n = b * s
    hf = h.reshape(n, d)
    grp_p = jax.nn.softmax((hf @ w_group + b_group).astype(jnp.float32), axis=-1)
    grp_w, grp_i = lax.top_k(grp_p, 1)
    e_logits = (hf @ w_expert + b_expert).astype(jnp.float32).reshape(n, MOE_GROUPS, MOE_EXPERTS_PER_GROUP)
    e_logits = jnp.take_along_axis(e_logits, grp_i[:, :, None], axis=1)[:, 0]
    top_p, top_i = lax.top_k(jax.nn.softmax(e_logits, axis=-1), MOE_TOP_K)
    weights = grp_w * top_p / jnp.sum(top_p, axis=-1, keepdims=True)
    experts = grp_i * MOE_EXPERTS_PER_GROUP + top_i

    e_flat = experts.reshape(-1)
    w_flat = weights.reshape(-1)
    tok = jnp.repeat(jnp.arange(n, dtype=jnp.int32), MOE_TOP_K)
    order = jnp.argsort(e_flat)
    se, st, sw = e_flat[order], tok[order], w_flat[order]
    counts = jnp.zeros((MOE_EXPERTS,), jnp.int32).at[e_flat].add(1)
    starts = jnp.cumsum(counts) - counts
    padded = (counts + MOE_ROW_BLOCK - 1) // MOE_ROW_BLOCK * MOE_ROW_BLOCK
    pend = jnp.cumsum(padded)
    pstarts = pend - padded
    dest = pstarts[se] + jnp.arange(n * MOE_TOP_K, dtype=jnp.int32) - starts[se]
    n_blocks = -(-(n * MOE_TOP_K) // MOE_ROW_BLOCK) + MOE_EXPERTS
    slot_tok = jnp.full((n_blocks * MOE_ROW_BLOCK,), n, jnp.int32).at[dest].set(st)
    slot_w = jnp.zeros((n_blocks * MOE_ROW_BLOCK,), jnp.float32).at[dest].set(sw)
    block_e = jnp.clip(jnp.searchsorted(pend, jnp.arange(n_blocks) * MOE_ROW_BLOCK, side='right'),
                       0, MOE_EXPERTS - 1)
    x_pad = jnp.concatenate([hf, jnp.zeros((1, d), hf.dtype)], axis=0)
    x_slots = x_pad[slot_tok].reshape(n_blocks, MOE_ROW_BLOCK, d)

    def expert_rows(args):
        xb, e = args
        return (jax.nn.silu(xb @ w_gate[e]) * (xb @ w_up[e])) @ w_down[e]

    out = lax.map(expert_rows, (x_slots, block_e)).reshape(-1, d)
    out = out * slot_w[:, None].astype(out.dtype)
    y = jnp.zeros((n + 1, d), out.dtype).at[slot_tok].add(out)[:n]
    return y.reshape(b, s, d)

def setup_inputs(seed: int = 0) -> dict:
    key = jax.random.key(seed)
    ks = iter(jax.random.split(key, 48))
    L = DEPTH
    hd = NSA_HEAD_DIM

    def nrm(shape, scale):
        return jax.random.normal(next(ks), shape, jnp.float32) * scale

    def gain(n):
        return 1.0 + nrm((L, n), 0.05)

    x = nrm((BATCH, SEQ, D_MODEL), 1.0)
    p = nrm((DEPTH, BATCH, SEQ, PLE_DIM), 1.0)
    dt = jnp.exp(jax.random.uniform(next(ks), (L, SSM_HEADS), jnp.float32,
                                    minval=math.log(SSM_DT_MIN), maxval=math.log(SSM_DT_MAX)))
    dt_bias = dt + jnp.log(-jnp.expm1(-dt))
    a_log = jnp.log(jax.random.uniform(next(ks), (L, SSM_HEADS), jnp.float32, minval=1.0, maxval=16.0))
    cl = NSA_CMP_BLOCK * hd
    return {
        'x': x,
        'p': p,
        'mix_norm': gain(D_MODEL),
        'w_in': nrm((L, D_MODEL, IN_W), D_MODEL ** -0.5),
        'nsa_q_gain': gain(hd),
        'nsa_kc_gain': gain(hd),
        'nsa_ks_gain': gain(hd),
        'nsa_kw_gain': gain(hd),
        'cmp_pos_k': nrm((L, NSA_CMP_BLOCK, hd), 0.1),
        'cmp_w1_k': nrm((L, cl, NSA_CMP_HIDDEN), cl ** -0.5),
        'cmp_w2_k': nrm((L, NSA_CMP_HIDDEN, hd), NSA_CMP_HIDDEN ** -0.5),
        'cmp_pos_v': nrm((L, NSA_CMP_BLOCK, hd), 0.1),
        'cmp_w1_v': nrm((L, cl, NSA_CMP_HIDDEN), cl ** -0.5),
        'cmp_w2_v': nrm((L, NSA_CMP_HIDDEN, hd), NSA_CMP_HIDDEN ** -0.5),
        'ssm_conv_w': nrm((L, SSM_CONV, SSM_CONV_DIM), SSM_CONV ** -0.5),
        'ssm_conv_b': nrm((L, SSM_CONV_DIM), 0.02),
        'ssm_dt_bias': dt_bias,
        'ssm_a_log': a_log,
        'ssm_d': 1.0 + nrm((L, SSM_HEADS), 0.1),
        'ssm_norm': gain(SSM_INNER),
        'w_branch_a': nrm((L, NSA_Q_W, D_MODEL), NSA_Q_W ** -0.5),
        'w_branch_b': nrm((L, SSM_INNER, D_MODEL), SSM_INNER ** -0.5),
        'w_out': nrm((L, D_MODEL, D_MODEL), D_MODEL ** -0.5),
        'moe_norm': gain(D_MODEL),
        'moe_w_group': nrm((L, D_MODEL, MOE_GROUPS), D_MODEL ** -0.5),
        'moe_b_group': nrm((L, MOE_GROUPS), 0.01),
        'moe_w_expert': nrm((L, D_MODEL, MOE_EXPERTS), D_MODEL ** -0.5),
        'moe_b_expert': nrm((L, MOE_EXPERTS), 0.01),
        'moe_w_gate': nrm((L, MOE_EXPERTS, D_MODEL, MOE_HIDDEN), D_MODEL ** -0.5),
        'moe_w_up': nrm((L, MOE_EXPERTS, D_MODEL, MOE_HIDDEN), D_MODEL ** -0.5),
        'moe_w_down': nrm((L, MOE_EXPERTS, MOE_HIDDEN, D_MODEL), MOE_HIDDEN ** -0.5),
        'ple_norm': gain(D_MODEL),
        'ple_w_gate': nrm((L, D_MODEL, D_MODEL), D_MODEL ** -0.5),
        'ple_w_proj': nrm((L, PLE_DIM, D_MODEL), PLE_DIM ** -0.5),
    }

def reference(x, p, mix_norm, w_in, nsa_q_gain, nsa_kc_gain, nsa_ks_gain, nsa_kw_gain,
              cmp_pos_k, cmp_w1_k, cmp_w2_k, cmp_pos_v, cmp_w1_v, cmp_w2_v,
              ssm_conv_w, ssm_conv_b, ssm_dt_bias, ssm_a_log, ssm_d, ssm_norm,
              w_branch_a, w_branch_b, w_out,
              moe_norm, moe_w_group, moe_b_group, moe_w_expert, moe_b_expert,
              moe_w_gate, moe_w_up, moe_w_down,
              ple_norm, ple_w_gate, ple_w_proj):
    b, s, _ = x.shape
    offsets = np.cumsum(IN_SIZES)[:-1].tolist()
    for i in range(DEPTH):
        h = rmsnorm(x, mix_norm[i])
        proj = h @ w_in[i]
        (q, kc, vc, ks, vs, kw, vw, nsa_g, z, xbc, dt_raw, br_g) = jnp.split(proj, offsets, axis=-1)
        kv = lambda t: t.reshape(b, s, NSA_KV_GROUPS, NSA_HEAD_DIM)
        y_a = nsa_mixer(q.reshape(b, s, NSA_HEADS, NSA_HEAD_DIM), kv(kc), kv(vc), kv(ks), kv(vs),
                        kv(kw), kv(vw), nsa_g, nsa_q_gain[i], nsa_kc_gain[i], nsa_ks_gain[i],
                        nsa_kw_gain[i], cmp_pos_k[i], cmp_w1_k[i], cmp_w2_k[i],
                        cmp_pos_v[i], cmp_w1_v[i], cmp_w2_v[i])
        y_b = ssd_mixer(z, xbc, dt_raw, ssm_conv_w[i], ssm_conv_b[i], ssm_dt_bias[i],
                        ssm_a_log[i], ssm_d[i], ssm_norm[i])
        gate_a, gate_b = jnp.split(jax.nn.sigmoid(br_g), 2, axis=-1)
        merged = gate_a * (y_a @ w_branch_a[i]) + gate_b * (y_b @ w_branch_b[i])
        x = x + merged @ w_out[i]
        h = rmsnorm(x, moe_norm[i])
        x = x + hier_moe(h, moe_w_group[i], moe_b_group[i], moe_w_expert[i], moe_b_expert[i],
                         moe_w_gate[i], moe_w_up[i], moe_w_down[i])
        h = rmsnorm(x, ple_norm[i])
        x = x + jax.nn.sigmoid(h @ ple_w_gate[i]) * (p[i] @ ple_w_proj[i])
    return x


_drawn_inputs = setup_inputs


def setup_inputs(seed=0):
    import zlib

    import numpy as np

    out = dict(_drawn_inputs(seed))
    spreads = {}
    factors = {'nsa_q_gain': 7.65,
     'nsa_kc_gain': 8.0,
     'nsa_ks_gain': 8.0,
     'nsa_kw_gain': 8.0,
     'cmp_pos_k': 8.0,
     'moe_b_group': 3.994,
     'moe_b_expert': 4.677,
     'ple_norm': 7.05}
    for name, (base, spread) in spreads.items():
        noise = np.random.default_rng([zlib.crc32(name.encode()), seed]).standard_normal(out[name].shape)
        drawn = base * np.exp(spread * noise) if base else spread * noise
        out[name] = __import__('jax').numpy.asarray(drawn.astype(out[name].dtype))
    for name, factor in factors.items():
        out[name] = (out[name] * factor).astype(out[name].dtype)
    return out
```

```python
import concourse.bass as bass
from concourse import mybir

F32 = mybir.dt.float32
BF16 = mybir.dt.bfloat16
I32 = mybir.dt.int32
U32 = mybir.dt.uint32
ALU = mybir.AluOpType
ACT = mybir.ActivationFunctionType
AX = mybir.AxisListType

P = 128
D = 1024
S = 1024
KD = D // P
NT = S // P
HALF = 512
EPS = 1e-6
MASK = -1e30

HEADS, GROUPS, HD = 8, 2, 64
E = HEADS // GROUPS
Q_W, KV_W, GATE_W = HEADS * HD, GROUPS * HD, HEADS * 3
NSA_W = Q_W + 6 * KV_W + GATE_W
SSM_HEADS, SSM_P, SSM_G, SSM_N = 16, 64, 2, 128
INNER = SSM_HEADS * SSM_P
GW = INNER // SSM_G
CONV_DIM = INNER + 2 * SSM_G * SSM_N
CONV = 4
MC = CONV_DIM // P
Z0 = NSA_W
XBC0 = Z0 + INNER
DT0 = XBC0 + CONV_DIM
BR0 = DT0 + SSM_HEADS
CMP_STRIDE, CMP_BLOCK, CMP_HIDDEN = 16, 32, 128
NCMP = S // CMP_STRIDE - 1
WINDOW = 512
EXPERTS, MGROUPS, PER_GROUP, MOE_H = 32, 4, 8, 256
ROUTES = MGROUPS + EXPERTS
EXTRA = 2 * S // P
BLOCKS = EXPERTS + EXTRA
SLOTS = BLOCKS * P
PLE = 256


class Chain:

    def __init__(self, eng, sem):
        self.eng, self.sem, self.start, self.base, self.n = eng, sem, 0, 0, 0

    def link(self, ins):
        ins.then_inc(self.sem, 1)
        self.n += 1
        self.eng.wait_ge(self.sem, self.base + self.n)

    def enter(self, i, per):
        self.start += self.n
        self.n, self.base = 0, self.start + i * per

    def leave(self, passes, per):
        assert self.n == per, (self.n, per)
        self.start += passes * per
        self.base, self.n = self.start, 0


class Machine:

    def __init__(self, nc, ins, out):
        self.nc, self.i, self.out, self.sems = nc, ins, out, []
        self.psum = nc.alloc_psum_tensor("banks", [P, 8 * HALF], F32)
        self.ps = [self.psum[:, b * HALF:(b + 1) * HALF] for b in range(8)]
        self.top = nc.sbuf_base + (-nc.sbuf_base) % 64
        self.end = nc.sbuf_usable_end

    def sb(self, name, shape, dt=F32):
        size = 2 if dt == BF16 else 4
        for n in shape[1:]:
            size *= n
        t = self.nc.alloc_sbuf_tensor_at(name, shape, dt, offset=self.top)
        self.top += size + (-size) % 64
        assert self.top <= self.end, (name, self.top, self.end)
        return t

    def sem(self, name):
        self.sems.append(self.nc.alloc_semaphore(name=name))
        return self.sems[-1]

    def chains(self, nc, phase):
        return Steps(self, phase)

    def renew_semaphores(self):
        self.nc.clear_and_free_semaphores(self.sems)
        self.sems = []
        self.nc.all_engine_barrier()


class Steps(dict):

    def __init__(self, m, phase):
        super().__init__()
        self.m, self.phase = m, phase

    def __missing__(self, engine):
        self[engine] = self.m.sem(f"{self.phase}_{engine}_step")
        return self[engine]


def constants(nc, m):
    m.ident = m.sb("ident", [P, P])
    m.ones = m.sb("ones", [P, P])
    m.tri_le = m.sb("tri_le", [P, P])
    m.tri_lt = m.sb("tri_lt", [P, P])
    m.identb = m.sb("identb", [P, P], BF16)
    m.mask_future = m.sb("mask_future", [P, P], BF16)
    m.mask_far = m.sb("mask_far", [P, P], BF16)
    m.mask_past = m.sb("mask_past", [P, P], BF16)
    m.mask_cmp = m.sb("mask_cmp", [P, NT, NCMP + 1], BF16)
    m.any_cmp = m.sb("any_cmp", [P, 1])
    m.small = m.sb("small", [P, 2, P])
    m.mix_gain = m.sb("mix_gain", [P, KD])
    m.moe_gain = m.sb("moe_gain", [P, KD])
    m.ple_gain = m.sb("ple_gain", [P, KD])
    m.ssm_gain = m.sb("ssm_gain", [P, KD])
    m.qk_gain = m.sb("qk_gain", [P, 4])
    m.dt_bias = m.sb("dt_bias", [P, SSM_HEADS])
    m.neg_a = m.sb("neg_a", [P, SSM_HEADS])
    m.d_skip = m.sb("d_skip", [P, SSM_HEADS])
    m.route_bias = m.sb("route_bias", [P, ROUTES])
    m.gate_scale = m.sb("gate_scale", [P, NT, GATE_W])
    m.junk = m.sb("junk", [P, 2, D])
    m.sumsq = m.sb("sumsq", [P, NT])
    m.rms = m.sb("rms", [P, NT])
    m.rstd = m.sb("rstd", [P, NT])
    made, loaded, turned = m.sem("const_made"), m.sem("const_loaded"), m.sem("const_turned")
    ch = m.chains(nc, "const")
    i = m.i
    m.const_dmas = 0
    with nc.Block() as block:
        @block.gpsimd
        def _(pool):
            c = Chain(pool, ch["pool"])

            def tri(t, op, cm, step, base, inside, outside, shape=(P,)):
                c.link(nc.gpsimd.memset(t, inside))
                c.link(nc.gpsimd.affine_select(out=t, in_=t, compare_op=op, fill=outside, base=base,
                                               pattern=[[step, P]], channel_multiplier=cm))
            tri(m.ident[:, :], ALU.not_equal, 1, -1, 0, 0.0, 1.0)
            tri(m.identb[:, :], ALU.not_equal, 1, -1, 0, 0.0, 1.0)
            tri(m.tri_le[:, :], ALU.is_ge, -1, 1, 0, 1.0, 0.0)
            tri(m.tri_lt[:, :], ALU.is_gt, -1, 1, 0, 1.0, 0.0)
            tri(m.mask_future[:, :], ALU.is_ge, 1, -1, 0, 0.0, MASK)
            tri(m.mask_far[:, :], ALU.is_gt, -1, 1, 0, 0.0, MASK)
            tri(m.mask_past[:, :], ALU.is_ge, -1, 1, 0, 0.0, MASK)
            c.link(nc.gpsimd.memset(m.ones[:, :], 1.0))
            c.link(nc.gpsimd.memset(m.mask_cmp[:, :, :], 0.0))
            c.link(nc.gpsimd.affine_select(out=m.mask_cmp[:, :, :], in_=m.mask_cmp[:, :, :], compare_op=ALU.is_ge,
                                           fill=MASK, base=-(CMP_BLOCK - 1), channel_multiplier=1,
                                           pattern=[[P, NT], [-CMP_STRIDE, NCMP + 1]]))
            c.link(nc.gpsimd.memset(m.any_cmp[:, :], 1.0))
            nc.gpsimd.affine_select(out=m.any_cmp[:, :], in_=m.any_cmp[:, :], compare_op=ALU.is_ge, fill=0.0,
                                    base=-(CMP_BLOCK - 1), channel_multiplier=1, pattern=[[0, 1]]).then_inc(made, 1)

        @block.sync
        def _(sp):
            def load(dst, src):
                sp.dma_start(dst, src).then_inc(loaded, 16)
                m.const_dmas += 1
            load(m.small[0:CONV * MC, 0, :], i["ssm_conv_w"][0].rearrange("j (m p) -> (j m) p", p=P))
            load(m.small[CONV * MC:(CONV + 1) * MC, 0, :], i["ssm_conv_b"][0].rearrange("(m p) -> m p", p=P))
            for t, name in ((m.mix_gain, "mix_norm"), (m.moe_gain, "moe_norm"), (m.ple_gain, "ple_norm"),
                            (m.ssm_gain, "ssm_norm")):
                load(t[:, :], i[name][0].rearrange("(p k) -> p k", k=KD))
            for n, name in enumerate(("nsa_q_gain", "nsa_kc_gain", "nsa_ks_gain", "nsa_kw_gain")):
                for g in range(GROUPS):
                    load(m.qk_gain[g * HD:(g + 1) * HD, n:n + 1], i[name][0].rearrange("(d a) -> d a", a=1))
            for t, name in ((m.dt_bias, "ssm_dt_bias"), (m.neg_a, "ssm_a_log"), (m.d_skip, "ssm_d")):
                load(t[:, :], i[name].partition_broadcast(P).rearrange("p a h -> p (a h)"))
            load(m.route_bias[:, 0:MGROUPS], i["moe_b_group"].partition_broadcast(P).rearrange("p a h -> p (a h)"))
            load(m.route_bias[:, MGROUPS:], i["moe_b_expert"].partition_broadcast(P).rearrange("p a h -> p (a h)"))

        @block.tensor
        def _(pe):
            pe.wait_ge(made, 1)
            pe.wait_ge(loaded, 16 * m.const_dmas)
            n = (CONV + 1) * MC
            nc.tensor.transpose(m.ps[0][:, 0:n], m.small[0:n, 0, :], m.ident[0:n, 0:n]).then_inc(turned, 1)

        @block.scalar
        def _(act):
            c = Chain(act, ch["act"])
            act.wait_ge(loaded, 16 * m.const_dmas)
            c.link(nc.scalar.activation(m.neg_a[:, :], m.neg_a[:, :], ACT.Exp))
            c.link(nc.scalar.mul(m.qk_gain[:, 0:1], m.qk_gain[:, 0:1], HD ** -0.5))
            nc.scalar.mul(m.neg_a[:, :], m.neg_a[:, :], -1.0).then_inc(turned, 1)

        @block.vector
        def _(dve):
            dve.wait_ge(turned, 2)
            n = (CONV + 1) * MC
            nc.vector.tensor_copy(m.small[:, 1, 0:n], m.ps[0][:, 0:n]).then_inc(turned, 1)
    m.conv_w = m.small[:, 1, 0:CONV * MC].rearrange("p (j m) -> p j m", j=CONV)
    m.conv_b = m.small[:, 1, CONV * MC:(CONV + 1) * MC]


def norm_transpose(nc, m, name, x, gain, xn, hT, load=None, store=None):
    here = [m.sem(f"{name}_x_loaded{t}") for t in range(NT)]
    squared, rooted, root, normed, turned = (m.sem(f"{name}_{n}") for n in
                                             ("squared", "mean_made", "rooted", "normed", "turned"))
    read = [m.sem(f"{name}_act_read"), m.sem(f"{name}_dve_read")]
    stored = m.sem(f"{name}_stored")
    ch = m.chains(nc, name)
    NG = 2 * KD
    with nc.Block() as block:
        @block.sync
        def _(sp):
            if load is not None:
                for t in range(NT):
                    sp.dma_start(x[:, t, :], load[t * P:(t + 1) * P, :]).then_inc(here[t], 16)
            if store is not None:
                for t in range(NT):
                    sp.wait_ge(normed, t + 1)
                    sp.dma_start(store[t * P:(t + 1) * P, :], xn[:, t, :]).then_inc(stored, 16)
                sp.wait_ge(stored, 16 * NT)

        @block.scalar
        def _(act):
            c = Chain(act, ch["act"])
            for t in range(NT):
                if load is not None:
                    act.wait_ge(here[t], 16)
                c.link(nc.scalar.activation(m.junk[:, 0, :], x[:, t, :], ACT.Square,
                                            accum_out=m.sumsq[:, t:t + 1]))
            nc.scalar.mul(m.rms[:, :], m.sumsq[:, :], 1.0 / D).then_inc(squared, 1)
            act.wait_ge(rooted, 1)
            nc.scalar.activation(m.rms[:, :], m.rms[:, :], ACT.Sqrt).then_inc(root, 1)
            for n in range(0, NG, 2):
                act.wait_ge(turned, n + 1)
                k = n % KD
                h = n // KD
                nc.scalar.activation(hT[:, k, h * HALF:(h + 1) * HALF], m.ps[n % 4][:, :], ACT.Copy,
                                     scale=gain[:, k:k + 1]).then_inc(read[0], 1)

        @block.vector
        def _(dve):
            c = Chain(dve, ch["dve"])
            dve.wait_ge(squared, 1)
            nc.vector.tensor_scalar_add(m.rms[:, :], m.rms[:, :], EPS).then_inc(rooted, 1)
            dve.wait_ge(root, 1)
            c.link(nc.vector.reciprocal(m.rstd[:, :], m.rms[:, :]))
            for t in range(NT):
                nc.vector.tensor_scalar(xn[:, t, :], x[:, t, :], m.rstd[:, t:t + 1], None,
                                        ALU.mult).then_inc(normed, 1)
            for n in range(1, NG, 2):
                dve.wait_ge(turned, n + 1)
                k = n % KD
                h = n // KD
                nc.vector.tensor_scalar(hT[:, k, h * HALF:(h + 1) * HALF], m.ps[n % 4][:, :], gain[:, k:k + 1],
                                        None, ALU.mult).then_inc(read[1], 1)

        @block.tensor
        def _(pe):
            for n in range(NG):
                k, h = n % KD, n // KD
                pe.wait_ge(normed, 4 * (h + 1))
                if n >= 4:
                    pe.wait_ge(read[n % 2], (n - 4) // 2 + 1)
                for j in range(4):
                    t = 4 * h + j
                    mm = nc.tensor.transpose(m.ps[n % 4][:, j * P:(j + 1) * P], xn[:, t, k:D:KD], m.ident[:, :])
                mm.then_inc(turned, 1)


def project_conv(nc, m):
    RING, BODY = 3, 6
    LOOPS = MC // BODY
    W = m.sb("conv_wring", [P, RING, KD, P])
    pre = m.sb("conv_pre", [P, 2, CONV - 1 + S])
    here = [m.sem(f"conv_w_loaded{r}") for r in range(RING)]
    done, used, free, pre_free = (m.sem(f"conv_{n}") for n in
                                          ("products_done", "w_free", "bank_free", "pre_free"))
    ch = m.chains(nc, "conv")
    with nc.Block() as block:
        @block.sync
        def _(sp):
            wv = m.i["w_in"][0][:, XBC0:XBC0 + CONV_DIM].rearrange("(p k) (m c) -> m p k c", k=KD, c=P)
            sp.sem_inc(used, RING)
            with sp.Fori(0, MC // RING) as it:
                for r in range(RING):
                    sp.wait_ge(used, RING * it + r + 1)
                    sp.dma_start(W[:, r, :, :], wv[RING * it + r, :, :, :]).then_inc(here[r], 16)

        @block.tensor
        def _(pe):
            pe.sem_inc(free, 4)
            with pe.Fori(0, LOOPS) as it:
                for r in range(BODY):
                    pe.wait_ge(here[r % RING], 16 * (2 * it + r // RING + 1))
                    for h in range(2):
                        pe.wait_ge(free, 2 * BODY * it + 2 * r + h + 1)
                        b = (2 * r + h) % 4
                        for k in range(KD):
                            mm = nc.tensor.matmul(m.ps[b][:, :], W[:, r % RING, k, :],
                                                  m.hT[:, k, h * HALF:(h + 1) * HALF],
                                                  start=(k == 0), stop=(k == KD - 1))
                        mm.then_inc(done, 1)
                    nc.tensor.matmul(m.ps[7][0:1, 0:1], m.ident[:, 0:1], m.ident[:, 0:1], start=True,
                                     stop=True).then_inc(used, 1)

        @block.scalar
        def _(act):
            with act.Fori(0, LOOPS) as it:
                for r in range(BODY):
                    act.wait_ge(pre_free, BODY * it + r + 1)
                    for h in range(2):
                        act.wait_ge(done, 2 * BODY * it + 2 * r + h + 1)
                        nc.scalar.copy(pre[:, r % 2, CONV - 1 + h * HALF:CONV - 1 + (h + 1) * HALF],
                                       m.ps[(2 * r + h) % 4][:, :]).then_inc(free, 1)

        @block.vector
        def _(dve):
            c = Chain(dve, ch["dve"])
            for r in range(2):
                c.link(dve.memset(pre[:, r, 0:CONV - 1], 0.0))
            dve.sem_inc(pre_free, 2)
            with dve.Fori(0, LOOPS) as it:
                c.enter(it, BODY * (CONV - 1))
                for r in range(BODY):
                    dve.wait_ge(free, 2 * BODY * it + 2 * r + 2 + 4)
                    out = m.xbc[:, BODY * it + r, :]
                    for j in range(CONV):
                        src = pre[:, r % 2, j:j + S]
                        w = m.conv_w[:, j, bass.ds(BODY * it + r, 1)]
                        if j == 0:
                            ins = nc.vector.tensor_scalar(out, src, w, None, ALU.mult)
                        else:
                            ins = nc.vector.scalar_tensor_tensor(out=out, in0=src, scalar=w, in1=out,
                                                                 op0=ALU.mult, op1=ALU.add)
                        if j < CONV - 1:
                            c.link(ins)
                        else:
                            ins.then_inc(pre_free, 1)
                c.leave(LOOPS, BODY * (CONV - 1))


def time_steps(nc, m):
    W = m.sb("dt_w", [P, KD, SSM_HEADS])
    raw, mag, ln = (m.sb(f"dt_{n}", [P, NT, SSM_HEADS]) for n in ("raw", "mag", "ln"))
    here, done, sized, logged = (m.sem(f"dt_{n}") for n in ("w_loaded", "products_done", "sized", "logged"))
    ch = m.chains(nc, "dt")
    per_head = [P, NT, SSM_HEADS]
    with nc.Block() as block:
        @block.sync
        def _(sp):
            sp.dma_start(m.wz[:, :, :], m.i["w_in"][0][:, Z0:Z0 + INNER].rearrange("(p k) n -> p k n", k=KD))\
                .then_inc(m.wz_loaded, 16)
            sp.dma_start(W[:, :, :], m.i["w_in"][0][:, DT0:DT0 + SSM_HEADS].rearrange("(p k) n -> p k n", k=KD))\
                .then_inc(here, 16)

        @block.tensor
        def _(pe):
            pe.wait_ge(here, 16)
            for t in range(NT):
                for k in range(KD):
                    mm = nc.tensor.matmul(m.ps[0][:, t * SSM_HEADS:(t + 1) * SSM_HEADS],
                                          m.hT[:, k, t * P:(t + 1) * P], W[:, k, :],
                                          start=(k == 0), stop=(k == KD - 1))
            mm.then_inc(done, 1)

        @block.vector
        def _(dve):
            c = Chain(dve, ch["dve"])
            dve.wait_ge(done, 1)
            c.link(nc.vector.tensor_tensor(raw[:, :, :], m.ps[0][:, 0:NT * SSM_HEADS].rearrange("p (t h) -> p t h", t=NT),
                                           m.dt_bias[:, :].unsqueeze(1).to_broadcast(per_head), ALU.add))
            nc.vector.scalar_tensor_tensor(out=mag[:, :, :], in0=raw[:, :, :], scalar=-1.0, in1=raw[:, :, :],
                                           op0=ALU.mult, op1=ALU.max).then_inc(sized, 1)
            dve.wait_ge(logged, 1)
            c.link(nc.vector.scalar_tensor_tensor(out=m.dt[:, :, :], in0=raw[:, :, :], scalar=0.0,
                                                  in1=ln[:, :, :], op0=ALU.max, op1=ALU.add))
            c.link(nc.vector.tensor_tensor(m.adt[:, :, :], m.dt[:, :, :],
                                           m.neg_a[:, :].unsqueeze(1).to_broadcast(per_head), ALU.mult))

        @block.scalar
        def _(act):
            c = Chain(act, ch["act"])
            act.wait_ge(sized, 1)
            c.link(nc.scalar.activation(mag[:, :, :], mag[:, :, :], ACT.Exp, scale=-1.0))
            nc.scalar.activation(ln[:, :, :], mag[:, :, :], ACT.Ln, bias=1.0).then_inc(logged, 1)


def ssd(nc, m):
    xc = m.sb("ssd_xc", [P, MC, P])
    hc = m.sb("ssd_hc", [P, KD, P])
    adt_c = m.sb("ssd_adt_c", [P, SSM_HEADS])
    xtok = m.sb("ssd_xtok", [P, INNER])
    btok = m.sb("ssd_btok", [P, SSM_G * SSM_N])
    xd, xdd, xskip, y1, zs = (m.sb(f"ssd_{n}", [P, INNER]) for n in ("xd", "xdd", "xskip", "y1", "zs"))
    seg = m.sb("ssd_seg", [P, SSM_HEADS, P])
    state = m.sb("ssd_state", [P, INNER])
    sums = m.sb("ssd_sums", [P, 3, SSM_HEADS])
    exps = m.sb("ssd_exps", [P, 3, SSM_HEADS])
    neg = m.sb("ssd_neg", [P, SSM_HEADS])
    dtin = m.sb("ssd_dtin", [P, SSM_HEADS])
    names = ("xc_ready", "xc_free", "x_turned", "xtok_ready", "xtok_used", "small_done", "cb_done", "sums_ready",
             "exps_ready", "adt_ready", "seg_done", "seg_exp", "mt_ready", "z_done", "z_ready", "hc_ready",
             "yoff_done", "yoff_read", "ydiag_done", "ydiag_read", "xd_ready", "xdd_ready", "dtin_ready",
             "st_done", "st_read", "decayed", "skip_ready", "gated")
    q = {n: m.sem(f"ssd_{n}") for n in names}
    ch = m.chains(nc, "ssd")
    CB0 = INNER // P
    HG = SSM_HEADS // SSM_G

    def heads(ap):
        return ap.rearrange("p (h d) -> p h d", d=SSM_P)

    def spread(ap, n):
        return ap.unsqueeze(2).to_broadcast([P, n, SSM_P])

    with nc.Block() as block:
        @block.scalar
        def _(act):
            c = Chain(act, ch["act"])
            with act.Fori(0, NT) as i:
                act.wait_ge(q["yoff_done"], i)
                for j in range(MC):
                    nc.scalar.activation(xc[:, j, :], m.xbc[:, j, bass.ds(i * P, P)], ACT.Silu,
                                         bias=m.conv_b[:, j:j + 1]).then_inc(q["xc_ready"], 1)
                act.wait_ge(q["xtok_used"], 3 * i)
                for h in range(2):
                    act.wait_ge(q["x_turned"], 2 * i + h + 1)
                    nc.scalar.copy(xtok[:, h * HALF:(h + 1) * HALF], m.ps[h][:, :]).then_inc(q["xtok_ready"], 1)
                act.wait_ge(q["sums_ready"], i + 1)
                act.wait_ge(q["yoff_read"], 2 * i)
                act.wait_ge(q["decayed"], i)
                nc.scalar.activation(exps[:, :, :], sums[:, :, :], ACT.Exp).then_inc(q["exps_ready"], 1)
                act.wait_ge(q["ydiag_done"], 2 * i)
                for r in range(4):
                    act.wait_ge(q["seg_done"], 4 * i + r + 1)
                    for hh in range(4):
                        h = 4 * r + hh
                        ins = nc.scalar.activation(seg[:, h, :], m.ps[4 + r % 2][:, hh * P:(hh + 1) * P], ACT.Exp,
                                                   bias=neg[:, h:h + 1])
                    ins.then_inc(q["seg_exp"], 1)
                act.wait_ge(q["gated"], i)
                for h in range(2):
                    act.wait_ge(q["z_done"], 2 * i + h + 1)
                    nc.scalar.activation(zs[:, h * HALF:(h + 1) * HALF], m.ps[h][:, :],
                                         ACT.Silu).then_inc(q["z_ready"], 1)

        @block.gpsimd
        def _(pool):
            c = Chain(pool, ch["pool"])
            nc.gpsimd.memset(state[:, :], 0.0).then_inc(q["st_read"], 2)
            with pool.Fori(0, NT) as i:
                pool.wait_ge(q["z_done"], 2 * i)
                nc.gpsimd.tensor_copy(hc[:, :, :], m.hT[:, :, bass.ds(i * P, P)]).then_inc(q["hc_ready"], 1)
                pool.wait_ge(q["xtok_ready"], 2 * i + 2)
                pool.wait_ge(q["gated"], i)
                nc.gpsimd.tensor_tensor(heads(xskip[:, :]), heads(xtok[:, :]), spread(m.d_skip[:, :], SSM_HEADS),
                                        ALU.mult).then_inc(q["xtok_used"], 1)
                pool.wait_ge(q["dtin_ready"], i + 1)
                pool.wait_ge(q["st_done"], 2 * i)
                nc.gpsimd.tensor_tensor(heads(xdd[:, :]), heads(xtok[:, :]), spread(dtin[:, :], SSM_HEADS),
                                        ALU.mult).then_inc(q["xtok_used"], 1)
                pool.wait_ge(q["yoff_done"], i + 1)
                nc.gpsimd.tensor_tensor(heads(state[:, :]), heads(state[:, :]),
                                        spread(exps[:, 1, :], SSM_HEADS), ALU.mult).then_inc(q["decayed"], 1)

        @block.vector
        def _(dve):
            c = Chain(dve, ch["dve"])
            PER = 4
            with dve.Fori(0, NT) as i:
                c.enter(i, PER)
                dve.wait_ge(q["seg_done"], 4 * i)
                nc.vector.tensor_copy(adt_c[:, :], m.adt[:, bass.ds(i, 1), :].rearrange("p a h -> p (a h)"))\
                    .then_inc(q["adt_ready"], 1)
                dve.wait_ge(q["small_done"], i + 1)
                dve.wait_ge(q["st_done"], 2 * i)
                c.link(nc.vector.tensor_copy(btok[:, :], m.ps[2][:, 0:256]))
                c.link(nc.vector.tensor_copy(sums[:, 0:2, :], m.ps[2][:, 256:288].rearrange("p (a h) -> p a h", a=2)))
                c.link(nc.vector.tensor_scalar(neg[:, :], sums[:, 0, :], -1.0, None, ALU.mult))
                nc.vector.tensor_tensor(sums[:, 2, :], sums[:, 1, :], sums[:, 0, :],
                                        ALU.subtract).then_inc(q["sums_ready"], 1)
                dve.wait_ge(q["exps_ready"], i + 1)
                dt_c = m.dt[:, bass.ds(i, 1), :].rearrange("p a h -> p (a h)")
                dve.wait_ge(q["xtok_used"], 3 * i + 1)
                nc.vector.tensor_tensor(dtin[:, :], dt_c, exps[:, 2, :], ALU.mult).then_inc(q["dtin_ready"], 1)
                dve.wait_ge(q["xtok_ready"], 2 * i + 2)
                dve.wait_ge(q["ydiag_done"], 2 * i)
                nc.vector.tensor_tensor(heads(xd[:, :]), heads(xtok[:, :]), spread(dt_c, SSM_HEADS),
                                        ALU.mult).then_inc(q["xtok_used"], 1)
                dve.wait_ge(q["cb_done"], i + 1)
                for r in range(4):
                    g = r // 2
                    dve.wait_ge(q["seg_exp"], 4 * i + r + 1)
                    part = seg[:, 4 * r:4 * r + 4, :]
                    nc.vector.tensor_tensor(part, part, m.ps[3][:, g * P:(g + 1) * P].unsqueeze(1)
                                            .to_broadcast([P, 4, P]), ALU.mult).then_inc(q["mt_ready"], 1)
                for g in range(2):
                    part = slice(g * HALF, (g + 1) * HALF)
                    dve.wait_ge(q["yoff_done"], i + 1)
                    ins = nc.vector.tensor_tensor(heads(y1[:, part]), heads(m.ps[6 + g][:, :]),
                                                  spread(exps[:, 0, g * HG:(g + 1) * HG], HG), ALU.mult)
                    ins.then_inc(q["yoff_read"], 1)
                for g in range(2):
                    part = slice(g * HALF, (g + 1) * HALF)
                    dve.wait_ge(q["yoff_read"], 2 * i + 2)
                    dve.wait_ge(q["ydiag_done"], 2 * i + g + 1)
                    nc.vector.tensor_tensor(y1[:, part], y1[:, part], m.ps[4 + g][:, :],
                                            ALU.add).then_inc(q["ydiag_read"], 1)
                dve.wait_ge(q["decayed"], i + 1)
                for g in range(2):
                    part = slice(g * HALF, (g + 1) * HALF)
                    dve.wait_ge(q["st_done"], 2 * i + g + 1)
                    nc.vector.tensor_tensor(state[:, part], state[:, part], m.ps[2 + g][:, :],
                                            ALU.add).then_inc(q["st_read"], 1)
                dve.wait_ge(q["ydiag_read"], 2 * i + 2)
                c.link(nc.vector.tensor_tensor(y1[:, :], y1[:, :], xskip[:, :], ALU.add))
                dve.wait_ge(q["z_ready"], 2 * i + 2)
                nc.vector.tensor_tensor(m.y[:, bass.ds(i, 1), :].rearrange("p a n -> p (a n)"), y1[:, :], zs[:, :],
                                        ALU.mult).then_inc(q["gated"], 1)
                c.leave(NT, PER)

        @block.tensor
        def _(pe):
            pe.wait_ge(m.wz_loaded, 16)
            with pe.Fori(0, NT) as i:
                pe.wait_ge(q["z_ready"], 2 * i)
                for h in range(2):
                    pe.wait_ge(q["xc_ready"], MC * i + 4 * h + 4)
                    for j in range(4):
                        mm = nc.tensor.transpose(m.ps[h][:, j * P:(j + 1) * P], xc[:, 4 * h + j, :], m.ident[:, :])
                    mm.then_inc(q["x_turned"], 1)
                pe.wait_ge(q["st_read"], 2 * i + 2)
                pe.wait_ge(q["xc_ready"], MC * i + MC)
                for g in range(SSM_G):
                    nc.tensor.transpose(m.ps[2][:, g * P:(g + 1) * P], xc[:, CB0 + g, :], m.ident[:, :])
                pe.wait_ge(q["adt_ready"], i + 1)
                nc.tensor.matmul(m.ps[2][:, 256:272], m.tri_le[:, :], adt_c[:, :], start=True, stop=True)
                nc.tensor.matmul(m.ps[2][:, 272:288], m.ones[:, :], adt_c[:, :], start=True,
                                 stop=True).then_inc(q["small_done"], 1)
                for g in range(SSM_G):
                    mm = nc.tensor.matmul(m.ps[3][:, g * P:(g + 1) * P], xc[:, CB0 + g, :], xc[:, CB0 + 2 + g, :],
                                          start=True, stop=True)
                mm.then_inc(q["cb_done"], 1)
                for r in range(4):
                    if r < 2:
                        pe.wait_ge(q["ydiag_read"], 2 * i)
                    else:
                        pe.wait_ge(q["seg_exp"], 4 * i + r - 1)
                    for hh in range(4):
                        h = 4 * r + hh
                        dst = m.ps[4 + r % 2][:, hh * P:(hh + 1) * P]
                        nc.tensor.matmul(dst, adt_c[:, h:h + 1].to_broadcast([P, P]), m.tri_le[:, :],
                                         start=True, stop=False)
                        mm = nc.tensor.matmul(dst, m.identb[:, :], m.mask_past[:, :], start=False, stop=True)
                    mm.then_inc(q["seg_done"], 1)
                pe.wait_ge(q["hc_ready"], i + 1)
                for h in range(2):
                    pe.wait_ge(q["xtok_ready"], 2 * i + h + 1)
                    for k in range(KD):
                        mm = nc.tensor.matmul(m.ps[h][:, :], hc[:, k, :], m.wz[:, k, h * HALF:(h + 1) * HALF],
                                              start=(k == 0), stop=(k == KD - 1))
                    mm.then_inc(q["z_done"], 1)
                pe.wait_ge(q["yoff_read"], 2 * i)
                for g in range(SSM_G):
                    mm = nc.tensor.matmul(m.ps[6 + g][:, :], xc[:, CB0 + 2 + g, :],
                                          state[:, g * HALF:(g + 1) * HALF], start=True, stop=True)
                mm.then_inc(q["yoff_done"], 1)
                pe.wait_ge(q["xtok_used"], 3 * i + 3)
                for h in range(SSM_HEADS):
                    if h % HG == 0:
                        pe.wait_ge(q["mt_ready"], 4 * i + 3 + h // HG)
                    mm = nc.tensor.matmul(m.ps[4 + h // HG][:, (h % HG) * SSM_P:(h % HG + 1) * SSM_P], seg[:, h, :],
                                          xd[:, h * SSM_P:(h + 1) * SSM_P], start=True, stop=True)
                    if h % HG == HG - 1:
                        mm.then_inc(q["ydiag_done"], 1)
                for g in range(SSM_G):
                    nc.tensor.matmul(m.ps[2 + g][:, :], btok[:, g * P:(g + 1) * P], xdd[:, g * HALF:(g + 1) * HALF],
                                     start=True, stop=True).then_inc(q["st_done"], 1)


def group_norm(nc, m, ybT):
    squared, mean, root, normed, turned = (m.sem(f"gn_{n}") for n in
                                           ("squared", "mean_made", "rooted", "normed", "turned"))
    read = [m.sem("gn_act_read"), m.sem("gn_dve_read")]
    ch = m.chains(nc, "gn")
    ss = m.sb("gn_ss", [P, NT * SSM_G])
    rs = m.sb("gn_rs", [P, NT * SSM_G])
    NG = 2 * KD
    with nc.Block() as block:
        @block.scalar
        def _(act):
            c = Chain(act, ch["act"])
            for n in range(NT * SSM_G):
                t, g = divmod(n, SSM_G)
                c.link(nc.scalar.activation(m.junk[:, 0, 0:GW], m.y[:, t, g * GW:(g + 1) * GW], ACT.Square,
                                            accum_out=ss[:, n:n + 1]))
            nc.scalar.mul(ss[:, :], ss[:, :], 1.0 / GW).then_inc(squared, 1)
            act.wait_ge(mean, 1)
            nc.scalar.activation(ss[:, :], ss[:, :], ACT.Sqrt).then_inc(root, 1)
            for n in range(0, NG, 2):
                act.wait_ge(turned, n + 1)
                k, h = n % KD, n // KD
                nc.scalar.activation(ybT[:, k, h * HALF:(h + 1) * HALF], m.ps[n % 4][:, :], ACT.Copy,
                                     scale=m.ssm_gain[:, k:k + 1]).then_inc(read[0], 1)

        @block.vector
        def _(dve):
            c = Chain(dve, ch["dve"])
            dve.wait_ge(squared, 1)
            nc.vector.tensor_scalar_add(ss[:, :], ss[:, :], EPS).then_inc(mean, 1)
            dve.wait_ge(root, 1)
            c.link(nc.vector.reciprocal(rs[:, :], ss[:, :]))
            for n in range(NT * SSM_G):
                t, g = divmod(n, SSM_G)
                part = m.y[:, t, g * GW:(g + 1) * GW]
                nc.vector.tensor_scalar(part, part, rs[:, n:n + 1], None, ALU.mult).then_inc(normed, 1)
            for n in range(1, NG, 2):
                dve.wait_ge(turned, n + 1)
                k, h = n % KD, n // KD
                nc.vector.tensor_scalar(ybT[:, k, h * HALF:(h + 1) * HALF], m.ps[n % 4][:, :],
                                        m.ssm_gain[:, k:k + 1], None, ALU.mult).then_inc(read[1], 1)

        @block.tensor
        def _(pe):
            for n in range(NG):
                k, h = n % KD, n // KD
                pe.wait_ge(normed, 4 * SSM_G * (h + 1))
                if n >= 4:
                    pe.wait_ge(read[n % 2], (n - 4) // 2 + 1)
                for j in range(4):
                    mm = nc.tensor.transpose(m.ps[n % 4][:, j * P:(j + 1) * P], m.y[:, 4 * h + j, k:D:KD],
                                             m.ident[:, :])
                mm.then_inc(turned, 1)


def nsa_project(nc, m):
    W = m.sb("nsa_w", [P, KD, NSA_W])
    hc = m.sb("nsa_hc", [P, 2, KD, P])
    NH = HEADS + 2 * GROUPS
    nb = m.sb("nsa_norm_in", [P, 2, NH, HD])
    cv = m.sb("nsa_cmp_in", [P, 2, 2 * KV_W])
    sq = m.sb("nsa_sq", [P, NH, HD])
    ss, rs = m.sb("nsa_ss", [P, NH]), m.sb("nsa_rs", [P, NH])
    q = {n: m.sem(f"nsa_{n}") for n in ("w_loaded", "hc_ready", "proj_done", "copied", "squared", "mean", "rooted",
                                        "normed", "turned", "spread", "ones", "gates")}
    ch = m.chains(nc, "nsa")
    LOOPS = NT // 2
    KS0, KW0 = HEADS * HD, HEADS * HD + KV_W
    nbf = nb[:, :, :, :].rearrange("p b h d -> p b (h d)")
    with nc.Block() as block:
        @block.sync
        def _(sp):
            sp.dma_start(W[:, :, :], m.i["w_in"][0][:, 0:NSA_W].rearrange("(p k) n -> p k n", k=KD))\
                .then_inc(q["w_loaded"], 16)

        @block.gpsimd
        def _(pool):
            nc.gpsimd.memset(m.v_sel[:, :, :, HD:HD + 1], 1.0).then_inc(q["ones"], 1)
            nc.gpsimd.memset(m.v_win[:, :, :, HD:HD + 1], 1.0).then_inc(q["ones"], 1)
            with pool.Fori(0, LOOPS) as i:
                for b in range(2):
                    pool.wait_ge(q["proj_done"], 6 * i)
                    nc.gpsimd.tensor_copy(hc[:, b, :, :], m.hT[:, :, bass.ds((2 * i + b) * P, P)])\
                        .then_inc(q["hc_ready"], 1)

        @block.tensor
        def _(pe):
            pe.wait_ge(q["w_loaded"], 16)
            with pe.Fori(0, LOOPS) as i:
                for b in range(2):
                    t = 2 * i + b
                    pe.wait_ge(q["hc_ready"], t + 1)
                    pe.wait_ge(q["copied"], 6 * t)
                    for n in range(3):
                        c0, c1 = n * HALF, min((n + 1) * HALF, NSA_W)
                        for k in range(KD):
                            mm = nc.tensor.matmul(m.ps[n][:, 0:c1 - c0], hc[:, b, k, :], W[:, k, c0:c1],
                                                  start=(k == 0), stop=(k == KD - 1))
                        mm.then_inc(q["proj_done"], 1)
                    pe.wait_ge(q["spread"], 4 * t)
                    pe.wait_ge(q["normed"], t + 1)
                    for n in range(E + 2):
                        nc.tensor.transpose(m.ps[3 + n // 4][:, n % 4 * P:(n % 4 + 1) * P],
                                            nbf[:, b, n * P:(n + 1) * P], m.ident[:, :])
                    for n in range(2):
                        mm = nc.tensor.transpose(m.ps[4][:, (2 + n) * P:(3 + n) * P], cv[:, b, n * P:(n + 1) * P],
                                                 m.ident[:, :])
                    mm.then_inc(q["turned"], 1)

        @block.scalar
        def _(act):
            act.wait_ge(q["ones"], 2)
            c = Chain(act, ch["act"])
            with act.Fori(0, LOOPS) as i:
                c.enter(i, 2)
                for b in range(2):
                    t = 2 * i + b
                    act.wait_ge(q["turned"], 2 * i)
                    act.wait_ge(q["proj_done"], 3 * t + 1)
                    nc.scalar.copy(nb[:, b, 0:HEADS, :].rearrange("p (e g) d -> p g e d", g=GROUPS),
                                   m.ps[0][:, :].rearrange("p (g e d) -> p g e d", g=GROUPS, e=E))\
                        .then_inc(q["copied"], 1)
                    act.wait_ge(q["proj_done"], 3 * t + 2)
                    nc.scalar.copy(cv[:, b, :], m.ps[1][:, 0:2 * KV_W]).then_inc(q["copied"], 1)
                    nc.scalar.copy(nbf[:, b, KS0:KS0 + KV_W], m.ps[1][:, 2 * KV_W:3 * KV_W]).then_inc(q["copied"], 1)
                    nc.scalar.copy(m.v_sel[:, bass.ds(t, 1), :, 0:HD].rearrange("p a g d -> p (a g) d"),
                                   m.ps[1][:, 3 * KV_W:4 * KV_W].rearrange("p (g d) -> p g d", d=HD))\
                        .then_inc(q["copied"], 1)
                    act.wait_ge(q["proj_done"], 3 * t + 3)
                    nc.scalar.copy(nbf[:, b, KW0:KW0 + KV_W], m.ps[2][:, 0:KV_W]).then_inc(q["copied"], 1)
                    nc.scalar.copy(m.v_win[:, bass.ds(t, 1), :, 0:HD].rearrange("p a g d -> p (a g) d"),
                                   m.ps[2][:, KV_W:2 * KV_W].rearrange("p (g d) -> p g d", d=HD))
                    c.link(nc.scalar.copy(m.gate_scale[:, bass.ds(t, 1), :].rearrange("p a g -> p (a g)"),
                                          m.ps[2][:, 2 * KV_W:2 * KV_W + GATE_W]))
                    nc.scalar.copy(m.junk[:, 0, 0:1], m.ones[:, 0:1]).then_inc(q["copied"], 1)
                    act.wait_ge(q["copied"], 6 * t + 6)
                    nc.scalar.activation(sq[:, :, :], nb[:, b, :, :], ACT.Square).then_inc(q["squared"], 1)
                    act.wait_ge(q["mean"], t + 1)
                    nc.scalar.activation(ss[:, :], ss[:, :], ACT.Sqrt).then_inc(q["rooted"], 1)
                c.leave(LOOPS, 2)
            g = m.gate_scale[:, :, :].rearrange("p t n -> p (t n)")
            nc.scalar.activation(g, g, ACT.Sigmoid).then_inc(q["gates"], 1)

        @block.vector
        def _(dve):
            c = Chain(dve, ch["dve"])
            PER = 2 * 2
            with dve.Fori(0, LOOPS) as i:
                c.enter(i, PER)
                for b in range(2):
                    t = 2 * i + b
                    cols = bass.ds(t * P, P)
                    dve.wait_ge(q["squared"], t + 1)
                    c.link(nc.vector.tensor_reduce(ss[:, :], sq[:, :, :], axis=AX.X, op=ALU.add))
                    nc.vector.tensor_scalar(ss[:, :], ss[:, :], 1.0 / HD, EPS, ALU.mult, ALU.add)\
                        .then_inc(q["mean"], 1)
                    dve.wait_ge(q["rooted"], t + 1)
                    c.link(nc.vector.reciprocal(rs[:, :], ss[:, :]))
                    nc.vector.tensor_tensor(nb[:, b, :, :], nb[:, b, :, :],
                                            rs[:, :].unsqueeze(2).to_broadcast([P, NH, HD]), ALU.mult)\
                        .then_inc(q["normed"], 1)
                    dve.wait_ge(q["turned"], t + 1)
                    nc.vector.tensor_scalar(m.qT[:, :, cols], m.ps[3][:, :].rearrange("p (e q) -> p e q", e=E),
                                            m.qk_gain[:, 0:1], None, ALU.mult).then_inc(q["spread"], 1)
                    nc.vector.tensor_scalar(m.ksT[:, cols], m.ps[4][:, 0:P], m.qk_gain[:, 2:3], None,
                                            ALU.mult).then_inc(q["spread"], 1)
                    nc.vector.tensor_scalar(m.kwT[:, cols], m.ps[4][:, P:2 * P], m.qk_gain[:, 3:4], None,
                                            ALU.mult).then_inc(q["spread"], 1)
                    nc.vector.tensor_copy(m.cT[:, :, cols], m.ps[4][:, 2 * P:].rearrange("p (a q) -> p a q", a=2))\
                        .then_inc(q["spread"], 1)
                c.leave(LOOPS, PER)
            dve.wait_ge(q["gates"], 1)
            first = m.gate_scale[:, 0, 0:GATE_W:3]
            c.link(nc.vector.tensor_scalar(first, first, m.any_cmp[:, 0:1], None, ALU.mult))


def compress(nc, m):
    W1 = m.sb("cmp_w1", [P, 2, CMP_BLOCK, CMP_HIDDEN])
    W2 = m.sb("cmp_w2", [P, 2, HD])
    pos = m.sb("cmp_pos", [CMP_BLOCK, 2, 2, HD])
    posT = m.sb("cmp_posT", [P, 2, CMP_BLOCK])
    bias = m.sb("cmp_bias", [P, 2])
    hid = m.sb("cmp_hid", [P, 2, GROUPS, NCMP])
    kc = m.sb("cmp_k", [NCMP, GROUPS, HD])
    sq = m.sb("cmp_sq", [NCMP, GROUPS, HD])
    ss, rs = m.sb("cmp_ss", [NCMP, GROUPS]), m.sb("cmp_rs", [NCMP, GROUPS])
    q = {n: m.sem(f"cmp_{n}") for n in ("loaded", "pos_turned", "pos_ready", "bias_done", "bias_ready", "hid_done",
                                        "hid_ready", "kv_done", "squared", "mean", "rooted", "normed", "k_turned",
                                        "ones")}
    ch = m.chains(nc, "cmp")
    LOADS = 2 * (2 + 1 + 2)
    i = m.i
    with nc.Block() as block:
        @block.sync
        def _(sp):
            for n, kv in enumerate("kv"):
                for g in range(GROUPS):
                    sp.dma_start(W1[g * HD:(g + 1) * HD, n, :, :],
                                 i[f"cmp_w1_{kv}"][0].rearrange("(j d) h -> d j h", d=HD)).then_inc(q["loaded"], 16)
                    sp.dma_start(pos[:, n, g, :], i[f"cmp_pos_{kv}"][0]).then_inc(q["loaded"], 16)
                sp.dma_start(W2[:, n, :], i[f"cmp_w2_{kv}"][0]).then_inc(q["loaded"], 16)

        @block.tensor
        def _(pe):
            pe.wait_ge(q["loaded"], 16 * LOADS)
            for n in range(2):
                mm = nc.tensor.transpose(m.ps[0][:, n * CMP_BLOCK:(n + 1) * CMP_BLOCK],
                                         pos[:, n, :, :].rearrange("j g d -> j (g d)"),
                                         m.ident[0:CMP_BLOCK, 0:CMP_BLOCK])
            mm.then_inc(q["pos_turned"], 1)
            pe.wait_ge(q["pos_ready"], 1)
            for n in range(2):
                for j in range(CMP_BLOCK):
                    mm = nc.tensor.matmul(m.ps[1][:, n:n + 1], W1[0:HD, n, j, :], posT[0:HD, n, j:j + 1],
                                          start=(j == 0), stop=(j == CMP_BLOCK - 1))
            mm.then_inc(q["bias_done"], 1)
            for n in range(2):
                for g in range(GROUPS):
                    half = slice(g * HD, (g + 1) * HD)
                    dst = m.ps[2 + g][:, n * P:n * P + NCMP]
                    for j in range(CMP_BLOCK):
                        last = CMP_STRIDE * (NCMP - 1) + j + 1
                        mm = nc.tensor.matmul(dst, W1[half, n, j, :], m.cT[half, n, j:last:CMP_STRIDE],
                                              start=(j == 0), stop=(j == CMP_BLOCK - 1))
            mm.then_inc(q["hid_done"], 1)
            pe.wait_ge(q["hid_ready"], 2 * GROUPS)
            for n in range(2):
                for g in range(GROUPS):
                    mm = nc.tensor.matmul(m.ps[4][0:NCMP, (2 * n + g) * HD:(2 * n + g + 1) * HD], hid[:, n, g, :],
                                          W2[:, n, :], start=True, stop=True)
            mm.then_inc(q["kv_done"], 1)
            pe.wait_ge(q["normed"], 1)
            nc.tensor.transpose(m.ps[5][:, 0:NCMP], kc[:, :, :].rearrange("c g d -> c (g d)"),
                                m.ident[0:NCMP, 0:NCMP]).then_inc(q["k_turned"], 1)

        @block.scalar
        def _(act):
            act.wait_ge(q["bias_ready"], 1)
            act.wait_ge(q["hid_done"], 1)
            for n in range(2):
                for g in range(GROUPS):
                    nc.scalar.activation(hid[:, n, g, :], m.ps[2 + g][:, n * P:n * P + NCMP], ACT.Silu,
                                         bias=bias[:, n:n + 1]).then_inc(q["hid_ready"], 1)
            act.wait_ge(q["kv_done"], 1)
            nc.scalar.activation(sq[:, :, :], m.ps[4][0:NCMP, 0:2 * HD].rearrange("c (g d) -> c g d", d=HD),
                                 ACT.Square).then_inc(q["squared"], 1)
            act.wait_ge(q["mean"], 1)
            nc.scalar.activation(ss[:, :], ss[:, :], ACT.Sqrt).then_inc(q["rooted"], 1)

        @block.gpsimd
        def _(pool):
            nc.gpsimd.memset(m.v_cmp[:, :, HD:HD + 1], 1.0).then_inc(q["ones"], 1)

        @block.vector
        def _(dve):
            c = Chain(dve, ch["dve"])
            dve.wait_ge(q["pos_turned"], 1)
            nc.vector.tensor_copy(posT[:, :, :], m.ps[0][:, 0:2 * CMP_BLOCK].rearrange("p (n j) -> p n j", n=2))\
                .then_inc(q["pos_ready"], 1)
            dve.wait_ge(q["bias_done"], 1)
            nc.vector.tensor_copy(bias[:, :], m.ps[1][:, 0:2]).then_inc(q["bias_ready"], 1)
            dve.wait_ge(q["squared"], 1)
            c.link(nc.vector.tensor_reduce(ss[:, :], sq[:, :, :], axis=AX.X, op=ALU.add))
            nc.vector.tensor_scalar(ss[:, :], ss[:, :], 1.0 / HD, EPS, ALU.mult, ALU.add).then_inc(q["mean"], 1)
            dve.wait_ge(q["ones"], 1)
            kv = m.ps[4][0:NCMP, 0:4 * HD].rearrange("c (n g d) -> c n g d", n=2, g=GROUPS)
            c.link(nc.vector.tensor_copy(m.v_cmp[:, :, 0:HD], kv[:, 1, :, :]))
            dve.wait_ge(q["rooted"], 1)
            c.link(nc.vector.reciprocal(rs[:, :], ss[:, :]))
            nc.vector.tensor_tensor(kc[:, :, :], kv[:, 0, :, :], rs[:, :].unsqueeze(2).to_broadcast([NCMP, GROUPS, HD]),
                                    ALU.mult).then_inc(q["normed"], 1)
            dve.wait_ge(q["k_turned"], 1)
            c.link(nc.vector.tensor_scalar(m.kcT[:, :], m.ps[5][:, 0:NCMP], m.qk_gain[:, 1:2], None, ALU.mult))


def attention(nc, m):
    qz = m.sb("att_q", [P, GROUPS, S])
    PAIRS = 3
    prob = m.sb("att_prob", [P, PAIRS, S])
    probT = m.sb("att_probT", [P, PAIRS, S])
    nmax = m.sb("att_nmax", [P, PAIRS, 2])
    rec = m.sb("att_rec", [P, 2, 3])
    acc = m.sb("att_acc", [P, 2, 2, HD])
    names = ("row_zeroed", "rows_cleared", "zeroed", "q_ready", "scored", "maxed", "exped", "turned", "sel_copied", "win_copied", "summed", "mixed", "recs")
    q = {n: m.sem(f"att_{n}") for n in names}
    copied = [q["sel_copied"], q["win_copied"]]
    ch = m.chains(nc, "att")
    WT = WINDOW // P
    CMP0 = (WT + 1) * P
    units = [(i, g, kind) for i in range(NT) for g in range(GROUPS) for kind in ("sel", "win")]
    U = len(units)

    def pair(u):
        return m.psum[:, 2 * HALF * (u % PAIRS):2 * HALF * (u % PAIRS + 1)]

    def before(u):
        return u - PAIRS if u >= PAIRS else U - PAIRS + (u - U % PAIRS) % PAIRS - U

    def tiles(u):
        i, _, kind = units[u]
        return range(0 if kind == "sel" else max(0, i - WT), i + 1)

    with nc.Block() as block:
        @block.gpsimd
        def _(pool):
            nc.gpsimd.memset(m.junk[:, 0, :], 0.0).then_inc(q["row_zeroed"], 1)
            pool.wait_ge(q["row_zeroed"], 1)
            for b in range(EXPERTS, BLOCKS):
                pool.dma_start(m.y_slots[b * P:(b + 1) * P, :], m.junk[:, 0, :]).then_inc(q["rows_cleared"], 16)
            for g in range(GROUPS):
                other = slice((1 - g) * HD, (2 - g) * HD)
                nc.gpsimd.memset(qz[other, g, :], 0.0).then_inc(q["zeroed"], 1)
            with pool.Fori(0, E) as e:
                for g in range(GROUPS):
                    own = slice(g * HD, (g + 1) * HD)
                    pool.wait_ge(q["scored"], U * e)
                    nc.gpsimd.tensor_copy(qz[own, g, :], m.qT[own, bass.ds(e, 1), :].rearrange("p a q -> p (a q)"))\
                        .then_inc(q["q_ready"], 1)
            pool.wait_ge(q["rows_cleared"], 16 * EXTRA)

        @block.tensor
        def _(pe):
            for n in copied:
                pe.sem_inc(n, 2)
            pe.sem_inc(q["mixed"], 2)
            pe.wait_ge(q["zeroed"], 2)

            def scores(e, u):
                i, g, kind = units[u]
                ps = pair(u)
                v = before(u)
                pe.wait_ge(copied[v % 2], U // 2 * e + v // 2 + 1 + 2)
                keys = m.ksT if kind == "sel" else m.kwT
                qs = qz[:, g, i * P:(i + 1) * P]
                k0, n = tiles(u)[0] * P, len(tiles(u)) * P
                for c0 in range(0, n, HALF):
                    c1 = min(c0 + HALF, n)
                    masks = []
                    if c1 == n:
                        masks.append((n - P, m.mask_future))
                    if kind == "win" and i >= WT and c0 == 0:
                        masks.append((0, m.mask_far))
                    mm = nc.tensor.matmul(ps[:, c0:c1], qs, keys[:, k0 + c0:k0 + c1], start=True, stop=not masks)
                    for x, (at, mask) in enumerate(masks):
                        mm = nc.tensor.matmul(ps[:, at:at + P], m.identb[:, :], mask[:, :], start=False,
                                              stop=(x == len(masks) - 1))
                if kind == "win":
                    nc.tensor.matmul(ps[:, CMP0:CMP0 + NCMP], qs, m.kcT[:, :], start=True, stop=False)
                    mm = nc.tensor.matmul(ps[:, CMP0:CMP0 + NCMP], m.identb[:, :], m.mask_cmp[:, i, 0:NCMP],
                                          start=False, stop=True)
                mm.then_inc(q["scored"], 1)

            def turn(e, u):
                ps, pr = pair(u), prob[:, u % PAIRS, :]
                pe.wait_ge(q["exped"], U * e + u + 1)
                for x in range(len(tiles(u))):
                    mm = nc.tensor.transpose(ps[:, x * P:(x + 1) * P], pr[:, x * P:(x + 1) * P], m.ident[:, :])
                if units[u][2] == "win":
                    mm = nc.tensor.transpose(ps[0:NCMP, CMP0:CMP0 + P], pr[:, CMP0:CMP0 + NCMP], m.ident[:, :])
                mm.then_inc(q["turned"], 1)

            def sums(e, u):
                i, g, kind = units[u]
                b = (u // 2) % 2
                dst, pt = m.ps[6 + b], probT[:, u % PAIRS, :]
                if kind == "sel":
                    pe.wait_ge(q["mixed"], U // 2 * e + u // 2 + 1)
                pe.wait_ge(copied[u % 2], U // 2 * e + u // 2 + 1 + 2)
                v, at = (m.v_sel, HD + 1) if kind == "sel" else (m.v_win, 2 * (HD + 1))
                ts = tiles(u)
                for x, t in enumerate(ts):
                    mm = nc.tensor.matmul(dst[:, at:at + HD + 1], pt[:, x * P:(x + 1) * P], v[:, t, g, :],
                                          start=(x == 0), stop=(x == len(ts) - 1))
                if kind == "win":
                    mm = nc.tensor.matmul(dst[:, 0:HD + 1], pt[0:NCMP, CMP0:CMP0 + P], m.v_cmp[:, g, :],
                                          start=True, stop=True)
                mm.then_inc(q["summed"], 1)

            with pe.Fori(0, E) as e:
                pe.wait_ge(q["q_ready"], GROUPS * (e + 1))
                for u in range(U + 3):
                    if u < U:
                        scores(e, u)
                    if 0 <= u - 2 < U:
                        turn(e, u - 2)
                    if 0 <= u - 3 < U:
                        sums(e, u - 3)

        @block.scalar
        def _(act):
            def copy(e, u):
                act.wait_ge(q["turned"], U * e + u + 1)
                n = len(tiles(u)) * P
                nc.scalar.copy(probT[:, u % PAIRS, 0:n], pair(u)[:, 0:n]).then_inc(copied[0], 1)

            with act.Fori(0, E) as e:
                for u in range(U + 1):
                    if u < U:
                        ps, pr, nm = pair(u), prob[:, u % PAIRS, :], nmax[:, u % PAIRS, :]
                        n = len(tiles(u)) * P
                        act.wait_ge(q["maxed"], U * e + u + 1)
                        ins = nc.scalar.activation(pr[:, 0:n], ps[:, 0:n], ACT.Exp, bias=nm[:, 0:1])
                        if units[u][2] == "win":
                            ins = nc.scalar.activation(pr[:, CMP0:CMP0 + NCMP], ps[:, CMP0:CMP0 + NCMP], ACT.Exp,
                                                       bias=nm[:, 1:2])
                        ins.then_inc(q["exped"], 1)
                    if u >= 1 and units[u - 1][2] == "sel":
                        copy(e, u - 1)

        @block.vector
        def _(dve):
            c = Chain(dve, ch["dve"])
            PER = (U // 2) * 5

            def maxima(e, u):
                ps, nm = pair(u), nmax[:, u % PAIRS, :]
                n = len(tiles(u)) * P
                dve.wait_ge(q["scored"], U * e + u + 1)
                ins = nc.vector.tensor_reduce(nm[:, 0:1], ps[:, 0:n], axis=AX.X, op=ALU.max, negate=True)
                if units[u][2] == "win":
                    ins = nc.vector.tensor_reduce(nm[:, 1:2], ps[:, CMP0:CMP0 + NCMP], axis=AX.X, op=ALU.max,
                                                  negate=True)
                ins.then_inc(q["maxed"], 1)

            def copy(e, u):
                dve.wait_ge(q["turned"], U * e + u + 1)
                n = len(tiles(u)) * P
                c.link(nc.vector.tensor_copy(probT[:, u % PAIRS, 0:n], pair(u)[:, 0:n]))
                nc.vector.tensor_copy(probT[0:NCMP, u % PAIRS, CMP0:CMP0 + P], pair(u)[0:NCMP, CMP0:CMP0 + P])\
                    .then_inc(copied[1], 1)

            def mix(e, w):
                i, g, _ = units[2 * w]
                dve.wait_ge(q["summed"], U * e + 2 * w + 2)
                o = m.ps[6 + w % 2][:, 0:3 * (HD + 1)].rearrange("p (b d) -> p b d", b=3)
                r, a = rec[:, w % 2, :], acc[:, w % 2, :, :]
                head = g * E + e
                c.link(nc.vector.reciprocal(r, o[:, :, HD:HD + 1].rearrange("p b a -> p (b a)")))
                c.link(nc.vector.tensor_tensor(r, r, m.gate_scale[:, i, bass.ds(3 * head, 3)], ALU.mult))
                c.link(nc.vector.tensor_scalar(a[:, 0, :], o[:, 0, 0:HD], r[:, 0:1], None, ALU.mult))
                c.link(nc.vector.scalar_tensor_tensor(out=a[:, 1, :], in0=o[:, 1, 0:HD], scalar=r[:, 1:2],
                                                      in1=a[:, 0, :], op0=ALU.mult, op1=ALU.add))
                nc.vector.scalar_tensor_tensor(out=m.ya[:, i, bass.ds(head, 1), :].rearrange("p a d -> p (a d)"),
                                               in0=o[:, 2, 0:HD], scalar=r[:, 2:3], in1=a[:, 1, :],
                                               op0=ALU.mult, op1=ALU.add).then_inc(q["mixed"], 1)

            with dve.Fori(0, E) as e:
                c.enter(e, PER)
                for u in range(U + 4):
                    if u < U:
                        maxima(e, u)
                    if 0 <= u - 1 < U and units[u - 1][2] == "win":
                        copy(e, u - 1)
                    if u >= 4 and u % 2 == 0 and (u - 4) // 2 < U // 2:
                        mix(e, (u - 4) // 2)
                c.leave(E, PER)


def turn_ya(nc, m):
    KA = Q_W // P
    turned = m.sem("ya_turned")
    read = [m.sem("ya_act_read"), m.sem("ya_dve_read")]
    src = m.ya[:, :, :, :].rearrange("p t h d -> p t (h d)")
    with nc.Block() as block:
        @block.tensor
        def _(pe):
            for n in range(2 * KA):
                k, h = n % KA, n // KA
                if n >= 4:
                    pe.wait_ge(read[n % 2], (n - 4) // 2 + 1)
                for j in range(4):
                    mm = nc.tensor.transpose(m.ps[n % 4][:, j * P:(j + 1) * P], src[:, 4 * h + j, k:Q_W:KA],
                                             m.ident[:, :])
                mm.then_inc(turned, 1)

        @block.scalar
        def _(act):
            for n in range(0, 2 * KA, 2):
                k, h = n % KA, n // KA
                act.wait_ge(turned, n + 1)
                nc.scalar.copy(m.yaT[:, k, h * HALF:(h + 1) * HALF], m.ps[n % 4][:, :]).then_inc(read[0], 1)

        @block.vector
        def _(dve):
            for n in range(1, 2 * KA, 2):
                k, h = n % KA, n // KA
                dve.wait_ge(turned, n + 1)
                nc.vector.tensor_copy(m.yaT[:, k, h * HALF:(h + 1) * HALF], m.ps[n % 4][:, :]).then_inc(read[1], 1)


def merge(nc, m):
    KA = Q_W // P
    parts = ((KD, BR0, "w_in", m.hT), (KA, 0, "w_branch_a", m.yaT),
             (KD, BR0 + D, "w_in", m.hT), (KD, 0, "w_branch_b", m.ybT))
    KW = sum(x[0] for x in parts)
    RING = 2
    W = m.sb("merge_w", [P, RING, KW, P])
    sg = m.sb("merge_sg", [P, 2, 2, HALF])
    half = m.sb("merge_half", [P, 2, HALF])
    here = [m.sem(f"merge_w_loaded{r}") for r in range(RING)]
    q = {n: m.sem(f"merge_{n}") for n in ("done", "sig_ready", "read")}
    ch = m.chains(nc, "merge")
    with nc.Block() as block:
        @block.sync
        def _(sp):
            with sp.Fori(0, KD // RING) as it:
                for r in range(RING):
                    sp.wait_ge(q["read"], 2 * RING * it)
                    at = 0
                    for kk, c0, name, _ in parts:
                        src = m.i[name][0][:, c0:c0 + D].rearrange("(p k) (m c) -> m p k c", k=kk, c=P)
                        sp.dma_start(W[:, r, at:at + kk, :], src[RING * it + r, :, :, :]).then_inc(here[r], 16)
                        at += kk
            for t in range(NT):
                sp.dma_start(m.x2[:, t, :], m.i["x"][0][t * P:(t + 1) * P, :]).then_inc(m.x_loaded, 16)

        @block.tensor
        def _(pe):
            with pe.Fori(0, KD // RING) as it:
                for r in range(RING):
                    pe.wait_ge(here[r], 16 * 4 * (it + 1))
                    for h in range(2):
                        pe.wait_ge(q["read"], 2 * RING * it + 2 * (r - 1) + h + 1 if r else 2 * RING * it)
                        at = 0
                        for n, (kk, _, _, src) in enumerate(parts):
                            for k in range(kk):
                                mm = nc.tensor.matmul(m.ps[4 * h + n][:, :], W[:, r, at + k, :],
                                                      src[:, k, h * HALF:(h + 1) * HALF],
                                                      start=(k == 0), stop=(k == kk - 1))
                            at += kk
                            mm.then_inc(q["done"], 1)

        @block.scalar
        def _(act):
            with act.Fori(0, KD // RING) as it:
                for r in range(RING):
                    for h in range(2):
                        n = 2 * RING * it + 2 * r + h
                        act.wait_ge(q["read"], 2 * RING * it + 2 * (r - 1) + h + 1 if r else 2 * RING * it)
                        for b in range(2):
                            act.wait_ge(q["done"], 4 * n + 2 * b + 1)
                            nc.scalar.activation(sg[:, h, b, :], m.ps[4 * h + 2 * b][:, :],
                                                 ACT.Sigmoid).then_inc(q["sig_ready"], 1)

        @block.vector
        def _(dve):
            c = Chain(dve, ch["dve"])
            PER = 2 * RING * 2
            with dve.Fori(0, KD // RING) as it:
                c.enter(it, PER)
                for r in range(RING):
                    for h in range(2):
                        n = 2 * RING * it + 2 * r + h
                        dve.wait_ge(q["read"], n)
                        for b in range(2):
                            dve.wait_ge(q["sig_ready"], 2 * n + b + 1)
                            dve.wait_ge(q["done"], 4 * n + 2 * b + 2)
                            c.link(nc.vector.tensor_tensor(half[:, b, :], sg[:, h, b, :], m.ps[4 * h + 2 * b + 1][:, :],
                                                           ALU.mult))
                        nc.vector.tensor_tensor(
                            m.mergedT[:, bass.ds(RING * it + r, 1), h * HALF:(h + 1) * HALF]
                            .rearrange("p a n -> p (a n)"), half[:, 0, :], half[:, 1, :], ALU.add).then_inc(q["read"], 1)
                c.leave(KD // RING, PER)


def project_out(nc, m):
    W = m.sb("out_w", [P, KD, D])
    q = {n: m.sem(f"out_{n}") for n in ("w_loaded", "done", "read")}
    with nc.Block() as block:
        @block.sync
        def _(sp):
            sp.dma_start(W[:, :, :], m.i["w_out"][0].rearrange("(k p) n -> p k n", k=KD)).then_inc(q["w_loaded"], 16)

        @block.tensor
        def _(pe):
            pe.wait_ge(q["w_loaded"], 16)
            with pe.Fori(0, 2) as n:
                for t in range(NT):
                    pe.wait_ge(q["read"], NT * n + t - 3 if t >= 4 else NT * n)
                    for k in range(KD):
                        mm = nc.tensor.matmul(m.ps[t % 4][:, :], m.mergedT[:, k, t * P:(t + 1) * P],
                                              W[:, k, bass.ds(n * HALF, HALF)], start=(k == 0), stop=(k == KD - 1))
                    mm.then_inc(q["done"], 1)

        @block.vector
        def _(dve):
            dve.wait_ge(m.x_loaded, 16 * NT)
            with dve.Fori(0, 2) as n:
                for t in range(NT):
                    dve.wait_ge(q["done"], NT * n + t + 1)
                    part = m.x2[:, t, bass.ds(n * HALF, HALF)]
                    nc.vector.tensor_tensor(part, part, m.ps[t % 4][:, :], ALU.add).then_inc(q["read"], 1)


def route(nc, m):
    W = m.sb("route_w", [P, KD, ROUTES])
    lg = m.sb("route_logits", [P, NT, ROUTES])
    f = {n: m.sb(f"route_{n}", [P, NT]) for n in ("gmax", "gsum", "grp", "gw", "m1", "i1", "m2", "i2", "e2", "den")}
    eg, gm = m.sb("route_eg", [P, NT, MGROUPS]), m.sb("route_gm", [P, NT, MGROUPS])
    el, eq, ex = (m.sb(f"route_{n}", [P, NT, PER_GROUP]) for n in ("el", "eq", "ex"))
    sel = m.sb("route_sel", [P, NT, PER_GROUP, MGROUPS])
    M1, M2, M, rank, tmp = (m.sb(f"route_{n}", [P, NT, EXPERTS]) for n in ("M1", "M2", "M", "rank", "tmp"))
    iota = m.sb("route_iota", [P, EXPERTS])
    iotai = m.sb("route_iotai", [P, EXPERTS], I32)
    tok = m.sb("route_tok", [P, NT], I32)
    cnt, carry, extra, incl = (m.sb(f"route_{n}", [P, EXPERTS]) for n in ("cnt", "carry", "extra", "incl"))
    r, j, own, pos, slot, more = (m.sb(f"route_{n}", [P, NT, 2]) for n in ("r", "j", "own", "pos", "slot", "more"))
    cmpx = m.sb("route_cmpx", [P, EXTRA, EXPERTS])
    bex = m.sb("route_bex", [P, EXTRA])
    zero = m.sb("route_zero", [BLOCKS, P], I32)
    rows, rowsf = m.sb("route_rows", [BLOCKS, P], I32), m.sb("route_rowsf", [BLOCKS, P])
    q = {n: m.sem(f"route_{n}") for n in ("w_loaded", "iota", "zeroed", "cleared", "logits", "maxed", "exped", "masks",
                                          "ranked", "slots", "scattered", "rows_loaded", "rows_ready", "rows_turned")}
    ch = m.chains(nc, "route")
    with nc.Block() as block:
        @block.sync
        def _(sp):
            sp.dma_start(W[:, :, 0:MGROUPS], m.i["moe_w_group"][0].rearrange("(p k) n -> p k n", k=KD))\
                .then_inc(q["w_loaded"], 16)
            sp.dma_start(W[:, :, MGROUPS:], m.i["moe_w_expert"][0].rearrange("(p k) n -> p k n", k=KD))\
                .then_inc(q["w_loaded"], 16)
            sp.wait_ge(q["zeroed"], 1)
            sp.dma_start(m.slot_tok.rearrange("(b p) a -> b (p a)", p=P), zero[:, :]).then_inc(q["cleared"], 16)
            sp.wait_ge(q["scattered"], 16 * 2 * NT)
            sp.dma_start(rows[:, :], m.slot_tok.rearrange("(b p) a -> b (p a)", p=P)).then_inc(q["rows_loaded"], 16)
            sp.wait_ge(q["rows_loaded"], 16)

        @block.gpsimd
        def _(pool):
            nc.gpsimd.memset(zero[:, :], 0).then_inc(q["zeroed"], 1)
            nc.gpsimd.iota(tok[:, :], pattern=[[P, NT]], base=0, channel_multiplier=1).then_inc(q["iota"], 1)
            nc.gpsimd.iota(iotai[:, :], pattern=[[1, EXPERTS]], base=0, channel_multiplier=0).then_inc(q["iota"], 1)
            pool.wait_ge(q["iota"], 2)
            pool.wait_ge(q["cleared"], 16)
            pool.wait_ge(q["slots"], 1)
            for t in range(NT):
                for s in range(2):
                    nc.gpsimd.indirect_dma_start(m.slot_tok, bass.IndirectOffsetOnAxis(ap=m.slot_u[:, t, s:s + 1], axis=0),
                                                 tok[:, t:t + 1], None).then_inc(q["scattered"], 16)
            pool.wait_ge(q["scattered"], 16 * 2 * NT)

        @block.tensor
        def _(pe):
            pe.wait_ge(q["w_loaded"], 32)
            for t in range(NT):
                for k in range(KD):
                    mm = nc.tensor.matmul(m.ps[0][:, t * ROUTES:(t + 1) * ROUTES], m.h2T[:, k, t * P:(t + 1) * P],
                                          W[:, k, :], start=(k == 0), stop=(k == KD - 1))
            mm.then_inc(q["logits"], 1)
            pe.wait_ge(q["masks"], 1)
            flat = M[:, :, :].rearrange("p t e -> p (t e)")
            nc.tensor.matmul(m.ps[1][:, 0:NT * EXPERTS], m.tri_lt[:, :], flat, start=True, stop=True)
            nc.tensor.matmul(m.ps[2][:, 0:NT * EXPERTS], m.ones[:, :], flat, start=True,
                             stop=True).then_inc(q["ranked"], 1)
            pe.wait_ge(q["rows_ready"], 1)
            nc.tensor.transpose(m.ps[3][:, 0:BLOCKS], rowsf[:, :], m.ident[0:BLOCKS, 0:BLOCKS])\
                .then_inc(q["rows_turned"], 1)

        @block.scalar
        def _(act):
            c = Chain(act, ch["act"])
            act.wait_ge(q["maxed"], 2)
            c.link(nc.scalar.activation(eg[:, :, :], gm[:, :, :], ACT.Exp))
            nc.scalar.activation(f["e2"][:, :], f["e2"][:, :], ACT.Exp).then_inc(q["exped"], 1)

        @block.vector
        def _(dve):
            c = Chain(dve, ch["dve"])
            v = nc.vector

            def wide(ap, n):
                return ap.unsqueeze(2).to_broadcast([P, NT, n])

            def row(ap, n):
                return ap.unsqueeze(1).to_broadcast([P, NT, n])

            def first(out, hit, n):
                c.link(v.scalar_tensor_tensor(out=hit, in0=hit, scalar=-64.0, in1=row(iota[:, 0:n], n),
                                              op0=ALU.mult, op1=ALU.add))
                c.link(v.tensor_reduce(out, hit, axis=AX.X, op=ALU.min))
                c.link(v.tensor_scalar(out, out, 64.0, None, ALU.add))

            dve.wait_ge(q["iota"], 2)
            c.link(v.tensor_copy(iota[:, :], iotai[:, :]))
            dve.wait_ge(q["logits"], 1)
            c.link(v.tensor_tensor(lg[:, :, :], m.ps[0][:, 0:NT * ROUTES].rearrange("p (t n) -> p t n", t=NT),
                                   row(m.route_bias[:, :], ROUTES), ALU.add))
            g = lg[:, :, 0:MGROUPS]
            c.link(v.tensor_reduce(f["gmax"][:, :], g, axis=AX.X, op=ALU.max))
            v.tensor_tensor(gm[:, :, :], g, wide(f["gmax"][:, :], MGROUPS), ALU.subtract).then_inc(q["maxed"], 1)
            hit = sel[:, :, 0, :]
            c.link(v.tensor_tensor(hit, g, wide(f["gmax"][:, :], MGROUPS), ALU.is_equal))
            first(f["grp"][:, :], hit, MGROUPS)
            c.link(v.tensor_tensor(eq[:, :, 0:MGROUPS], row(iota[:, 0:MGROUPS], MGROUPS),
                                   wide(f["grp"][:, :], MGROUPS), ALU.is_equal))
            c.link(v.tensor_tensor(sel[:, :, :, :],
                                   lg[:, :, MGROUPS:].rearrange("p t (g e) -> p t e g", g=MGROUPS),
                                   eq[:, :, 0:MGROUPS].unsqueeze(2).to_broadcast([P, NT, PER_GROUP, MGROUPS]), ALU.mult))
            c.link(v.tensor_reduce(el[:, :, :], sel[:, :, :, :], axis=AX.X, op=ALU.add))
            c.link(v.tensor_reduce(f["m1"][:, :], el[:, :, :], axis=AX.X, op=ALU.max))
            c.link(v.tensor_tensor(eq[:, :, :], el[:, :, :], wide(f["m1"][:, :], PER_GROUP), ALU.is_equal))
            first(f["i1"][:, :], eq[:, :, :], PER_GROUP)
            c.link(v.tensor_tensor(eq[:, :, :], row(iota[:, 0:PER_GROUP], PER_GROUP), wide(f["i1"][:, :], PER_GROUP),
                                   ALU.is_equal))
            c.link(v.scalar_tensor_tensor(out=ex[:, :, :], in0=eq[:, :, :], scalar=MASK, in1=el[:, :, :],
                                          op0=ALU.mult, op1=ALU.add))
            c.link(v.tensor_reduce(f["m2"][:, :], ex[:, :, :], axis=AX.X, op=ALU.max))
            c.link(v.tensor_tensor(eq[:, :, :], ex[:, :, :], wide(f["m2"][:, :], PER_GROUP), ALU.is_equal))
            first(f["i2"][:, :], eq[:, :, :], PER_GROUP)
            v.tensor_tensor(f["e2"][:, :], f["m2"][:, :], f["m1"][:, :], ALU.subtract).then_inc(q["maxed"], 1)
            for i in ("i1", "i2"):
                c.link(v.scalar_tensor_tensor(out=f[i][:, :], in0=f["grp"][:, :], scalar=float(PER_GROUP), in1=f[i][:, :],
                                              op0=ALU.mult, op1=ALU.add))
            for mask, i in ((M1, "i1"), (M2, "i2")):
                c.link(v.tensor_tensor(mask[:, :, :], row(iota[:, :], EXPERTS), wide(f[i][:, :], EXPERTS), ALU.is_equal))
            v.tensor_tensor(M[:, :, :], M1[:, :, :], M2[:, :, :], ALU.add).then_inc(q["masks"], 1)
            dve.wait_ge(q["exped"], 1)
            c.link(v.tensor_reduce(f["gsum"][:, :], eg[:, :, :], axis=AX.X, op=ALU.add))
            c.link(v.scalar_tensor_tensor(out=f["den"][:, :], in0=f["e2"][:, :], scalar=1.0, in1=f["gsum"][:, :],
                                          op0=ALU.add, op1=ALU.mult))
            c.link(v.reciprocal(m.weight[:, :, 0], f["den"][:, :]))
            c.link(v.tensor_tensor(m.weight[:, :, 1], m.weight[:, :, 0], f["e2"][:, :], ALU.mult))
            dve.wait_ge(q["ranked"], 1)
            c.link(v.tensor_copy(rank[:, :, :], m.ps[1][:, 0:NT * EXPERTS].rearrange("p (t e) -> p t e", t=NT)))
            c.link(v.tensor_copy(cnt[:, :], m.ps[2][:, 0:EXPERTS]))
            for t in range(1, NT):
                c.link(v.tensor_tensor(rank[:, t, :], rank[:, t, :], cnt[:, :], ALU.add))
                c.link(v.tensor_tensor(cnt[:, :], cnt[:, :], m.ps[2][:, t * EXPERTS:(t + 1) * EXPERTS], ALU.add))
            c.link(v.tensor_scalar(extra[:, :], cnt[:, :], float(P), None, ALU.is_gt))
            for n in range(2, NT):
                c.link(v.scalar_tensor_tensor(out=extra[:, :], in0=cnt[:, :], scalar=float(n * P), in1=extra[:, :],
                                              op0=ALU.is_gt, op1=ALU.add))
            c.link(v.tensor_tensor_scan(incl[:, :], m.ones[:, 0:EXPERTS], extra[:, :], 0.0, ALU.mult, ALU.add))
            c.link(v.tensor_tensor(carry[:, :], incl[:, :], extra[:, :], ALU.subtract))
            for s, mask in ((0, M1), (1, M2)):
                c.link(v.tensor_tensor(tmp[:, :, :], mask[:, :, :], rank[:, :, :], ALU.mult))
                c.link(v.tensor_reduce(r[:, :, s], tmp[:, :, :], axis=AX.X, op=ALU.add))
                c.link(v.tensor_tensor(tmp[:, :, :], mask[:, :, :], row(carry[:, :], EXPERTS), ALU.mult))
                c.link(v.tensor_reduce(own[:, :, s], tmp[:, :, :], axis=AX.X, op=ALU.add))
                c.link(v.tensor_copy(pos[:, :, s], f["i1" if s == 0 else "i2"][:, :]))
            c.link(v.tensor_scalar(j[:, :, :], r[:, :, :], float(P), None, ALU.is_ge))
            c.link(v.tensor_copy(more[:, :, :], j[:, :, :]))
            for n in range(2, NT):
                c.link(v.scalar_tensor_tensor(out=j[:, :, :], in0=r[:, :, :], scalar=float(n * P), in1=j[:, :, :],
                                              op0=ALU.is_ge, op1=ALU.add))
            c.link(v.tensor_tensor(own[:, :, :], own[:, :, :], j[:, :, :], ALU.add))
            c.link(v.tensor_scalar(own[:, :, :], own[:, :, :], float(EXPERTS - 1), None, ALU.add))
            c.link(v.tensor_tensor(own[:, :, :], own[:, :, :], pos[:, :, :], ALU.subtract))
            c.link(v.tensor_tensor(own[:, :, :], own[:, :, :], more[:, :, :], ALU.mult))
            c.link(v.tensor_tensor(own[:, :, :], own[:, :, :], pos[:, :, :], ALU.add))
            c.link(v.tensor_tensor(own[:, :, :], own[:, :, :], j[:, :, :], ALU.subtract))
            c.link(v.scalar_tensor_tensor(out=slot[:, :, :], in0=own[:, :, :], scalar=float(P), in1=r[:, :, :],
                                          op0=ALU.mult, op1=ALU.add))
            v.tensor_copy(m.slot_u[:, :, :], slot[:, :, :]).then_inc(q["slots"], 1)
            c.link(v.tensor_tensor(cmpx[:, :, :], incl[:, :].unsqueeze(1).to_broadcast([P, EXTRA, EXPERTS]),
                                   iota[:, 0:EXTRA].unsqueeze(2).to_broadcast([P, EXTRA, EXPERTS]), ALU.is_le))
            c.link(v.tensor_reduce(bex[:, :], cmpx[:, :, :], axis=AX.X, op=ALU.add))
            c.link(v.tensor_scalar(bex[:, :], bex[:, :], float(EXPERTS - 1), None, ALU.min))
            c.link(v.tensor_copy(m.plan[:, 0:EXTRA], bex[:, :]))
            c.link(v.tensor_copy(m.plan[:, EXTRA:EXTRA + 1], incl[:, EXPERTS - 1:EXPERTS]))
            dve.wait_ge(q["rows_loaded"], 16)
            v.tensor_copy(rowsf[:, :], rows[:, :]).then_inc(q["rows_ready"], 1)
            dve.wait_ge(q["rows_turned"], 1)
            c.link(v.tensor_copy(m.slot_idx[:, :], m.ps[3][:, 0:BLOCKS]))


def experts(nc, m, name, further):
    KH = MOE_H // P
    wg, wu, wd = m.moe_w
    b = m.moe_buf
    q = {n: m.sem(f"{name}_{n}") for n in ("idx_ready", "turned", "xT_ready", "gu_done", "silu_ready", "h_ready",
                                           "down_done", "out_ready", "pool_past", "act_past")}
    w_here = [m.sem(f"{name}_w_loaded{r}") for r in range(2)]
    x_here = [m.sem(f"{name}_x_gathered{r}") for r in range(2)]
    stored = [m.sem(f"{name}_stored{r}") for r in range(2)]
    PASSES = (EXTRA if further else EXPERTS) // 2
    first_block = EXPERTS if further else 0
    out_banks = ((6, 7), (0, 1))

    def passes(eng, body):
        if not further:
            with eng.Fori(0, PASSES) as i:
                body(i)
            return
        number = eng.value_load(m.plan[0:1, EXTRA:EXTRA + 1], min_val=0, max_val=EXTRA)
        with eng.Fori(0, PASSES) as i:
            with eng.If(number > 2 * i):
                body(i)
            eng.nop()

    with nc.Block() as block:
        @block.sync
        def _(sp):
            def body(i):
                for r in range(2):
                    e = 2 * i + r
                    if further:
                        e = sp.value_load(m.plan[0:1, bass.ds(2 * i + r, 1)], min_val=0, max_val=EXPERTS - 1)
                    sp.wait_ge(q["gu_done"], 2 * i)
                    sp.dma_start(wg[:, r, :, :], m.i["moe_w_gate"][0][e, :, :].rearrange("(p k) n -> p k n", k=KD))\
                        .then_inc(w_here[r], 16)
                    sp.dma_start(wu[:, r, :, :], m.i["moe_w_up"][0][e, :, :].rearrange("(p k) n -> p k n", k=KD))\
                        .then_inc(w_here[r], 16)
                    sp.wait_ge(q["down_done"], 2 * i)
                    sp.dma_start(wd[:, r, :, :], m.i["moe_w_down"][0][e, :, :].rearrange("(k p) n -> p k n", k=KH))\
                        .then_inc(w_here[r], 16)
            passes(sp, body)

        @block.gpsimd
        def _(pool):
            def body(i):
                for r in range(2):
                    pool.wait_ge(q["turned"], 4 * i)
                    nc.gpsimd.tensor_copy(b["idx"][:, r:r + 1], m.slot_idx[:, bass.ds(2 * i + r + first_block, 1)])\
                        .then_inc(q["idx_ready"], 1)
                    pool.wait_ge(q["idx_ready"], 2 * i + r + 1)
                    pool.sem_inc(q["pool_past"], 1)
                    nc.gpsimd.indirect_dma_start(b["x"][r][:, :], None, m.xn_dram,
                                                 bass.IndirectOffsetOnAxis(ap=b["idx"][:, r:r + 1], axis=0))\
                        .then_inc(x_here[r], 16)
            passes(pool, body)

        @block.tensor
        def _(pe):
            def body(i):
                for r in range(2):
                    pe.wait_ge(x_here[r], 16 * (i + 1))
                    pe.wait_ge(q["out_ready"], 2 * i)
                    for h in range(2):
                        for k in range(4):
                            mm = nc.tensor.transpose(m.ps[2 * r + h][:, k * P:(k + 1) * P],
                                                     b["x"][r][:, 4 * h + k:D:KD], m.ident[:, :])
                        mm.then_inc(q["turned"], 1)
                for r in range(2):
                    pe.wait_ge(w_here[r], 48 * (i + 1))
                    pe.wait_ge(q["xT_ready"], 2 * (2 * i + r) + 2)
                    pe.wait_ge(q["h_ready"], 2 * i)
                    for n, w in enumerate((wg, wu)):
                        for c in range(KH):
                            for k in range(KD):
                                mm = nc.tensor.matmul(m.ps[4 + r][:, (KH * n + c) * P:(KH * n + c + 1) * P],
                                                      w[:, r, k, c * P:(c + 1) * P], b["xT"][:, r, k, :],
                                                      start=(k == 0), stop=(k == KD - 1))
                    mm.then_inc(q["gu_done"], 1)
                for r in range(2):
                    pe.wait_ge(q["h_ready"], 2 * i + r + 1)
                    for h in range(2):
                        for k in range(KH):
                            mm = nc.tensor.matmul(m.ps[out_banks[r][h]][:, :], b["h"][:, r, k, :],
                                                  wd[:, r, k, h * HALF:(h + 1) * HALF],
                                                  start=(k == 0), stop=(k == KH - 1))
                    mm.then_inc(q["down_done"], 1)
            passes(pe, body)

        @block.scalar
        def _(act):
            def body(i):
                for r in range(2):
                    act.wait_ge(q["gu_done"], 2 * i + r + 1)
                    act.wait_ge(q["h_ready"], 2 * i)
                    nc.scalar.activation(b["sg"][:, r, :], m.ps[4 + r][:, 0:MOE_H], ACT.Silu)\
                        .then_inc(q["silu_ready"], 1)
                for r in range(2):
                    act.wait_ge(q["down_done"], 2 * i + r + 1)
                    act.wait_ge(stored[r], 16 * i)
                    banks = m.psum[:, out_banks[r][0] * HALF:(out_banks[r][1] + 1) * HALF]
                    nc.scalar.copy(b["out"][:, r, :], banks).then_inc(q["out_ready"], 1)
                    act.wait_ge(q["out_ready"], 2 * i + r + 1)
                    act.dma_start(m.y_slots[bass.ds((2 * i + r + first_block) * P, P), :], b["out"][:, r, :])\
                        .then_inc(stored[r], 16)
                for r in range(2):
                    act.wait_ge(stored[r], 16 * (i + 1))
                act.sem_inc(q["act_past"], 1)
            passes(act, body)

        @block.vector
        def _(dve):
            def body(i):
                for r in range(2):
                    for h in range(2):
                        dve.wait_ge(q["turned"], 4 * i + 2 * r + h + 1)
                        dve.wait_ge(q["gu_done"], 2 * i)
                        nc.vector.tensor_tensor(b["xT"][:, r, 4 * h:4 * h + 4, :],
                                                m.ps[2 * r + h][:, :].rearrange("p (k n) -> p k n", k=4),
                                                m.moe_gain[:, 4 * h:4 * h + 4].unsqueeze(2).to_broadcast([P, 4, P]),
                                                ALU.mult).then_inc(q["xT_ready"], 1)
                for r in range(2):
                    dve.wait_ge(q["silu_ready"], 2 * i + r + 1)
                    dve.wait_ge(q["down_done"], 2 * i)
                    nc.vector.tensor_tensor(b["h"][:, r, :, :].rearrange("p k n -> p (k n)"), b["sg"][:, r, :],
                                            m.ps[4 + r][:, MOE_H:2 * MOE_H], ALU.mult).then_inc(q["h_ready"], 1)
            passes(dve, body)


def combine(nc, m):
    RING = 2
    rows = m.sb("combine_rows", [P, RING, 2, D])
    here = [m.sem(f"combine_gathered{r}{s}") for r in range(RING) for s in range(2)]
    added = m.sem("combine_added")
    with nc.Block() as block:
        @block.gpsimd
        def _(pool):
            for t in range(NT):
                if t >= RING:
                    pool.wait_ge(added, 2 * (t - RING + 1))
                for s in range(2):
                    nc.gpsimd.indirect_dma_start(rows[:, t % RING, s, :], None, m.y_slots,
                                                 bass.IndirectOffsetOnAxis(ap=m.slot_u[:, t, s:s + 1], axis=0))\
                        .then_inc(here[2 * (t % RING) + s], 16)

        @block.vector
        def _(dve):
            for t in range(NT):
                for s in range(2):
                    dve.wait_ge(here[2 * (t % RING) + s], 16 * (t // RING + 1))
                    if s:
                        dve.wait_ge(added, 2 * t + 1)
                    nc.vector.scalar_tensor_tensor(out=m.x2[:, t, :], in0=rows[:, t % RING, s, :],
                                                   scalar=m.weight[:, t, s:s + 1], in1=m.x2[:, t, :],
                                                   op0=ALU.mult, op1=ALU.add).then_inc(added, 1)


def per_layer(nc, m):
    KP = PLE // P
    pin = m.sb("ple_in", [P, NT, PLE])
    pT = m.sb("ple_pT", [P, KP, S])
    sg = m.sb("ple_sg", [P, 2, HALF])
    res = m.sb("ple_out", [P, 2, HALF])
    q = {n: m.sem(f"ple_{n}") for n in ("p_loaded", "p_turned", "pT_ready", "done", "sig_ready", "read")}
    stored = [m.sem(f"ple_stored{r}") for r in range(2)]
    ch = m.chains(nc, "ple")
    with nc.Block() as block:
        @block.sync
        def _(sp):
            sp.dma_start(pin[:, :, :], m.i["p"][0, 0].rearrange("(t p) n -> p t n", p=P)).then_inc(q["p_loaded"], 16)
            with sp.Fori(0, 2) as n:
                for t in range(NT):
                    sp.wait_ge(q["read"], NT * n + t + 1)
                    sp.dma_start(m.out[0, t * P:(t + 1) * P, bass.ds(n * HALF, HALF)], res[:, t % 2, :])\
                        .then_inc(stored[t % 2], 16)
            for r in range(2):
                sp.wait_ge(stored[r], 16 * NT)

        @block.tensor
        def _(pe):
            pe.wait_ge(q["p_loaded"], 16)
            for n in range(4):
                k, h = n % KP, n // KP
                for j in range(4):
                    mm = nc.tensor.transpose(m.ps[n][:, j * P:(j + 1) * P], pin[:, 4 * h + j, k:PLE:KP], m.ident[:, :])
                mm.then_inc(q["p_turned"], 1)
            pe.wait_ge(q["pT_ready"], 4)
            pe.wait_ge(m.ple_loaded, 32)
            with pe.Fori(0, 2) as n:
                for t in range(NT):
                    pe.wait_ge(q["read"], NT * n + t - 1 if t >= 2 else NT * n)
                    cols = bass.ds(n * HALF, HALF)
                    for k in range(KD):
                        mm = nc.tensor.matmul(m.ps[4 + t % 2][:, :], m.hT[:, k, t * P:(t + 1) * P],
                                              m.ple_wg[:, k, cols], start=(k == 0), stop=(k == KD - 1))
                    mm.then_inc(q["done"], 1)
                    for k in range(KP):
                        mm = nc.tensor.matmul(m.ps[6 + t % 2][:, :], pT[:, k, t * P:(t + 1) * P],
                                              m.ple_wp[:, k, cols], start=(k == 0), stop=(k == KP - 1))
                    mm.then_inc(q["done"], 1)

        @block.scalar
        def _(act):
            with act.Fori(0, 2) as n:
                for t in range(NT):
                    act.wait_ge(q["done"], 2 * (NT * n + t) + 1)
                    act.wait_ge(q["read"], NT * n + t - 1 if t >= 2 else NT * n)
                    nc.scalar.activation(sg[:, t % 2, :], m.ps[4 + t % 2][:, :], ACT.Sigmoid)\
                        .then_inc(q["sig_ready"], 1)

        @block.vector
        def _(dve):
            c = Chain(dve, ch["dve"])
            for n in range(4):
                k, h = n % KP, n // KP
                dve.wait_ge(q["p_turned"], n + 1)
                nc.vector.tensor_copy(pT[:, k, h * HALF:(h + 1) * HALF], m.ps[n][:, :]).then_inc(q["pT_ready"], 1)
            with dve.Fori(0, 2) as n:
                c.enter(n, NT)
                for t in range(NT):
                    dve.wait_ge(q["sig_ready"], NT * n + t + 1)
                    dve.wait_ge(q["done"], 2 * (NT * n + t) + 2)
                    dve.wait_ge(stored[t % 2], 64 * n + 16 * (t // 2))
                    c.link(nc.vector.tensor_tensor(res[:, t % 2, :], sg[:, t % 2, :], m.ps[6 + t % 2][:, :], ALU.mult))
                    nc.vector.tensor_tensor(res[:, t % 2, :], res[:, t % 2, :], m.x2[:, t, bass.ds(n * HALF, HALF)],
                                            ALU.add).then_inc(q["read"], 1)
                c.leave(2, NT)


def phase_constants(nc, m):
    m.slot_tok = nc.dram_tensor("slot_tok", [SLOTS, 1], I32).ap()
    m.xn_dram = nc.dram_tensor("xn_rows", [S, D], F32).ap()
    m.y_slots = nc.dram_tensor("y_slots", [SLOTS, D], F32).ap()
    constants(nc, m)
    m.low = m.top
    m.hT = m.sb("hT", [P, KD, S])
    m.base = m.top


def phase_mix_norm(nc, m):
    x = m.sb("x_in", [P, NT, D])
    norm_transpose(nc, m, "mix", x, m.mix_gain, x, m.hT, load=m.i["x"][0])
    m.top = m.base


def phase_ssm(nc, m):
    m.xbc = m.sb("xbc", [P, MC, S])
    m.y = m.sb("y", [P, NT, INNER])
    m.dt = m.sb("dt", [P, NT, SSM_HEADS])
    m.adt = m.sb("adt", [P, NT, SSM_HEADS])
    keep = m.top
    project_conv(nc, m)
    m.top = keep
    m.wz = m.sb("wz", [P, KD, INNER])
    m.wz_loaded = m.sem("wz_loaded")
    ssd_base = m.top
    time_steps(nc, m)
    m.top = ssd_base
    ssd(nc, m)
    m.top = m.base
    m.ybT = m.sb("ybT", [P, KD, S])
    keep, m.top = m.top, ssd_base
    group_norm(nc, m, m.ybT)
    m.top = m.base = keep


def phase_nsa(nc, m):
    m.yaT = m.sb("yaT", [P, Q_W // P, S])
    m.base = m.top
    m.qT = m.sb("qT", [P, E, S])
    m.ksT, m.kwT = m.sb("ksT", [P, S]), m.sb("kwT", [P, S])
    m.v_sel, m.v_win = m.sb("v_sel", [P, NT, GROUPS, HD + 1]), m.sb("v_win", [P, NT, GROUPS, HD + 1])
    m.cT = m.sb("cT", [P, 2, S])
    m.kcT = m.sb("kcT", [P, NCMP])
    m.v_cmp = m.sb("v_cmp", [NCMP, GROUPS, HD + 1])
    keep = m.top
    nsa_project(nc, m)
    m.top = keep
    compress(nc, m)
    m.top = keep
    m.ya = m.sb("ya", [P, NT, HEADS, HD])
    attention(nc, m)
    turn_ya(nc, m)
    m.renew_semaphores()
    m.top = m.base


def phase_merge(nc, m):
    m.x2 = m.sb("x2", [P, NT, D])
    m.x_loaded = m.sem("x_loaded")
    m.above = m.top
    m.mergedT = m.sb("mergedT", [P, KD, S])
    keep = m.top
    merge(nc, m)
    m.top = keep
    project_out(nc, m)
    m.top = m.above


def phase_route(nc, m):
    m.weight = m.sb("weight", [P, NT, 2])
    m.slot_u = m.sb("slot_u", [P, NT, 2], U32)
    m.slot_idx = m.sb("slot_idx", [P, BLOCKS], U32)
    m.plan = m.sb("plan", [P, EXTRA + 1], I32)
    m.above = m.top
    m.h2T = m.sb("h2T", [P, KD, S])
    route_base = m.top
    m.top = m.low
    xn = m.sb("xn", [P, NT, D])
    norm_transpose(nc, m, "moe", m.x2, m.moe_gain, xn, m.h2T, store=m.xn_dram)
    m.top = route_base
    route(nc, m)
    m.top = m.above


def phase_experts(nc, m):
    m.top = m.low
    m.moe_w = (m.sb("moe_wg", [P, 2, KD, MOE_H]), m.sb("moe_wu", [P, 2, KD, MOE_H]),
               m.sb("moe_wd", [P, 2, MOE_H // P, D]))
    m.top = m.above
    m.ple_wg = m.sb("ple_wg", [P, KD, D])
    m.ple_wp = m.sb("ple_wp", [P, PLE // P, D])
    m.ple_loaded = m.sem("ple_loaded")
    m.above = m.top
    m.moe_buf = {"idx": m.sb("moe_idx", [P, 2], U32), "x": [m.sb(f"moe_x{r}", [P, D]) for r in range(2)],
                 "xT": m.sb("moe_xT", [P, 2, KD, P]), "sg": m.sb("moe_sg", [P, 2, MOE_H]),
                 "h": m.sb("moe_h", [P, 2, MOE_H // P, P]), "out": m.sb("moe_out", [P, 2, D])}
    experts(nc, m, "moe_first", False)
    experts(nc, m, "moe_more", True)
    m.top = m.above


def phase_ple(nc, m):
    with nc.Block() as block:
        @block.sync
        def _(sp):
            sp.dma_start(m.ple_wg[:, :, :], m.i["ple_w_gate"][0].rearrange("(p k) n -> p k n", k=KD))\
                .then_inc(m.ple_loaded, 16)
            sp.dma_start(m.ple_wp[:, :, :], m.i["ple_w_proj"][0].rearrange("(p k) n -> p k n", k=PLE // P))\
                .then_inc(m.ple_loaded, 16)
    combine(nc, m)
    m.top = m.low
    xn = m.sb("xn3", [P, NT, D])
    m.hT = m.sb("h3T", [P, KD, S])
    norm_transpose(nc, m, "ple_norm", m.x2, m.ple_gain, xn, m.hT)
    m.top = m.above
    per_layer(nc, m)


PHASES = [phase_constants, phase_mix_norm, phase_ssm, phase_nsa, phase_merge, phase_route, phase_experts, phase_ple]


def program(nc, ins, out):
    m = Machine(nc, ins, out)
    for phase in PHASES:
        phase(nc, m)


def kernel(**inputs):
    import numpy as np
    from concourse import bacc
    from concourse.bass_utils import run_bass_kernel_spmd

    nc = bacc.Bacc("TRN2", target_bir_lowering=False, num_devices=1)
    arrays, ins = {}, {}
    for name, value in inputs.items():
        a = np.ascontiguousarray(value)
        arrays[f"in_{name}"] = a
        ins[name] = nc.dram_tensor(f"in_{name}", a.shape, mybir.dt.from_np(a.dtype), kind="ExternalInput").ap()
    out = nc.dram_tensor("out", (1, S, D), F32, kind="ExternalOutput").ap()
    program(nc, ins, out)
    r = run_bass_kernel_spmd(nc, [arrays], core_ids=[0])
    return r.results[0]["out"]
```

```python
import concourse.bass as bass
from concourse import mybir

F32 = mybir.dt.float32
BF16 = mybir.dt.bfloat16
I32 = mybir.dt.int32
U32 = mybir.dt.uint32
ALU = mybir.AluOpType
ACT = mybir.ActivationFunctionType
AX = mybir.AxisListType

P = 128
D = 1024
S = 1024
KD = D // P
NT = S // P
HALF = 512
EPS = 1e-6
MASK = -1e30

HEADS, GROUPS, HD = 8, 2, 64
E = HEADS // GROUPS
Q_W, KV_W, GATE_W = HEADS * HD, GROUPS * HD, HEADS * 3
NSA_W = Q_W + 6 * KV_W + GATE_W
SSM_HEADS, SSM_P, SSM_G, SSM_N = 16, 64, 2, 128
INNER = SSM_HEADS * SSM_P
GW = INNER // SSM_G
CONV_DIM = INNER + 2 * SSM_G * SSM_N
CONV = 4
MC = CONV_DIM // P
Z0 = NSA_W
XBC0 = Z0 + INNER
DT0 = XBC0 + CONV_DIM
BR0 = DT0 + SSM_HEADS
CMP_STRIDE, CMP_BLOCK, CMP_HIDDEN = 16, 32, 128
NCMP = S // CMP_STRIDE - 1
WINDOW = 512
EXPERTS, MGROUPS, PER_GROUP, MOE_H = 32, 4, 8, 256
ROUTES = MGROUPS + EXPERTS
EXTRA = 2 * S // P
BLOCKS = EXPERTS + EXTRA
SLOTS = BLOCKS * P
PLE = 256


class Chain:

    def __init__(self, eng, sem):
        self.eng, self.sem, self.start, self.base, self.n = eng, sem, 0, 0, 0

    def link(self, ins):
        ins.then_inc(self.sem, 1)
        self.n += 1
        self.eng.wait_ge(self.sem, self.base + self.n)

    def put(self, ins):
        ins.then_inc(self.sem, 1)
        self.n += 1
        return self.base + self.n

    def need(self, count):
        self.eng.wait_ge(self.sem, count)

    def enter(self, i, per):
        self.start += self.n
        self.n, self.base = 0, self.start + i * per

    def leave(self, passes, per):
        assert self.n == per, (self.n, per)
        self.start += passes * per
        self.base, self.n = self.start, 0


class Machine:

    def __init__(self, nc, ins, out):
        self.nc, self.i, self.out, self.sems = nc, ins, out, []
        self.psum = nc.alloc_psum_tensor("banks", [P, 8 * HALF], F32)
        self.ps = [self.psum[:, b * HALF:(b + 1) * HALF] for b in range(8)]
        self.top = nc.sbuf_base + (-nc.sbuf_base) % 64
        self.end = nc.sbuf_usable_end

    def sb(self, name, shape, dt=F32):
        size = 2 if dt == BF16 else 4
        for n in shape[1:]:
            size *= n
        t = self.nc.alloc_sbuf_tensor_at(name, shape, dt, offset=self.top)
        self.top += size + (-size) % 64
        assert self.top <= self.end, (name, self.top, self.end)
        return t

    def sb_at_end(self, name, shape):
        size = 4
        for n in shape[1:]:
            size *= n
        at = (self.end - size) // 64 * 64
        return self.nc.alloc_sbuf_tensor_at(name, shape, F32, offset=at), at

    def lasting_sem(self, name):
        return self.nc.alloc_semaphore(name=name)

    def sem(self, name):
        self.sems.append(self.nc.alloc_semaphore(name=name))
        return self.sems[-1]

    def chains(self, nc, phase):
        return Steps(self, phase)

    def renew_semaphores(self):
        self.nc.clear_and_free_semaphores(self.sems)
        self.sems = []
        self.nc.all_engine_barrier()


class Steps(dict):

    def __init__(self, m, phase):
        super().__init__()
        self.m, self.phase = m, phase

    def __missing__(self, engine):
        self[engine] = self.m.sem(f"{self.phase}_{engine}_step")
        return self[engine]


def constants(nc, m):
    m.ident = m.sb("ident", [P, P])
    m.ones = m.sb("ones", [P, P])
    m.tri_le = m.sb("tri_le", [P, P])
    m.tri_lt = m.sb("tri_lt", [P, P])
    m.identb = m.sb("identb", [P, P], BF16)
    m.mask_future = m.sb("mask_future", [P, P], BF16)
    m.mask_far = m.sb("mask_far", [P, P], BF16)
    m.mask_past = m.sb("mask_past", [P, P], BF16)
    m.mask_cmp = m.sb("mask_cmp", [P, NT, NCMP + 1], BF16)
    m.any_cmp = m.sb("any_cmp", [P, 1])
    m.small = m.sb("small", [P, 2, P])
    m.mix_gain = m.sb("mix_gain", [P, KD])
    m.moe_gain = m.sb("moe_gain", [P, KD])
    m.ple_gain = m.sb("ple_gain", [P, KD])
    m.ssm_gain = m.sb("ssm_gain", [P, KD])
    m.qk_gain = m.sb("qk_gain", [P, 4])
    m.dt_bias = m.sb("dt_bias", [P, SSM_HEADS])
    m.neg_a = m.sb("neg_a", [P, SSM_HEADS])
    m.d_skip = m.sb("d_skip", [P, SSM_HEADS])
    m.route_bias = m.sb("route_bias", [P, ROUTES])
    m.gate_scale = m.sb("gate_scale", [P, NT, GATE_W])
    m.junk = m.sb("junk", [P, 2, D])
    m.sumsq = m.sb("sumsq", [P, NT])
    m.rms = m.sb("rms", [P, NT])
    m.rstd = m.sb("rstd", [P, NT])
    m.low = m.top
    m.hT = m.sb("hT", [P, KD, S])
    m.base = m.top
    m.x_in = m.sb("x_in", [P, NT, D])
    m.mix_x_loaded = [m.sem(f"mix_x_loaded{t}") for t in range(NT)]
    m.top = m.base
    made, loaded, turned = m.sem("const_made"), m.sem("const_loaded"), m.sem("const_turned")
    ch = m.chains(nc, "const")
    i = m.i
    m.const_dmas = 0
    with nc.Block() as block:
        @block.gpsimd
        def _(pool):
            c = Chain(pool, ch["pool"])

            def tri(t, op, cm, step, base, inside, outside, shape=(P,)):
                c.link(nc.gpsimd.memset(t, inside))
                c.link(nc.gpsimd.affine_select(out=t, in_=t, compare_op=op, fill=outside, base=base,
                                               pattern=[[step, P]], channel_multiplier=cm))
            tri(m.ident[:, :], ALU.not_equal, 1, -1, 0, 0.0, 1.0)
            tri(m.identb[:, :], ALU.not_equal, 1, -1, 0, 0.0, 1.0)
            tri(m.tri_le[:, :], ALU.is_ge, -1, 1, 0, 1.0, 0.0)
            tri(m.tri_lt[:, :], ALU.is_gt, -1, 1, 0, 1.0, 0.0)
            tri(m.mask_future[:, :], ALU.is_ge, 1, -1, 0, 0.0, MASK)
            tri(m.mask_far[:, :], ALU.is_gt, -1, 1, 0, 0.0, MASK)
            tri(m.mask_past[:, :], ALU.is_ge, -1, 1, 0, 0.0, MASK)
            c.link(nc.gpsimd.memset(m.ones[:, :], 1.0))
            c.link(nc.gpsimd.memset(m.mask_cmp[:, :, :], 0.0))
            c.link(nc.gpsimd.affine_select(out=m.mask_cmp[:, :, :], in_=m.mask_cmp[:, :, :], compare_op=ALU.is_ge,
                                           fill=MASK, base=-(CMP_BLOCK - 1), channel_multiplier=1,
                                           pattern=[[P, NT], [-CMP_STRIDE, NCMP + 1]]))
            c.link(nc.gpsimd.memset(m.any_cmp[:, :], 1.0))
            nc.gpsimd.affine_select(out=m.any_cmp[:, :], in_=m.any_cmp[:, :], compare_op=ALU.is_ge, fill=0.0,
                                    base=-(CMP_BLOCK - 1), channel_multiplier=1, pattern=[[0, 1]]).then_inc(made, 1)

        @block.sync
        def _(sp):
            def load(dst, src):
                sp.dma_start(dst, src).then_inc(loaded, 16)
                m.const_dmas += 1
            load(m.small[0:CONV * MC, 0, :], i["ssm_conv_w"][0].rearrange("j (m p) -> (j m) p", p=P))
            load(m.small[CONV * MC:(CONV + 1) * MC, 0, :], i["ssm_conv_b"][0].rearrange("(m p) -> m p", p=P))
            for t, name in ((m.mix_gain, "mix_norm"), (m.moe_gain, "moe_norm"), (m.ple_gain, "ple_norm"),
                            (m.ssm_gain, "ssm_norm")):
                load(t[:, :], i[name][0].rearrange("(p k) -> p k", k=KD))
            for n, name in enumerate(("nsa_q_gain", "nsa_kc_gain", "nsa_ks_gain", "nsa_kw_gain")):
                for g in range(GROUPS):
                    load(m.qk_gain[g * HD:(g + 1) * HD, n:n + 1], i[name][0].rearrange("(d a) -> d a", a=1))
            for t, name in ((m.dt_bias, "ssm_dt_bias"), (m.neg_a, "ssm_a_log"), (m.d_skip, "ssm_d")):
                load(t[:, :], i[name].partition_broadcast(P).rearrange("p a h -> p (a h)"))
            load(m.route_bias[:, 0:MGROUPS], i["moe_b_group"].partition_broadcast(P).rearrange("p a h -> p (a h)"))
            load(m.route_bias[:, MGROUPS:], i["moe_b_expert"].partition_broadcast(P).rearrange("p a h -> p (a h)"))

        @block.tensor
        def _(pe):
            pe.wait_ge(made, 1)
            pe.wait_ge(loaded, 16 * m.const_dmas)
            n = (CONV + 1) * MC
            nc.tensor.transpose(m.ps[0][:, 0:n], m.small[0:n, 0, :], m.ident[0:n, 0:n]).then_inc(turned, 1)

        @block.scalar
        def _(act):
            c = Chain(act, ch["act"])
            for t in range(NT):
                act.dma_start(m.x_in[:, t, :], m.i["x"][0][t * P:(t + 1) * P, :]).then_inc(m.mix_x_loaded[t], 16)
            act.wait_ge(loaded, 16 * m.const_dmas)
            c.link(nc.scalar.activation(m.neg_a[:, :], m.neg_a[:, :], ACT.Exp))
            c.link(nc.scalar.mul(m.qk_gain[:, 0:1], m.qk_gain[:, 0:1], HD ** -0.5))
            nc.scalar.mul(m.neg_a[:, :], m.neg_a[:, :], -1.0).then_inc(turned, 1)

        @block.vector
        def _(dve):
            dve.wait_ge(turned, 2)
            n = (CONV + 1) * MC
            nc.vector.tensor_copy(m.small[:, 1, 0:n], m.ps[0][:, 0:n]).then_inc(turned, 1)
    m.conv_w = m.small[:, 1, 0:CONV * MC].rearrange("p (j m) -> p j m", j=CONV)
    m.conv_b = m.small[:, 1, CONV * MC:(CONV + 1) * MC]


def norm_transpose(nc, m, x, gain, hT):
    here = m.mix_x_loaded
    squared, mean_made, rooted, normed, turned = (m.sem(f"mix_{n}") for n in
                                                  ("squared", "mean_made", "rooted", "normed", "turned"))
    read = [m.sem("mix_act_read"), m.sem("mix_dve_read")]
    ch = m.chains(nc, "mix")
    NG = 2 * KD
    with nc.Block() as block:
        @block.sync
        def _(sp):
            load_conv_weights(m, sp, range(len(m.conv_w_loaded)))
            sp.dma_start(m.dt_w[:, :, :], m.i["w_in"][0][:, DT0:DT0 + SSM_HEADS].rearrange("(p k) n -> p k n", k=KD))\
                .then_inc(m.dt_w_loaded, 16)

        @block.scalar
        def _(act):
            def square(t):
                act.wait_ge(here[t], 16)
                nc.scalar.activation(m.junk[:, t % 2, :], x[:, t, :], ACT.Square,
                                     accum_out=m.sumsq[:, t:t + 1]).then_inc(squared, 1)

            def root(t):
                act.wait_ge(mean_made, t + 1)
                nc.scalar.activation(m.rms[:, t:t + 1], m.rms[:, t:t + 1], ACT.Sqrt).then_inc(rooted, 1)

            square(0)
            for t in range(NT):
                if t + 1 < NT:
                    if t >= 1:
                        act.wait_ge(squared, t)
                    square(t + 1)
                root(t)
            for n in range(0, NG, 2):
                act.wait_ge(turned, n + 1)
                k = n % KD
                h = n // KD
                nc.scalar.activation(hT[:, k, h * HALF:(h + 1) * HALF], m.ps[n % 4][:, :], ACT.Copy,
                                     scale=gain[:, k:k + 1]).then_inc(read[0], 1)

        @block.vector
        def _(dve):
            c = Chain(dve, ch["dve"])

            def mean(t):
                dve.wait_ge(squared, t + 1)
                nc.vector.tensor_scalar(m.rms[:, t:t + 1], m.sumsq[:, t:t + 1], 1.0 / D, EPS, ALU.mult,
                                        ALU.add).then_inc(mean_made, 1)

            mean(0)
            for t in range(NT):
                if t + 1 < NT:
                    mean(t + 1)
                dve.wait_ge(rooted, t + 1)
                c.link(nc.vector.reciprocal(m.rstd[:, t:t + 1], m.rms[:, t:t + 1]))
                nc.vector.tensor_scalar(x[:, t, :], x[:, t, :], m.rstd[:, t:t + 1], None,
                                        ALU.mult).then_inc(normed, 1)
            for n in range(1, NG, 2):
                dve.wait_ge(turned, n + 1)
                k = n % KD
                h = n // KD
                nc.vector.tensor_scalar(hT[:, k, h * HALF:(h + 1) * HALF], m.ps[n % 4][:, :], gain[:, k:k + 1],
                                        None, ALU.mult).then_inc(read[1], 1)

        @block.tensor
        def _(pe):
            for n in range(NG):
                k, h = n % KD, n // KD
                pe.wait_ge(normed, 4 * (h + 1))
                if n >= 4:
                    pe.wait_ge(read[n % 2], (n - 4) // 2 + 1)
                for j in range(4):
                    t = 4 * h + j
                    mm = nc.tensor.transpose(m.ps[n % 4][:, j * P:(j + 1) * P], x[:, t, k:D:KD], m.ident[:, :])
                mm.then_inc(turned, 1)


def load_conv_weights(m, eng, slots, it=0):
    wv = m.i["w_in"][0][:, XBC0:XBC0 + CONV_DIM].rearrange("(p k) (m c) -> m p k c", k=KD, c=P)
    ring = len(m.conv_w_loaded)
    for r in slots:
        eng.dma_start(m.conv_ring[:, r, :, :], wv[ring * it + r, :, :, :]).then_inc(m.conv_w_loaded[r], 16)


def project_conv(nc, m):
    RING, BODY = 3, 6
    LOOPS = MC // BODY
    W, here = m.conv_ring, m.conv_w_loaded
    pre = m.sb("conv_pre", [P, 2, CONV - 1 + S])
    raw, mag, ln = (m.sb(f"dt_{n}", [P, NT, SSM_HEADS]) for n in ("raw", "mag", "ln"))
    dt_done, sized, logged = (m.sem(f"dt_{n}") for n in ("products_done", "sized", "logged"))
    per_head = [P, NT, SSM_HEADS]
    done, used, free, pre_free = (m.sem(f"conv_{n}") for n in
                                          ("products_done", "w_free", "bank_free", "pre_free"))
    ch = m.chains(nc, "conv")
    with nc.Block() as block:
        @block.sync
        def _(sp):
            sp.dma_start(m.wz[:, :, :], m.i["w_in"][0][:, Z0:Z0 + INNER].rearrange("(p k) n -> p k n", k=KD))\
                .then_inc(m.wz_loaded, 16)
            with sp.Fori(0, MC // RING - 1) as it:
                for r in range(RING):
                    sp.wait_ge(used, RING * it + r + 1)
                    load_conv_weights(m, sp, (r,), it + 1)

        @block.tensor
        def _(pe):
            pe.wait_ge(m.dt_w_loaded, 16)
            for t in range(NT):
                for k in range(KD):
                    mm = nc.tensor.matmul(m.ps[6][:, t * SSM_HEADS:(t + 1) * SSM_HEADS],
                                          m.hT[:, k, t * P:(t + 1) * P], m.dt_w[:, k, :],
                                          start=(k == 0), stop=(k == KD - 1))
            mm.then_inc(dt_done, 1)
            pe.sem_inc(free, 4)
            with pe.Fori(0, LOOPS) as it:
                for r in range(BODY):
                    pe.wait_ge(here[r % RING], 16 * (2 * it + r // RING + 1))
                    for h in range(2):
                        pe.wait_ge(free, 2 * BODY * it + 2 * r + h + 1)
                        b = (2 * r + h) % 4
                        for k in range(KD):
                            mm = nc.tensor.matmul(m.ps[b][:, :], W[:, r % RING, k, :],
                                                  m.hT[:, k, h * HALF:(h + 1) * HALF],
                                                  start=(k == 0), stop=(k == KD - 1))
                        mm.then_inc(done, 1)
                    nc.tensor.matmul(m.ps[7][0:1, 0:1], m.ident[:, 0:1], m.ident[:, 0:1], start=True,
                                     stop=True).then_inc(used, 1)

        @block.scalar
        def _(act):
            a = Chain(act, ch["act"])
            act.wait_ge(sized, 1)
            a.link(nc.scalar.activation(mag[:, :, :], mag[:, :, :], ACT.Exp, scale=-1.0))
            nc.scalar.activation(ln[:, :, :], mag[:, :, :], ACT.Ln, bias=1.0).then_inc(logged, 1)
            with act.Fori(0, LOOPS) as it:
                for r in range(BODY):
                    act.wait_ge(pre_free, BODY * it + r + 1)
                    for h in range(2):
                        act.wait_ge(done, 2 * BODY * it + 2 * r + h + 1)
                        nc.scalar.copy(pre[:, r % 2, CONV - 1 + h * HALF:CONV - 1 + (h + 1) * HALF],
                                       m.ps[(2 * r + h) % 4][:, :]).then_inc(free, 1)

        @block.vector
        def _(dve):
            c = Chain(dve, ch["dve"])
            for r in range(2):
                c.link(dve.memset(pre[:, r, 0:CONV - 1], 0.0))
            dve.wait_ge(dt_done, 1)
            c.link(nc.vector.tensor_tensor(raw[:, :, :], m.ps[6][:, 0:NT * SSM_HEADS].rearrange("p (t h) -> p t h", t=NT),
                                           m.dt_bias[:, :].unsqueeze(1).to_broadcast(per_head), ALU.add))
            nc.vector.scalar_tensor_tensor(out=mag[:, :, :], in0=raw[:, :, :], scalar=-1.0, in1=raw[:, :, :],
                                           op0=ALU.mult, op1=ALU.max).then_inc(sized, 1)
            dve.wait_ge(logged, 1)
            c.link(nc.vector.scalar_tensor_tensor(out=m.dt[:, :, :], in0=raw[:, :, :], scalar=0.0,
                                                  in1=ln[:, :, :], op0=ALU.max, op1=ALU.add))
            c.link(dve.memset(m.adt[:, NT, :], 0.0))
            c.link(nc.vector.tensor_tensor(m.adt[:, 0:NT, :], m.dt[:, :, :],
                                           m.neg_a[:, :].unsqueeze(1).to_broadcast(per_head), ALU.mult))
            dve.sem_inc(pre_free, 2)
            with dve.Fori(0, LOOPS) as it:
                c.enter(it, BODY * (CONV - 1))
                for r in range(BODY):
                    dve.wait_ge(free, 2 * BODY * it + 2 * r + 2 + 4)
                    out = m.xbc[:, BODY * it + r, :]
                    for j in range(CONV):
                        src = pre[:, r % 2, j:j + S]
                        w = m.conv_w[:, j, bass.ds(BODY * it + r, 1)]
                        if j == 0:
                            ins = nc.vector.tensor_scalar(out, src, w, None, ALU.mult)
                        else:
                            ins = nc.vector.scalar_tensor_tensor(out=out, in0=src, scalar=w, in1=out,
                                                                 op0=ALU.mult, op1=ALU.add)
                        if j < CONV - 1:
                            c.link(ins)
                        else:
                            ins.then_inc(pre_free, 1)
                c.leave(LOOPS, BODY * (CONV - 1))


def ssd(nc, m):
    xc = m.sb("ssd_xc", [P, MC, P])
    hc = m.sb("ssd_hc", [P, KD, P])
    adt_c = m.sb("ssd_adt_c", [P, SSM_HEADS])
    xtok = m.sb("ssd_xtok", [P, INNER])
    btok = m.sb("ssd_btok", [P, SSM_G * SSM_N])
    xd, xdd, xskip, y1, zs = (m.sb(f"ssd_{n}", [P, INNER]) for n in ("xd", "xdd", "xskip", "y1", "zs"))
    seg = m.sb("ssd_seg", [P, SSM_HEADS, P])
    state = m.sb("ssd_state", [P, INNER])
    sums = m.sb("ssd_sums", [P, 3, SSM_HEADS])
    exps = m.sb("ssd_exps", [P, 3, SSM_HEADS])
    neg = m.sb("ssd_neg", [P, SSM_HEADS])
    dtin = m.sb("ssd_dtin", [P, SSM_HEADS])
    names = ("xc_ready", "xc_free", "x_turned", "xtok_ready", "xtok_used", "small_done", "cb_done", "sums_ready",
             "exps_ready", "adt_ready", "seg_done", "seg_exp", "mt_ready", "z_done", "z_ready", "hc_ready",
             "yoff_done", "yoff_read", "ydiag_done", "ydiag_read", "xd_ready", "xdd_ready", "dtin_ready",
             "st_done", "st_read", "decayed", "skip_ready", "gated")
    q = {n: m.sem(f"ssd_{n}") for n in names}
    ch = m.chains(nc, "ssd")
    CB0 = INNER // P
    HG = SSM_HEADS // SSM_G

    def heads(ap):
        return ap.rearrange("p (h d) -> p h d", d=SSM_P)

    def spread(ap, n):
        return ap.unsqueeze(2).to_broadcast([P, n, SSM_P])

    with nc.Block() as block:
        @block.scalar
        def _(act):
            c = Chain(act, ch["act"])
            with act.Fori(0, NT) as i:
                act.wait_ge(q["yoff_done"], i)
                for j in range(MC):
                    nc.scalar.activation(xc[:, j, :], m.xbc[:, j, bass.ds(i * P, P)], ACT.Silu,
                                         bias=m.conv_b[:, j:j + 1]).then_inc(q["xc_ready"], 1)
                act.wait_ge(q["xtok_used"], 3 * i)
                for h in range(2):
                    act.wait_ge(q["x_turned"], 2 * i + h + 1)
                    nc.scalar.copy(xtok[:, h * HALF:(h + 1) * HALF], m.ps[h][:, :]).then_inc(q["xtok_ready"], 1)
                act.wait_ge(q["sums_ready"], i + 1)
                act.wait_ge(q["yoff_read"], 2 * i)
                act.wait_ge(q["decayed"], i)
                nc.scalar.activation(exps[:, :, :], sums[:, :, :], ACT.Exp).then_inc(q["exps_ready"], 1)
                act.wait_ge(q["ydiag_done"], 2 * i)
                for r in range(4):
                    act.wait_ge(q["seg_done"], 4 * i + r + 1)
                    for hh in range(4):
                        h = 4 * r + hh
                        ins = nc.scalar.activation(seg[:, h, :], m.ps[4 + r % 2][:, hh * P:(hh + 1) * P], ACT.Exp,
                                                   bias=neg[:, h:h + 1])
                    ins.then_inc(q["seg_exp"], 1)
                act.wait_ge(q["gated"], i)
                for h in range(2):
                    act.wait_ge(q["z_done"], 2 * i + h + 1)
                    nc.scalar.activation(zs[:, h * HALF:(h + 1) * HALF], m.ps[h][:, :],
                                         ACT.Silu).then_inc(q["z_ready"], 1)

        @block.gpsimd
        def _(pool):
            c = Chain(pool, ch["pool"])
            nc.gpsimd.memset(state[:, :], 0.0).then_inc(q["st_read"], 2)
            with pool.Fori(0, NT) as i:
                pool.wait_ge(q["z_done"], 2 * i)
                nc.gpsimd.tensor_copy(hc[:, :, :], m.hT[:, :, bass.ds(i * P, P)]).then_inc(q["hc_ready"], 1)
                pool.wait_ge(q["xtok_ready"], 2 * i + 2)
                pool.wait_ge(q["gated"], i)
                nc.gpsimd.tensor_tensor(heads(xskip[:, :]), heads(xtok[:, :]), spread(m.d_skip[:, :], SSM_HEADS),
                                        ALU.mult).then_inc(q["xtok_used"], 1)
                pool.wait_ge(q["dtin_ready"], i + 1)
                pool.wait_ge(q["st_done"], 2 * i)
                nc.gpsimd.tensor_tensor(heads(xdd[:, :]), heads(xtok[:, :]), spread(dtin[:, :], SSM_HEADS),
                                        ALU.mult).then_inc(q["xtok_used"], 1)
                pool.wait_ge(q["yoff_done"], i + 1)
                nc.gpsimd.tensor_tensor(heads(state[:, :]), heads(state[:, :]),
                                        spread(exps[:, 1, :], SSM_HEADS), ALU.mult).then_inc(q["decayed"], 1)

        @block.vector
        def _(dve):
            c = Chain(dve, ch["dve"])
            PER = 4
            def next_adt(i):
                nc.vector.tensor_copy(adt_c[:, :], m.adt[:, bass.ds(i, 1), :].rearrange("p a h -> p (a h)"))\
                    .then_inc(q["adt_ready"], 1)

            next_adt(0)
            with dve.Fori(0, NT) as i:
                c.enter(i, PER)
                dve.wait_ge(q["small_done"], i + 1)
                dve.wait_ge(q["st_done"], 2 * i)
                c.link(nc.vector.tensor_copy(btok[:, :], m.ps[2][:, 0:256]))
                c.link(nc.vector.tensor_copy(sums[:, 0:2, :], m.ps[2][:, 256:288].rearrange("p (a h) -> p a h", a=2)))
                c.link(nc.vector.tensor_scalar(neg[:, :], sums[:, 0, :], -1.0, None, ALU.mult))
                nc.vector.tensor_tensor(sums[:, 2, :], sums[:, 1, :], sums[:, 0, :],
                                        ALU.subtract).then_inc(q["sums_ready"], 1)
                dve.wait_ge(q["exps_ready"], i + 1)
                dt_c = m.dt[:, bass.ds(i, 1), :].rearrange("p a h -> p (a h)")
                dve.wait_ge(q["xtok_used"], 3 * i + 1)
                nc.vector.tensor_tensor(dtin[:, :], dt_c, exps[:, 2, :], ALU.mult).then_inc(q["dtin_ready"], 1)
                dve.wait_ge(q["xtok_ready"], 2 * i + 2)
                dve.wait_ge(q["ydiag_done"], 2 * i)
                nc.vector.tensor_tensor(heads(xd[:, :]), heads(xtok[:, :]), spread(dt_c, SSM_HEADS),
                                        ALU.mult).then_inc(q["xtok_used"], 1)
                dve.wait_ge(q["cb_done"], i + 1)
                for r in range(4):
                    g = r // 2
                    dve.wait_ge(q["seg_exp"], 4 * i + r + 1)
                    part = seg[:, 4 * r:4 * r + 4, :]
                    nc.vector.tensor_tensor(part, part, m.ps[3][:, g * P:(g + 1) * P].unsqueeze(1)
                                            .to_broadcast([P, 4, P]), ALU.mult).then_inc(q["mt_ready"], 1)
                dve.wait_ge(q["seg_done"], 4 * i + 4)
                next_adt(i + 1)
                for g in range(2):
                    part = slice(g * HALF, (g + 1) * HALF)
                    dve.wait_ge(q["yoff_done"], i + 1)
                    ins = nc.vector.tensor_tensor(heads(y1[:, part]), heads(m.ps[6 + g][:, :]),
                                                  spread(exps[:, 0, g * HG:(g + 1) * HG], HG), ALU.mult)
                    ins.then_inc(q["yoff_read"], 1)
                dve.wait_ge(q["decayed"], i + 1)
                for g in range(2):
                    part = slice(g * HALF, (g + 1) * HALF)
                    dve.wait_ge(q["st_done"], 2 * i + g + 1)
                    nc.vector.tensor_tensor(state[:, part], state[:, part], m.ps[2 + g][:, :],
                                            ALU.add).then_inc(q["st_read"], 1)
                dve.wait_ge(q["yoff_read"], 2 * i + 2)
                dve.wait_ge(q["xtok_used"], 3 * i + 3)
                c.link(nc.vector.tensor_tensor(y1[:, :], y1[:, :], xskip[:, :], ALU.add))
                for g in range(2):
                    part = slice(g * HALF, (g + 1) * HALF)
                    dve.wait_ge(q["ydiag_done"], 2 * i + g + 1)
                    nc.vector.tensor_tensor(y1[:, part], y1[:, part], m.ps[4 + g][:, :],
                                            ALU.add).then_inc(q["ydiag_read"], 1)
                dve.wait_ge(q["ydiag_read"], 2 * i + 2)
                dve.wait_ge(q["z_ready"], 2 * i + 2)
                nc.vector.tensor_tensor(m.y[:, bass.ds(i, 1), :].rearrange("p a n -> p (a n)"), y1[:, :], zs[:, :],
                                        ALU.mult).then_inc(q["gated"], 1)
                c.leave(NT, PER)

        @block.tensor
        def _(pe):
            pe.wait_ge(m.wz_loaded, 16)
            with pe.Fori(0, NT) as i:
                pe.wait_ge(q["z_ready"], 2 * i)
                for h in range(2):
                    pe.wait_ge(q["xc_ready"], MC * i + 4 * h + 4)
                    for j in range(4):
                        mm = nc.tensor.transpose(m.ps[h][:, j * P:(j + 1) * P], xc[:, 4 * h + j, :], m.ident[:, :])
                    mm.then_inc(q["x_turned"], 1)
                pe.wait_ge(q["st_read"], 2 * i + 2)
                pe.wait_ge(q["xc_ready"], MC * i + MC)
                for g in range(SSM_G):
                    nc.tensor.transpose(m.ps[2][:, g * P:(g + 1) * P], xc[:, CB0 + g, :], m.ident[:, :])
                pe.wait_ge(q["adt_ready"], i + 1)
                nc.tensor.matmul(m.ps[2][:, 256:272], m.tri_le[:, :], adt_c[:, :], start=True, stop=True)
                nc.tensor.matmul(m.ps[2][:, 272:288], m.ones[:, :], adt_c[:, :], start=True,
                                 stop=True).then_inc(q["small_done"], 1)
                for g in range(SSM_G):
                    mm = nc.tensor.matmul(m.ps[3][:, g * P:(g + 1) * P], xc[:, CB0 + g, :], xc[:, CB0 + 2 + g, :],
                                          start=True, stop=True)
                mm.then_inc(q["cb_done"], 1)
                for r in range(4):
                    if r < 2:
                        pe.wait_ge(q["ydiag_read"], 2 * i)
                    else:
                        pe.wait_ge(q["seg_exp"], 4 * i + r - 1)
                    bank = m.ps[4 + r % 2]
                    nc.tensor.matmul(bank[:, :].rearrange("p (h l) -> p h l", l=P), m.identb[:, :],
                                     m.mask_past[:, :].unsqueeze(1).to_broadcast([P, 4, P]), start=True, stop=False)
                    for hh in range(4):
                        h = 4 * r + hh
                        mm = nc.tensor.matmul(bank[:, hh * P:(hh + 1) * P], adt_c[:, h:h + 1].to_broadcast([P, P]),
                                              m.tri_le[:, :], start=False, stop=(hh == 3))
                    mm.then_inc(q["seg_done"], 1)
                pe.wait_ge(q["hc_ready"], i + 1)
                for h in range(2):
                    pe.wait_ge(q["xtok_ready"], 2 * i + h + 1)
                    for k in range(KD):
                        mm = nc.tensor.matmul(m.ps[h][:, :], hc[:, k, :], m.wz[:, k, h * HALF:(h + 1) * HALF],
                                              start=(k == 0), stop=(k == KD - 1))
                    mm.then_inc(q["z_done"], 1)
                pe.wait_ge(q["yoff_read"], 2 * i)
                for g in range(SSM_G):
                    mm = nc.tensor.matmul(m.ps[6 + g][:, :], xc[:, CB0 + 2 + g, :],
                                          state[:, g * HALF:(g + 1) * HALF], start=True, stop=True)
                mm.then_inc(q["yoff_done"], 1)
                pe.wait_ge(q["xtok_used"], 3 * i + 3)
                pe.wait_ge(q["mt_ready"], 4 * i + 4)
                for g in range(SSM_G):
                    nc.tensor.matmul(m.ps[2 + g][:, :], btok[:, g * P:(g + 1) * P], xdd[:, g * HALF:(g + 1) * HALF],
                                     start=True, stop=True).then_inc(q["st_done"], 1)
                for h in range(SSM_HEADS):
                    mm = nc.tensor.matmul(m.ps[4 + h // HG][:, (h % HG) * SSM_P:(h % HG + 1) * SSM_P], seg[:, h, :],
                                          xd[:, h * SSM_P:(h + 1) * SSM_P], start=True, stop=True)
                    if h % HG == HG - 1:
                        mm.then_inc(q["ydiag_done"], 1)


def group_norm(nc, m, ybT):
    squared, mean, root, normed, turned = (m.sem(f"gn_{n}") for n in
                                           ("squared", "mean_made", "rooted", "normed", "turned"))
    read = [m.sem("gn_act_read"), m.sem("gn_dve_read")]
    ch = m.chains(nc, "gn")
    ss = m.sb("gn_ss", [P, NT * SSM_G])
    rs = m.sb("gn_rs", [P, NT * SSM_G])
    NG = 2 * KD
    with nc.Block() as block:
        @block.sync
        def _(sp):
            sp.dma_start(m.nsa_w[:, :, :], m.i["w_in"][0][:, 0:NSA_W].rearrange("(p k) n -> p k n", k=KD))\
                .then_inc(m.nsa_w_loaded, 16)

        @block.scalar
        def _(act):
            def square(t):
                for g in range(SSM_G):
                    n = SSM_G * t + g
                    if n >= 2:
                        act.wait_ge(squared, n - 1)
                    nc.scalar.activation(m.junk[:, g, 0:GW], m.y[:, t, g * GW:(g + 1) * GW], ACT.Square,
                                         accum_out=ss[:, n:n + 1]).then_inc(squared, 1)

            def rooted(t):
                act.wait_ge(mean, t + 1)
                part = ss[:, SSM_G * t:SSM_G * (t + 1)]
                nc.scalar.activation(part, part, ACT.Sqrt).then_inc(root, 1)

            square(0)
            for t in range(NT):
                if t + 1 < NT:
                    square(t + 1)
                rooted(t)
            for n in range(0, NG, 2):
                act.wait_ge(turned, n + 1)
                k, h = n % KD, n // KD
                nc.scalar.activation(ybT[:, k, h * HALF:(h + 1) * HALF], m.ps[n % 4][:, :], ACT.Copy,
                                     scale=m.ssm_gain[:, k:k + 1]).then_inc(read[0], 1)

        @block.vector
        def _(dve):
            c = Chain(dve, ch["dve"])

            def means(t):
                dve.wait_ge(squared, SSM_G * (t + 1))
                part = ss[:, SSM_G * t:SSM_G * (t + 1)]
                nc.vector.tensor_scalar(part, part, 1.0 / GW, EPS, ALU.mult, ALU.add).then_inc(mean, 1)

            means(0)
            for t in range(NT):
                if t + 1 < NT:
                    means(t + 1)
                dve.wait_ge(root, t + 1)
                tile = slice(SSM_G * t, SSM_G * (t + 1))
                c.link(nc.vector.reciprocal(rs[:, tile], ss[:, tile]))
                part = m.y[:, t, :].rearrange("p (g n) -> p g n", g=SSM_G)
                nc.vector.tensor_tensor(part, part, rs[:, tile].unsqueeze(2).to_broadcast([P, SSM_G, GW]),
                                        ALU.mult).then_inc(normed, 1)
            for n in range(1, NG, 2):
                dve.wait_ge(turned, n + 1)
                k, h = n % KD, n // KD
                nc.vector.tensor_scalar(ybT[:, k, h * HALF:(h + 1) * HALF], m.ps[n % 4][:, :],
                                        m.ssm_gain[:, k:k + 1], None, ALU.mult).then_inc(read[1], 1)

        @block.tensor
        def _(pe):
            for n in range(NG):
                k, h = n % KD, n // KD
                pe.wait_ge(normed, 4 * (h + 1))
                if n >= 4:
                    pe.wait_ge(read[n % 2], (n - 4) // 2 + 1)
                for j in range(4):
                    mm = nc.tensor.transpose(m.ps[n % 4][:, j * P:(j + 1) * P], m.y[:, 4 * h + j, k:D:KD],
                                             m.ident[:, :])
                mm.then_inc(turned, 1)


def nsa_project(nc, m):
    W = m.nsa_w
    hc = m.sb("nsa_hc", [P, 2, KD, P])
    NH = HEADS + 2 * GROUPS
    nb = m.sb("nsa_norm_in", [P, 2, NH, HD])
    cv = m.sb("nsa_cmp_in", [P, 2, 2 * KV_W])
    sq = m.sb("nsa_sq", [P, NH, HD])
    ss, rs = m.sb("nsa_ss", [P, NH]), m.sb("nsa_rs", [P, NH])
    q = {n: m.sem(f"nsa_{n}") for n in ("hc_ready", "proj_done", "copied", "squared", "mean", "rooted",
                                        "normed", "turned", "spread", "ones", "gates")}
    ch = m.chains(nc, "nsa")
    LOOPS = NT // 2
    KS0, KW0 = HEADS * HD, HEADS * HD + KV_W
    nbf = nb[:, :, :, :].rearrange("p b h d -> p b (h d)")
    with nc.Block() as block:
        @block.sync
        def _(sp):
            load_compress(m, sp)

        @block.gpsimd
        def _(pool):
            nc.gpsimd.memset(m.v_sel[:, :, :, HD:HD + 1], 1.0).then_inc(q["ones"], 1)
            nc.gpsimd.memset(m.v_win[:, :, :, HD:HD + 1], 1.0).then_inc(q["ones"], 1)
            for b in range(2):
                nc.gpsimd.tensor_copy(hc[:, b, :, :], m.hT[:, :, b * P:(b + 1) * P]).then_inc(q["hc_ready"], 1)
            with pool.Fori(0, LOOPS - 1) as i:
                for b in range(2):
                    pool.wait_ge(q["proj_done"], 3 * (2 * i + b) + 3)
                    nc.gpsimd.tensor_copy(hc[:, b, :, :], m.hT[:, :, bass.ds((2 * i + b + 2) * P, P)])\
                        .then_inc(q["hc_ready"], 1)

        @block.tensor
        def _(pe):
            def project(t, b):
                pe.wait_ge(q["hc_ready"], t + 1)
                pe.wait_ge(q["copied"], 6 * t)
                for n in range(3):
                    c0, c1 = n * HALF, min((n + 1) * HALF, NSA_W)
                    for k in range(KD):
                        mm = nc.tensor.matmul(m.ps[n][:, 0:c1 - c0], hc[:, b, k, :], W[:, k, c0:c1],
                                              start=(k == 0), stop=(k == KD - 1))
                    mm.then_inc(q["proj_done"], 1)

            def turn(t, b):
                pe.wait_ge(q["spread"], 4 * t)
                pe.wait_ge(q["normed"], t + 1)
                for n in range(E + 2):
                    nc.tensor.transpose(m.ps[3 + n // 4][:, n % 4 * P:(n % 4 + 1) * P],
                                        nbf[:, b, n * P:(n + 1) * P], m.ident[:, :])
                for n in range(2):
                    mm = nc.tensor.transpose(m.ps[4][:, (2 + n) * P:(3 + n) * P], cv[:, b, n * P:(n + 1) * P],
                                             m.ident[:, :])
                mm.then_inc(q["turned"], 1)

            pe.sem_inc(q["turned"], 1)
            pe.wait_ge(m.nsa_w_loaded, 16)
            project(0, 0)
            with pe.Fori(0, LOOPS - 1) as i:
                project(2 * i + 1, 1)
                turn(2 * i, 0)
                project(2 * i + 2, 0)
                turn(2 * i + 1, 1)
            project(NT - 1, 1)
            turn(NT - 2, 0)
            turn(NT - 1, 1)

        @block.scalar
        def _(act):
            act.wait_ge(q["ones"], 2)
            c = Chain(act, ch["act"])
            with act.Fori(0, LOOPS) as i:
                c.enter(i, 2)
                for b in range(2):
                    t = 2 * i + b
                    act.wait_ge(q["turned"], t)
                    act.wait_ge(q["proj_done"], 3 * t + 1)
                    nc.scalar.copy(nb[:, b, 0:HEADS, :].rearrange("p (e g) d -> p g e d", g=GROUPS),
                                   m.ps[0][:, :].rearrange("p (g e d) -> p g e d", g=GROUPS, e=E))\
                        .then_inc(q["copied"], 1)
                    act.wait_ge(q["proj_done"], 3 * t + 2)
                    nc.scalar.copy(cv[:, b, :], m.ps[1][:, 0:2 * KV_W]).then_inc(q["copied"], 1)
                    nc.scalar.copy(nbf[:, b, KS0:KS0 + KV_W], m.ps[1][:, 2 * KV_W:3 * KV_W]).then_inc(q["copied"], 1)
                    nc.scalar.copy(m.v_sel[:, bass.ds(t, 1), :, 0:HD].rearrange("p a g d -> p (a g) d"),
                                   m.ps[1][:, 3 * KV_W:4 * KV_W].rearrange("p (g d) -> p g d", d=HD))\
                        .then_inc(q["copied"], 1)
                    act.wait_ge(q["proj_done"], 3 * t + 3)
                    nc.scalar.copy(nbf[:, b, KW0:KW0 + KV_W], m.ps[2][:, 0:KV_W]).then_inc(q["copied"], 1)
                    nc.scalar.copy(m.v_win[:, bass.ds(t, 1), :, 0:HD].rearrange("p a g d -> p (a g) d"),
                                   m.ps[2][:, KV_W:2 * KV_W].rearrange("p (g d) -> p g d", d=HD))
                    c.link(nc.scalar.copy(m.gate_scale[:, bass.ds(t, 1), :].rearrange("p a g -> p (a g)"),
                                          m.ps[2][:, 2 * KV_W:2 * KV_W + GATE_W]))
                    nc.scalar.copy(m.junk[:, 0, 0:1], m.ones[:, 0:1]).then_inc(q["copied"], 1)
                    act.wait_ge(q["copied"], 6 * t + 6)
                    nc.scalar.activation(sq[:, :, :], nb[:, b, :, :], ACT.Square).then_inc(q["squared"], 1)
                    act.wait_ge(q["mean"], t + 1)
                    nc.scalar.activation(ss[:, :], ss[:, :], ACT.Sqrt).then_inc(q["rooted"], 1)
                c.leave(LOOPS, 2)
            g = m.gate_scale[:, :, :].rearrange("p t n -> p (t n)")
            nc.scalar.activation(g, g, ACT.Sigmoid).then_inc(q["gates"], 1)

        @block.vector
        def _(dve):
            c = Chain(dve, ch["dve"])
            PER = 2 * 2
            with dve.Fori(0, LOOPS) as i:
                c.enter(i, PER)
                for b in range(2):
                    t = 2 * i + b
                    cols = bass.ds(t * P, P)
                    dve.wait_ge(q["squared"], t + 1)
                    c.link(nc.vector.tensor_reduce(ss[:, :], sq[:, :, :], axis=AX.X, op=ALU.add))
                    nc.vector.tensor_scalar(ss[:, :], ss[:, :], 1.0 / HD, EPS, ALU.mult, ALU.add)\
                        .then_inc(q["mean"], 1)
                    dve.wait_ge(q["rooted"], t + 1)
                    c.link(nc.vector.reciprocal(rs[:, :], ss[:, :]))
                    nc.vector.tensor_tensor(nb[:, b, :, :], nb[:, b, :, :],
                                            rs[:, :].unsqueeze(2).to_broadcast([P, NH, HD]), ALU.mult)\
                        .then_inc(q["normed"], 1)
                    dve.wait_ge(q["turned"], t + 2)
                    nc.vector.tensor_scalar(m.qT[:, :, cols], m.ps[3][:, :].rearrange("p (e q) -> p e q", e=E),
                                            m.qk_gain[:, 0:1], None, ALU.mult).then_inc(q["spread"], 1)
                    nc.vector.tensor_scalar(m.ksT[:, cols], m.ps[4][:, 0:P], m.qk_gain[:, 2:3], None,
                                            ALU.mult).then_inc(q["spread"], 1)
                    nc.vector.tensor_scalar(m.kwT[:, cols], m.ps[4][:, P:2 * P], m.qk_gain[:, 3:4], None,
                                            ALU.mult).then_inc(q["spread"], 1)
                    nc.vector.tensor_copy(m.cT[:, :, cols], m.ps[4][:, 2 * P:].rearrange("p (a q) -> p a q", a=2))\
                        .then_inc(q["spread"], 1)
                c.leave(LOOPS, PER)
            dve.wait_ge(q["gates"], 1)
            first = m.gate_scale[:, 0, 0:GATE_W:3]
            c.link(nc.vector.tensor_scalar(first, first, m.any_cmp[:, 0:1], None, ALU.mult))


def load_compress(m, eng):
    W1, W2, pos = m.cmp_w
    for n, kv in enumerate("kv"):
        eng.dma_start(pos[:, n, :], m.i[f"cmp_pos_{kv}"][0].rearrange("(j a) d -> j (a d)", a=2))\
            .then_inc(m.cmp_loaded, 16)
        for part in range(2):
            js = slice(part * CMP_BLOCK // 4, (part + 1) * CMP_BLOCK // 4)
            eng.dma_start(W1[:, n, js, :], m.i[f"cmp_w1_{kv}"][0].rearrange("(j p) h -> p j h", p=P)[:, js, :])\
                .then_inc(m.cmp_loaded, 16)
        eng.dma_start(W2[:, n, :], m.i[f"cmp_w2_{kv}"][0]).then_inc(m.cmp_loaded, 16)


def compress(nc, m):
    JP = CMP_BLOCK // 2
    W1, W2, pos = m.cmp_w
    pairs = m.sb("cmp_pairs", [P, 2, GROUPS, S])
    posT = m.sb("cmp_posT", [P, 2, JP])
    bias = m.sb("cmp_bias", [P, 2])
    hid = m.sb("cmp_hid", [P, 2, GROUPS, NCMP])
    kc = m.sb("cmp_k", [NCMP, GROUPS, HD])
    sq = m.sb("cmp_sq", [NCMP, GROUPS, HD])
    ss, rs = m.sb("cmp_ss", [NCMP, GROUPS]), m.sb("cmp_rs", [NCMP, GROUPS])
    q = {n: m.sem(f"cmp_{n}") for n in ("paired", "pos_turned", "pos_ready", "bias_done", "bias_ready", "hid_done",
                                        "hid_ready", "kv_done", "squared", "mean", "rooted", "normed", "k_turned",
                                        "ones")}
    ch = m.chains(nc, "cmp")
    with nc.Block() as block:
        @block.sync
        def _(sp):
            for n in range(2):
                for g in range(GROUPS):
                    own = slice(g * HD, (g + 1) * HD)
                    sp.dma_start(pairs[0:HD, n, g, :], m.cT[own, n, :]).then_inc(q["paired"], 16)
                    sp.dma_start(pairs[HD:P, n, g, 0:S - 1], m.cT[own, n, 1:S]).then_inc(q["paired"], 16)

        @block.tensor
        def _(pe):
            pe.wait_ge(m.cmp_loaded, 16 * 2 * 4)
            for n in range(2):
                mm = nc.tensor.transpose(m.ps[0][:, n * JP:(n + 1) * JP], pos[:, n, :], m.ident[0:JP, 0:JP])
            mm.then_inc(q["pos_turned"], 1)
            pe.wait_ge(q["pos_ready"], 1)
            for n in range(2):
                for j in range(JP):
                    mm = nc.tensor.matmul(m.ps[1][:, n:n + 1], W1[:, n, j, :], posT[:, n, j:j + 1],
                                          start=(j == 0), stop=(j == JP - 1))
            mm.then_inc(q["bias_done"], 1)
            pe.wait_ge(q["paired"], 16 * 4 * GROUPS)
            for n in range(2):
                dst = m.ps[2 + n][:, 0:GROUPS * NCMP].rearrange("h (g c) -> h g c", g=GROUPS)
                for j in range(JP):
                    last = CMP_STRIDE * (NCMP - 1) + 2 * j + 1
                    mm = nc.tensor.matmul(dst, W1[:, n, j, :], pairs[:, n, :, 2 * j:last:CMP_STRIDE],
                                          start=(j == 0), stop=(j == JP - 1))
                mm.then_inc(q["hid_done"], 1)
            pe.wait_ge(q["hid_ready"], 2)
            for n in range(2):
                for g in range(GROUPS):
                    mm = nc.tensor.matmul(m.ps[4][0:NCMP, (2 * n + g) * HD:(2 * n + g + 1) * HD], hid[:, n, g, :],
                                          W2[:, n, :], start=True, stop=True)
            mm.then_inc(q["kv_done"], 1)
            pe.wait_ge(q["normed"], 1)
            nc.tensor.transpose(m.ps[5][:, 0:NCMP], kc[:, :, :].rearrange("c g d -> c (g d)"),
                                m.ident[0:NCMP, 0:NCMP]).then_inc(q["k_turned"], 1)

        @block.scalar
        def _(act):
            act.wait_ge(q["bias_ready"], 1)
            for n in range(2):
                act.wait_ge(q["hid_done"], n + 1)
                nc.scalar.activation(hid[:, n, :, :], m.ps[2 + n][:, 0:GROUPS * NCMP]
                                     .rearrange("h (g c) -> h g c", g=GROUPS), ACT.Silu,
                                     bias=bias[:, n:n + 1]).then_inc(q["hid_ready"], 1)
            act.wait_ge(q["kv_done"], 1)
            nc.scalar.activation(sq[:, :, :], m.ps[4][0:NCMP, 0:2 * HD].rearrange("c (g d) -> c g d", d=HD),
                                 ACT.Square).then_inc(q["squared"], 1)
            act.wait_ge(q["mean"], 1)
            nc.scalar.activation(ss[:, :], ss[:, :], ACT.Sqrt).then_inc(q["rooted"], 1)

        @block.gpsimd
        def _(pool):
            nc.gpsimd.memset(m.v_cmp[:, :, HD:HD + 1], 1.0).then_inc(q["ones"], 1)

        @block.vector
        def _(dve):
            c = Chain(dve, ch["dve"])
            dve.wait_ge(q["pos_turned"], 1)
            nc.vector.tensor_copy(posT[:, :, :], m.ps[0][:, 0:2 * JP].rearrange("p (n j) -> p n j", n=2))\
                .then_inc(q["pos_ready"], 1)
            dve.wait_ge(q["bias_done"], 1)
            nc.vector.tensor_copy(bias[:, :], m.ps[1][:, 0:2]).then_inc(q["bias_ready"], 1)
            dve.wait_ge(q["squared"], 1)
            c.link(nc.vector.tensor_reduce(ss[:, :], sq[:, :, :], axis=AX.X, op=ALU.add))
            nc.vector.tensor_scalar(ss[:, :], ss[:, :], 1.0 / HD, EPS, ALU.mult, ALU.add).then_inc(q["mean"], 1)
            dve.wait_ge(q["ones"], 1)
            kv = m.ps[4][0:NCMP, 0:4 * HD].rearrange("c (n g d) -> c n g d", n=2, g=GROUPS)
            c.link(nc.vector.tensor_copy(m.v_cmp[:, :, 0:HD], kv[:, 1, :, :]))
            dve.wait_ge(q["rooted"], 1)
            c.link(nc.vector.reciprocal(rs[:, :], ss[:, :]))
            nc.vector.tensor_tensor(kc[:, :, :], kv[:, 0, :, :], rs[:, :].unsqueeze(2).to_broadcast([NCMP, GROUPS, HD]),
                                    ALU.mult).then_inc(q["normed"], 1)
            dve.wait_ge(q["k_turned"], 1)
            c.link(nc.vector.tensor_scalar(m.kcT[:, :], m.ps[5][:, 0:NCMP], m.qk_gain[:, 1:2], None, ALU.mult))


def attention(nc, m):
    qz = m.sb("att_q", [P, GROUPS, S])
    prob = m.sb("att_prob", [P, 2, S])
    probT = m.sb("att_probT", [P, 2, S])
    nmax = m.sb("att_nmax", [P, 2, 2])
    rec = m.sb("att_rec", [P, 2, 3])
    acc = m.sb("att_acc", [P, 2, 2, HD])
    names = ("row_zeroed", "rows_cleared", "zeroed", "q_ready", "scored", "maxed", "exped", "turned", "act_copied",
             "dve_copied", "summed", "mixed")
    q = {n: m.sem(f"att_{n}") for n in names}
    copied = [q["act_copied"], q["dve_copied"]]
    ch = m.chains(nc, "att")
    WT = WINDOW // P
    CMP0 = (WT + 1) * P
    TURN = HALF // P
    units = [(i, g, kind) for i in range(NT) for g in range(GROUPS) for kind in ("sel", "win")]
    U = len(units)

    def pair(u):
        return m.psum[:, 2 * HALF * (u % 2):2 * HALF * (u % 2 + 1)]

    def tiles(u):
        i, _, kind = units[u]
        return range(0 if kind == "sel" else max(0, i - WT), i + 1)

    def pieces(u):
        at = [x * P for x in range(len(tiles(u)))] + ([CMP0] if units[u][2] == "win" else [])
        return [at[x:x + TURN] for x in range(0, len(at), TURN)]

    start = [0]
    for u in range(U):
        start.append(start[-1] + len(pieces(u)))
    TURNS = start[-1]
    assert TURNS % 2 == 0

    def wait_turns(eng, e, n):
        eng.wait_ge(copied[0], TURNS // 2 * e + (n + 1) // 2)
        eng.wait_ge(copied[1], TURNS // 2 * e + n // 2)

    def copies(eng, which, e, u):
        for x, at in enumerate(pieces(u)):
            n = start[u] + x
            if n % 2 == which:
                if u >= 2 and x < 2:
                    eng.wait_ge(q["summed"], U * e + u - 1)
                elif x < 2:
                    eng.wait_ge(q["summed"], U * e)
                eng.wait_ge(q["turned"], TURNS * e + n + 1)
                dst = probT[:, u % 2, x * HALF:x * HALF + len(at) * P]
                src = m.ps[4 + n % 2][:, 0:len(at) * P]
                ins = nc.scalar.copy(dst, src) if which == 0 else nc.vector.tensor_copy(dst, src)
                ins.then_inc(copied[which], 1)

    with nc.Block() as block:
        @block.gpsimd
        def _(pool):
            nc.gpsimd.memset(m.junk[:, 0, :], 0.0).then_inc(q["row_zeroed"], 1)
            pool.wait_ge(q["row_zeroed"], 1)
            for g in range(GROUPS):
                other = slice((1 - g) * HD, (2 - g) * HD)
                nc.gpsimd.memset(qz[other, g, :], 0.0).then_inc(q["zeroed"], 1)
            pool.wait_ge(q["zeroed"], 2)
            nc.gpsimd.memset(prob[:, :, CMP0:CMP0 + P], 0.0).then_inc(q["zeroed"], 1)
            pool.wait_ge(q["zeroed"], 3)
            def q_tile(e, i, g):
                own = slice(g * HD, (g + 1) * HD)
                cols = slice(i * P, (i + 1) * P)
                nc.gpsimd.tensor_copy(qz[own, g, cols], m.qT[own, bass.ds(e, 1), cols].rearrange("p a q -> p (a q)"))\
                    .then_inc(q["q_ready"], 1)

            for i in range(NT):
                for g in range(GROUPS):
                    q_tile(0, i, g)
            with pool.Fori(0, E - 1) as e:
                for i in range(NT):
                    for g in range(GROUPS):
                        pool.wait_ge(q["scored"], U * e + 2 * (GROUPS * i + g) + 2)
                        q_tile(e + 1, i, g)

        @block.sync
        def _(sp):
            sp.wait_ge(q["row_zeroed"], 1)
            for b in range(EXPERTS, BLOCKS):
                sp.dma_start(m.y_slots[b * P:(b + 1) * P, :], m.junk[:, 0, :]).then_inc(q["rows_cleared"], 16)
            sp.wait_ge(q["rows_cleared"], 16 * EXTRA)
            for r in range(len(m.merge_w_loaded)):
                load_merge(m, sp, r, 0)

        @block.tensor
        def _(pe):
            pe.wait_ge(q["zeroed"], 3)

            def scores(e, u):
                i, g, kind = units[u]
                ps = pair(u)
                pe.wait_ge(q["exped"], U * e + max(u - 1, 0))
                if kind == "sel":
                    pe.wait_ge(q["q_ready"], GROUPS * (NT * e + i) + g + 1)
                keys = m.ksT if kind == "sel" else m.kwT
                qs = qz[:, g, i * P:(i + 1) * P]
                k0, n = tiles(u)[0] * P, len(tiles(u)) * P
                for c0 in range(0, n, HALF):
                    c1 = min(c0 + HALF, n)
                    masks = []
                    if c1 == n:
                        masks.append((n - P, m.mask_future))
                    if kind == "win" and i >= WT and c0 == 0:
                        masks.append((0, m.mask_far))
                    mm = nc.tensor.matmul(ps[:, c0:c1], qs, keys[:, k0 + c0:k0 + c1], start=True, stop=not masks)
                    for x, (at, mask) in enumerate(masks):
                        mm = nc.tensor.matmul(ps[:, at:at + P], m.identb[:, :], mask[:, :], start=False,
                                              stop=(x == len(masks) - 1))
                if kind == "win":
                    nc.tensor.matmul(ps[:, CMP0:CMP0 + NCMP], qs, m.kcT[:, :], start=True, stop=False)
                    mm = nc.tensor.matmul(ps[:, CMP0:CMP0 + NCMP], m.identb[:, :], m.mask_cmp[:, i, 0:NCMP],
                                          start=False, stop=True)
                mm.then_inc(q["scored"], 1)

            def turn(e, u):
                pe.wait_ge(q["exped"], U * e + u + 1)
                for x, at in enumerate(pieces(u)):
                    n = start[u] + x
                    pe.wait_ge(copied[n % 2], TURNS // 2 * e + n // 2)
                    for y, c in enumerate(at):
                        mm = nc.tensor.transpose(m.ps[4 + n % 2][:, y * P:(y + 1) * P], prob[:, u % 2, c:c + P],
                                                 m.ident[:, :])
                    mm.then_inc(q["turned"], 1)

            def sums(e, u):
                i, g, kind = units[u]
                dst, pt = m.ps[6 + (u // 2) % 2], probT[:, u % 2, :]
                if kind == "sel":
                    pe.wait_ge(q["mixed"], U // 2 * e + max(u // 2 - 1, 0))
                wait_turns(pe, e, start[u + 1])
                v, at = (m.v_sel, HD + 1) if kind == "sel" else (m.v_win, 2 * (HD + 1))
                ts = tiles(u)
                for x, t in enumerate(ts):
                    mm = nc.tensor.matmul(dst[:, at:at + HD + 1], pt[:, x * P:(x + 1) * P], v[:, t, g, :],
                                          start=(x == 0), stop=(x == len(ts) - 1))
                if kind == "win":
                    mm = nc.tensor.matmul(dst[:, 0:HD + 1], pt[0:NCMP, len(ts) * P:(len(ts) + 1) * P],
                                          m.v_cmp[:, g, :], start=True, stop=True)
                mm.then_inc(q["summed"], 1)

            with pe.Fori(0, E) as e:
                for u in range(U + 2):
                    if u < U:
                        scores(e, u)
                    if u >= 2:
                        sums(e, u - 2)
                    if 1 <= u <= U:
                        turn(e, u - 1)

        @block.scalar
        def _(act):
            with act.Fori(0, E) as e:
                for u in range(U + 1):
                    if u < U:
                        ps, pr, nm = pair(u), prob[:, u % 2, :], nmax[:, u % 2, :]
                        n = len(tiles(u)) * P
                        act.wait_ge(q["maxed"], U * e + u + 1)
                        act.wait_ge(q["turned"], TURNS * e + start[max(u - 1, 0)])
                        ins = nc.scalar.activation(pr[:, 0:n], ps[:, 0:n], ACT.Exp, bias=nm[:, 0:1])
                        if units[u][2] == "win":
                            ins = nc.scalar.activation(pr[:, CMP0:CMP0 + NCMP], ps[:, CMP0:CMP0 + NCMP], ACT.Exp,
                                                       bias=nm[:, 1:2])
                        ins.then_inc(q["exped"], 1)
                    if u >= 1:
                        copies(act, 0, e, u - 1)

        @block.vector
        def _(dve):
            c = Chain(dve, ch["dve"])
            PER = (U // 2) * 4

            def maxima(e, u):
                ps, nm = pair(u), nmax[:, u % 2, :]
                n = len(tiles(u)) * P
                dve.wait_ge(q["scored"], U * e + u + 1)
                ins = nc.vector.tensor_reduce(nm[:, 0:1], ps[:, 0:n], axis=AX.X, op=ALU.max, negate=True)
                if units[u][2] == "win":
                    ins = nc.vector.tensor_reduce(nm[:, 1:2], ps[:, CMP0:CMP0 + NCMP], axis=AX.X, op=ALU.max,
                                                  negate=True)
                ins.then_inc(q["maxed"], 1)

            def mix(e, w):
                i, g, _ = units[2 * w]
                o = m.ps[6 + w % 2][:, 0:3 * (HD + 1)].rearrange("p (b d) -> p b d", b=3)
                r, a = rec[:, w % 2, :], acc[:, w % 2, :, :]
                head = g * E + e
                dve.wait_ge(q["summed"], U * e + 2 * w + 2)
                done = c.put(nc.vector.reciprocal(r, o[:, :, HD:HD + 1].rearrange("p b a -> p (b a)")))
                yield
                c.need(done)
                done = c.put(nc.vector.tensor_tensor(r, r, m.gate_scale[:, i, bass.ds(3 * head, 3)], ALU.mult))
                yield
                c.need(done)
                done = c.put(nc.vector.tensor_scalar(a[:, 0, :], o[:, 0, 0:HD], r[:, 0:1], None, ALU.mult))
                yield
                c.need(done)
                done = c.put(nc.vector.scalar_tensor_tensor(out=a[:, 1, :], in0=o[:, 1, 0:HD], scalar=r[:, 1:2],
                                                            in1=a[:, 0, :], op0=ALU.mult, op1=ALU.add))
                yield
                c.need(done)
                nc.vector.scalar_tensor_tensor(out=m.ya[:, i, bass.ds(head, 1), :].rearrange("p a d -> p (a d)"),
                                               in0=o[:, 2, 0:HD], scalar=r[:, 2:3], in1=a[:, 1, :],
                                               op0=ALU.mult, op1=ALU.add).then_inc(q["mixed"], 1)

            with dve.Fori(0, E) as e:
                c.enter(e, PER)
                for u in range(U + 2):
                    if u >= 4 and u % 2 == 0:
                        steps = mix(e, u // 2 - 2)
                    elif u < 4:
                        steps = iter(())
                    if u < U:
                        maxima(e, u)
                    next(steps, None)
                    if 1 <= u <= U:
                        copies(dve, 1, e, u - 1)
                    next(steps, None)
                    if u % 2 == 1:
                        next(steps, None)
                for _ in mix(e, U // 2 - 1):
                    pass
                c.leave(E, PER)


def turn_ya(nc, m):
    KA = Q_W // P
    turned = m.sem("ya_turned")
    read = [m.sem("ya_act_read"), m.sem("ya_dve_read")]
    src = m.ya[:, :, :, :].rearrange("p t h d -> p t (h d)")
    with nc.Block() as block:
        @block.tensor
        def _(pe):
            for n in range(2 * KA):
                k, h = n % KA, n // KA
                if n >= 4:
                    pe.wait_ge(read[n % 2], (n - 4) // 2 + 1)
                for j in range(4):
                    mm = nc.tensor.transpose(m.ps[n % 4][:, j * P:(j + 1) * P], src[:, 4 * h + j, k:Q_W:KA],
                                             m.ident[:, :])
                mm.then_inc(turned, 1)

        @block.scalar
        def _(act):
            for n in range(0, 2 * KA, 2):
                k, h = n % KA, n // KA
                act.wait_ge(turned, n + 1)
                nc.scalar.copy(m.yaT[:, k, h * HALF:(h + 1) * HALF], m.ps[n % 4][:, :]).then_inc(read[0], 1)

        @block.vector
        def _(dve):
            for n in range(1, 2 * KA, 2):
                k, h = n % KA, n // KA
                dve.wait_ge(turned, n + 1)
                nc.vector.tensor_copy(m.yaT[:, k, h * HALF:(h + 1) * HALF], m.ps[n % 4][:, :]).then_inc(read[1], 1)


def merge_parts(m):
    return ((KD, BR0, "w_in", m.hT), (Q_W // P, 0, "w_branch_a", m.yaT),
            (KD, BR0 + D, "w_in", m.hT), (KD, 0, "w_branch_b", m.ybT))


def load_merge(m, eng, r, it):
    at = 0
    for kk, c0, name, _ in merge_parts(m):
        src = m.i[name][0][:, c0:c0 + D].rearrange("(p k) (m c) -> m p k c", k=kk, c=P)
        eng.dma_start(m.merge_w[:, r, at:at + kk, :], src[len(m.merge_w_loaded) * it + r, :, :, :])\
            .then_inc(m.merge_w_loaded[r], 16)
        at += kk


def merge(nc, m):
    parts = [x[0:1] + x[3:] for x in merge_parts(m)]
    W, here = m.merge_w, m.merge_w_loaded
    RING = len(here)
    sg = m.sb("merge_sg", [P, 2, 2, HALF])
    half = m.sb("merge_half", [P, 2, HALF])
    q = {n: m.sem(f"merge_{n}") for n in ("done", "sig_ready", "read")}
    ch = m.chains(nc, "merge")
    with nc.Block() as block:
        @block.sync
        def _(sp):
            with sp.Fori(0, KD // RING - 1) as it:
                for r in range(RING):
                    sp.wait_ge(q["read"], 2 * RING * it + 2 * r + 2)
                    load_merge(m, sp, r, it + 1)
            for t in range(NT):
                sp.dma_start(m.x2[:, t, :], m.i["x"][0][t * P:(t + 1) * P, :]).then_inc(m.x_loaded, 16)

        @block.tensor
        def _(pe):
            with pe.Fori(0, KD // RING) as it:
                for r in range(RING):
                    pe.wait_ge(here[r], 16 * 4 * (it + 1))
                    for h in range(2):
                        pe.wait_ge(q["read"], 2 * RING * it + 2 * (r - 1) + h + 1 if r else 2 * RING * it)
                        at = 0
                        for n, (kk, src) in enumerate(parts):
                            for k in range(kk):
                                mm = nc.tensor.matmul(m.ps[4 * h + n][:, :], W[:, r, at + k, :],
                                                      src[:, k, h * HALF:(h + 1) * HALF],
                                                      start=(k == 0), stop=(k == kk - 1))
                            at += kk
                            mm.then_inc(q["done"], 1)

        @block.scalar
        def _(act):
            with act.Fori(0, KD // RING) as it:
                for r in range(RING):
                    for h in range(2):
                        n = 2 * RING * it + 2 * r + h
                        act.wait_ge(q["read"], 2 * RING * it + 2 * (r - 1) + h + 1 if r else 2 * RING * it)
                        for b in range(2):
                            act.wait_ge(q["done"], 4 * n + 2 * b + 1)
                            nc.scalar.activation(sg[:, h, b, :], m.ps[4 * h + 2 * b][:, :],
                                                 ACT.Sigmoid).then_inc(q["sig_ready"], 1)

        @block.vector
        def _(dve):
            c = Chain(dve, ch["dve"])
            PER = 2 * RING * 2
            with dve.Fori(0, KD // RING) as it:
                c.enter(it, PER)
                for r in range(RING):
                    for h in range(2):
                        n = 2 * RING * it + 2 * r + h
                        dve.wait_ge(q["read"], n)
                        for b in range(2):
                            dve.wait_ge(q["sig_ready"], 2 * n + b + 1)
                            dve.wait_ge(q["done"], 4 * n + 2 * b + 2)
                            c.link(nc.vector.tensor_tensor(half[:, b, :], sg[:, h, b, :], m.ps[4 * h + 2 * b + 1][:, :],
                                                           ALU.mult))
                        nc.vector.tensor_tensor(
                            m.mergedT[:, bass.ds(RING * it + r, 1), h * HALF:(h + 1) * HALF]
                            .rearrange("p a n -> p (a n)"), half[:, 0, :], half[:, 1, :], ALU.add).then_inc(q["read"], 1)
                c.leave(KD // RING, PER)


def project_out(nc, m):
    FIRST = 3
    W = m.sb("out_w", [P, KD, D])
    q = {n: m.sem(f"out_{n}") for n in ("done", "read", "squared", "mean_made", "rooted", "normed", "turned",
                                        "hT_ready", "logits")}
    w_here = [m.sem(f"out_w_loaded{k}") for k in range(KD)]
    stored = [m.sem(f"xn_stored{r}") for r in range(2)]
    ch = m.chains(nc, "out")
    with nc.Block() as block:
        @block.sync
        def _(sp):
            for k in range(KD):
                sp.dma_start(W[:, k, :], m.i["w_out"][0][k * P:(k + 1) * P, :]).then_inc(w_here[k], 16)
            sp.dma_start(m.route_w[:, :, 0:MGROUPS], m.i["moe_w_group"][0].rearrange("(p k) n -> p k n", k=KD))\
                .then_inc(m.route_w_loaded, 16)
            sp.dma_start(m.route_w[:, :, MGROUPS:], m.i["moe_w_expert"][0].rearrange("(p k) n -> p k n", k=KD))\
                .then_inc(m.route_w_loaded, 16)
            sp.dma_start(m.pin[:, :, :], m.i["p"][0, 0].rearrange("(t p) n -> p t n", p=P)).then_inc(m.p_loaded, 16)
            for r in range(2):
                load_expert_gate_up(m, sp, r, r, m.moe_w_loaded[0][r])
            load_expert_down(m, sp, 0, 0, m.moe_w_loaded[1][0])
            for t in range(NT):
                sp.wait_ge(q["normed"], t + 1)
                sp.dma_start(m.xn_dram[t * P:(t + 1) * P, :], m.xn[:, t % 2, :]).then_inc(stored[t % 2], 16)
            for r in range(2):
                sp.wait_ge(stored[r], 16 * NT // 2)

        @block.tensor
        def _(pe):
            def product(t, n, k, bank):
                return nc.tensor.matmul(m.ps[bank][:, :], m.mergedT[:, k, t * P:(t + 1) * P],
                                        W[:, k, n * HALF:(n + 1) * HALF], start=(k == 0), stop=(k == KD - 1))

            def turn(t):
                pe.wait_ge(q["normed"], t + 1)
                if t:
                    pe.wait_ge(q["hT_ready"], 2 * t)
                for n in range(2):
                    for k in range(4):
                        mm = nc.tensor.transpose(m.ps[6 + n][:, k * P:(k + 1) * P],
                                                 m.xn[:, t % 2, 4 * n + k:D:KD], m.ident[:, :])
                    mm.then_inc(q["turned"], 1)

            def logits(t):
                pe.wait_ge(q["hT_ready"], 2 * t + 2)
                for k in range(KD):
                    nc.tensor.matmul(m.logits[:, t * ROUTES:(t + 1) * ROUTES], m.h2T[:, t % 2, k, :],
                                     m.route_w[:, k, :], start=(k == 0), stop=(k == KD - 1))

            for k in range(KD):
                pe.wait_ge(w_here[k], 16)
                for t in range(FIRST):
                    for n in range(2):
                        mm = product(t, n, k, 2 * t + n)
                        if k == KD - 1:
                            mm.then_inc(q["done"], 1)
            turns = {3: (0,), 4: (1, 2), 5: (3, 4), 6: (5,), 7: (6, 7)}
            for t in range(FIRST, NT):
                last = {3: 1, 4: 0}.get(t, t - 2)
                for n in range(2):
                    pe.wait_ge(q["read"], 2 * last + n + 1)
                    for k in range(KD):
                        mm = product(t, n, k, 2 * (t % 2) + n)
                    mm.then_inc(q["done"], 1)
                for u in turns[t]:
                    if u == 1:
                        pe.wait_ge(m.route_w_loaded, 32)
                        pe.wait_ge(q["read"], 2 * FIRST)
                    if u:
                        logits(u - 1)
                    turn(u)
            logits(NT - 1)

        @block.scalar
        def _(act):
            for t in range(NT):
                act.wait_ge(q["read"], 2 * t + 2)
                nc.scalar.activation(m.junk[:, t % 2, :], m.x2[:, t, :], ACT.Square,
                                     accum_out=m.sumsq[:, t:t + 1]).then_inc(q["squared"], 1)
                act.wait_ge(q["mean_made"], t + 1)
                nc.scalar.activation(m.rms[:, t:t + 1], m.rms[:, t:t + 1], ACT.Sqrt).then_inc(q["rooted"], 1)

        @block.vector
        def _(dve):
            c = Chain(dve, ch["dve"])

            def add(t):
                for n in range(2):
                    bank = 2 * t + n if t < FIRST else 2 * (t % 2) + n
                    dve.wait_ge(q["done"], 2 * t + n + 1)
                    part = m.x2[:, t, n * HALF:(n + 1) * HALF]
                    nc.vector.tensor_tensor(part, part, m.ps[bank][:, :], ALU.add).then_inc(q["read"], 1)

            def norm(t):
                dve.wait_ge(q["squared"], t + 1)
                nc.vector.tensor_scalar(m.rms[:, t:t + 1], m.sumsq[:, t:t + 1], 1.0 / D, EPS, ALU.mult,
                                        ALU.add).then_inc(q["mean_made"], 1)
                dve.wait_ge(q["rooted"], t + 1)
                c.link(nc.vector.reciprocal(m.rstd[:, t:t + 1], m.rms[:, t:t + 1]))
                if t >= 2:
                    dve.wait_ge(q["turned"], 2 * (t - 1))
                    dve.wait_ge(stored[t % 2], 16 * (t // 2))
                nc.vector.tensor_scalar(m.xn[:, t % 2, :], m.x2[:, t, :], m.rstd[:, t:t + 1], None,
                                        ALU.mult).then_inc(q["normed"], 1)

            def scale(t):
                for n in range(2):
                    dve.wait_ge(q["turned"], 2 * t + n + 1)
                    nc.vector.tensor_tensor(m.h2T[:, t % 2, 4 * n:4 * n + 4, :],
                                            m.ps[6 + n][:, :].rearrange("p (k n) -> p k n", k=4),
                                            m.moe_gain[:, 4 * n:4 * n + 4].unsqueeze(2).to_broadcast([P, 4, P]),
                                            ALU.mult).then_inc(q["hT_ready"], 1)

            dve.wait_ge(m.x_loaded, 16 * NT)
            for t in range(FIRST):
                add(t)
            norm(0)
            norm(1)
            add(3)
            scale(0)
            norm(2)
            add(4)
            scale(1)
            norm(3)
            scale(2)
            norm(4)
            add(5)
            scale(3)
            norm(5)
            scale(4)
            add(6)
            norm(6)
            scale(5)
            add(7)
            scale(6)
            norm(7)
            scale(7)


def route(nc, m):
    KP = PLE // P
    lg = m.sb("route_logits", [P, NT, ROUTES])
    f = {n: m.sb(f"route_{n}", [P, NT]) for n in ("gmax", "gsum", "grp", "gw", "m1", "i1", "m2", "i2", "e2", "den")}
    eg, gm = m.sb("route_eg", [P, NT, MGROUPS]), m.sb("route_gm", [P, NT, MGROUPS])
    el, eq, ex = (m.sb(f"route_{n}", [P, NT, PER_GROUP]) for n in ("el", "eq", "ex"))
    sel = m.sb("route_sel", [P, NT, PER_GROUP, MGROUPS])
    M1, M2, M, rank, tmp = (m.sb(f"route_{n}", [P, NT, EXPERTS]) for n in ("M1", "M2", "M", "rank", "tmp"))
    iota = m.sb("route_iota", [P, EXPERTS])
    iotai = m.sb("route_iotai", [P, EXPERTS], I32)
    tok = m.sb("route_tok", [P, NT], I32)
    cnt, carry, extra, incl = (m.sb(f"route_{n}", [P, EXPERTS]) for n in ("cnt", "carry", "extra", "incl"))
    r, j, own, pos, slot, more = (m.sb(f"route_{n}", [P, NT, 2]) for n in ("r", "j", "own", "pos", "slot", "more"))
    cmpx = m.sb("route_cmpx", [P, EXTRA, EXPERTS])
    bex = m.sb("route_bex", [P, EXTRA])
    zero = m.sb("route_zero", [BLOCKS, P], I32)
    rows, rowsf = m.sb("route_rows", [BLOCKS, P], I32), m.sb("route_rowsf", [BLOCKS, P])
    q = {n: m.sem(f"route_{n}") for n in ("iota", "zeroed", "cleared", "maxed", "exped", "masks",
                                          "ranked", "slots", "scattered", "rows_loaded", "rows_ready", "rows_turned",
                                          "proj_w_loaded", "p_turned", "pT_ready", "proj_done", "proj_read")}
    ch = m.chains(nc, "route")
    with nc.Block() as block:
        @block.sync
        def _(sp):
            sp.dma_start(m.ple_wp[:, :, :], m.i["ple_w_proj"][0].rearrange("(p k) n -> p k n", k=KP))\
                .then_inc(q["proj_w_loaded"], 16)
            sp.wait_ge(q["zeroed"], 1)
            sp.dma_start(m.slot_tok.rearrange("(b p) a -> b (p a)", p=P), zero[:, :]).then_inc(q["cleared"], 16)
            sp.wait_ge(q["scattered"], 16 * 2 * NT)
            sp.dma_start(rows[:, :], m.slot_tok.rearrange("(b p) a -> b (p a)", p=P)).then_inc(q["rows_loaded"], 16)
            sp.wait_ge(q["rows_loaded"], 16)

        @block.gpsimd
        def _(pool):
            nc.gpsimd.memset(zero[:, :], 0).then_inc(q["zeroed"], 1)
            nc.gpsimd.iota(tok[:, :], pattern=[[P, NT]], base=0, channel_multiplier=1).then_inc(q["iota"], 1)
            nc.gpsimd.iota(iotai[:, :], pattern=[[1, EXPERTS]], base=0, channel_multiplier=0).then_inc(q["iota"], 1)
            pool.wait_ge(q["iota"], 2)
            pool.wait_ge(q["cleared"], 16)
            pool.wait_ge(q["slots"], 1)
            for t in range(NT):
                for s in range(2):
                    nc.gpsimd.indirect_dma_start(m.slot_tok, bass.IndirectOffsetOnAxis(ap=m.slot_u[:, t, s:s + 1], axis=0),
                                                 tok[:, t:t + 1], None).then_inc(q["scattered"], 16)
            pool.wait_ge(q["scattered"], 16 * 2 * NT)

        @block.tensor
        def _(pe):
            def turn_p():
                pe.wait_ge(m.p_loaded, 16)
                for n in range(4):
                    k, h = n % KP, n // KP
                    if n >= 2:
                        pe.wait_ge(q["pT_ready"], n - 1)
                    for j in range(4):
                        mm = nc.tensor.transpose(m.ps[6 + n % 2][:, j * P:(j + 1) * P],
                                                 m.pin[:, 4 * h + j, k:PLE:KP], m.ident[:, :])
                    mm.then_inc(q["p_turned"], 1)

            def project_p(t0, t1):
                for t in range(t0, t1):
                    for n in range(2):
                        if t:
                            pe.wait_ge(q["proj_read"], 2 * t + n - 1)
                        for k in range(KP):
                            mm = nc.tensor.matmul(m.ps[6 + n][:, :], m.pT[:, k, t * P:(t + 1) * P],
                                                  m.ple_wp[:, k, n * HALF:(n + 1) * HALF],
                                                  start=(k == 0), stop=(k == KP - 1))
                        mm.then_inc(q["proj_done"], 1)

            turn_p()
            pe.wait_ge(q["pT_ready"], 4)
            pe.wait_ge(q["proj_w_loaded"], 16)
            project_p(0, 2)
            pe.wait_ge(q["masks"], 1)
            flat = M[:, :, :].rearrange("p t e -> p (t e)")
            nc.tensor.matmul(m.ps[1][:, 0:NT * EXPERTS], m.tri_lt[:, :], flat, start=True, stop=True)
            nc.tensor.matmul(m.ps[2][:, 0:NT * EXPERTS], m.ones[:, :], flat, start=True,
                             stop=True).then_inc(q["ranked"], 1)
            project_p(2, NT)
            pe.wait_ge(q["rows_ready"], 1)
            nc.tensor.transpose(m.ps[3][:, 0:BLOCKS], rowsf[:, :], m.ident[0:BLOCKS, 0:BLOCKS])\
                .then_inc(q["rows_turned"], 1)

        @block.scalar
        def _(act):
            c = Chain(act, ch["act"])
            for n in range(4):
                k, h = n % KP, n // KP
                act.wait_ge(q["p_turned"], n + 1)
                nc.scalar.copy(m.pT[:, k, h * HALF:(h + 1) * HALF], m.ps[6 + n % 2][:, :]).then_inc(q["pT_ready"], 1)
            for t in range(NT):
                if t == 2:
                    act.wait_ge(q["maxed"], 2)
                    c.link(nc.scalar.activation(eg[:, :, :], gm[:, :, :], ACT.Exp))
                    nc.scalar.activation(f["e2"][:, :], f["e2"][:, :], ACT.Exp).then_inc(q["exped"], 1)
                for n in range(2):
                    act.wait_ge(q["proj_done"], 2 * t + n + 1)
                    nc.scalar.copy(m.proj[:, t, n * HALF:(n + 1) * HALF], m.ps[6 + n][:, :])\
                        .then_inc(q["proj_read"], 1)

        @block.vector
        def _(dve):
            c = Chain(dve, ch["dve"])
            v = nc.vector

            def wide(ap, n):
                return ap.unsqueeze(2).to_broadcast([P, NT, n])

            def row(ap, n):
                return ap.unsqueeze(1).to_broadcast([P, NT, n])

            def first(out, hit, n):
                c.link(v.scalar_tensor_tensor(out=hit, in0=hit, scalar=-64.0, in1=row(iota[:, 0:n], n),
                                              op0=ALU.mult, op1=ALU.add))
                c.link(v.tensor_reduce(out, hit, axis=AX.X, op=ALU.min))
                c.link(v.tensor_scalar(out, out, 64.0, None, ALU.add))

            dve.wait_ge(q["iota"], 2)
            c.link(v.tensor_copy(iota[:, :], iotai[:, :]))
            c.link(v.tensor_tensor(lg[:, :, :], m.logits[:, 0:NT * ROUTES].rearrange("p (t n) -> p t n", t=NT),
                                   row(m.route_bias[:, :], ROUTES), ALU.add))
            g = lg[:, :, 0:MGROUPS]
            c.link(v.tensor_reduce(f["gmax"][:, :], g, axis=AX.X, op=ALU.max))
            v.tensor_tensor(gm[:, :, :], g, wide(f["gmax"][:, :], MGROUPS), ALU.subtract).then_inc(q["maxed"], 1)
            hit = sel[:, :, 0, :]
            c.link(v.tensor_tensor(hit, g, wide(f["gmax"][:, :], MGROUPS), ALU.is_equal))
            first(f["grp"][:, :], hit, MGROUPS)
            c.link(v.tensor_tensor(eq[:, :, 0:MGROUPS], row(iota[:, 0:MGROUPS], MGROUPS),
                                   wide(f["grp"][:, :], MGROUPS), ALU.is_equal))
            c.link(v.tensor_tensor(sel[:, :, :, :],
                                   lg[:, :, MGROUPS:].rearrange("p t (g e) -> p t e g", g=MGROUPS),
                                   eq[:, :, 0:MGROUPS].unsqueeze(2).to_broadcast([P, NT, PER_GROUP, MGROUPS]), ALU.mult))
            c.link(v.tensor_reduce(el[:, :, :], sel[:, :, :, :], axis=AX.X, op=ALU.add))
            c.link(v.tensor_reduce(f["m1"][:, :], el[:, :, :], axis=AX.X, op=ALU.max))
            c.link(v.tensor_tensor(eq[:, :, :], el[:, :, :], wide(f["m1"][:, :], PER_GROUP), ALU.is_equal))
            first(f["i1"][:, :], eq[:, :, :], PER_GROUP)
            c.link(v.tensor_tensor(eq[:, :, :], row(iota[:, 0:PER_GROUP], PER_GROUP), wide(f["i1"][:, :], PER_GROUP),
                                   ALU.is_equal))
            c.link(v.scalar_tensor_tensor(out=ex[:, :, :], in0=eq[:, :, :], scalar=MASK, in1=el[:, :, :],
                                          op0=ALU.mult, op1=ALU.add))
            c.link(v.tensor_reduce(f["m2"][:, :], ex[:, :, :], axis=AX.X, op=ALU.max))
            c.link(v.tensor_tensor(eq[:, :, :], ex[:, :, :], wide(f["m2"][:, :], PER_GROUP), ALU.is_equal))
            first(f["i2"][:, :], eq[:, :, :], PER_GROUP)
            v.tensor_tensor(f["e2"][:, :], f["m2"][:, :], f["m1"][:, :], ALU.subtract).then_inc(q["maxed"], 1)
            for i in ("i1", "i2"):
                c.link(v.scalar_tensor_tensor(out=f[i][:, :], in0=f["grp"][:, :], scalar=float(PER_GROUP), in1=f[i][:, :],
                                              op0=ALU.mult, op1=ALU.add))
            for mask, i in ((M1, "i1"), (M2, "i2")):
                c.link(v.tensor_tensor(mask[:, :, :], row(iota[:, :], EXPERTS), wide(f[i][:, :], EXPERTS), ALU.is_equal))
            v.tensor_tensor(M[:, :, :], M1[:, :, :], M2[:, :, :], ALU.add).then_inc(q["masks"], 1)
            dve.wait_ge(q["exped"], 1)
            c.link(v.tensor_reduce(f["gsum"][:, :], eg[:, :, :], axis=AX.X, op=ALU.add))
            c.link(v.scalar_tensor_tensor(out=f["den"][:, :], in0=f["e2"][:, :], scalar=1.0, in1=f["gsum"][:, :],
                                          op0=ALU.add, op1=ALU.mult))
            c.link(v.reciprocal(m.weight[:, :, 0], f["den"][:, :]))
            c.link(v.tensor_tensor(m.weight[:, :, 1], m.weight[:, :, 0], f["e2"][:, :], ALU.mult))
            dve.wait_ge(q["ranked"], 1)
            c.link(v.tensor_copy(rank[:, :, :], m.ps[1][:, 0:NT * EXPERTS].rearrange("p (t e) -> p t e", t=NT)))
            c.link(v.tensor_copy(cnt[:, :], m.ps[2][:, 0:EXPERTS]))
            for t in range(1, NT):
                c.link(v.tensor_tensor(rank[:, t, :], rank[:, t, :], cnt[:, :], ALU.add))
                c.link(v.tensor_tensor(cnt[:, :], cnt[:, :], m.ps[2][:, t * EXPERTS:(t + 1) * EXPERTS], ALU.add))
            c.link(v.tensor_scalar(extra[:, :], cnt[:, :], float(P), None, ALU.is_gt))
            for n in range(2, NT):
                c.link(v.scalar_tensor_tensor(out=extra[:, :], in0=cnt[:, :], scalar=float(n * P), in1=extra[:, :],
                                              op0=ALU.is_gt, op1=ALU.add))
            c.link(v.tensor_tensor_scan(incl[:, :], m.ones[:, 0:EXPERTS], extra[:, :], 0.0, ALU.mult, ALU.add))
            c.link(v.tensor_tensor(carry[:, :], incl[:, :], extra[:, :], ALU.subtract))
            for s, mask in ((0, M1), (1, M2)):
                c.link(v.tensor_tensor(tmp[:, :, :], mask[:, :, :], rank[:, :, :], ALU.mult))
                c.link(v.tensor_reduce(r[:, :, s], tmp[:, :, :], axis=AX.X, op=ALU.add))
                c.link(v.tensor_tensor(tmp[:, :, :], mask[:, :, :], row(carry[:, :], EXPERTS), ALU.mult))
                c.link(v.tensor_reduce(own[:, :, s], tmp[:, :, :], axis=AX.X, op=ALU.add))
                c.link(v.tensor_copy(pos[:, :, s], f["i1" if s == 0 else "i2"][:, :]))
            c.link(v.tensor_scalar(j[:, :, :], r[:, :, :], float(P), None, ALU.is_ge))
            c.link(v.tensor_copy(more[:, :, :], j[:, :, :]))
            for n in range(2, NT):
                c.link(v.scalar_tensor_tensor(out=j[:, :, :], in0=r[:, :, :], scalar=float(n * P), in1=j[:, :, :],
                                              op0=ALU.is_ge, op1=ALU.add))
            c.link(v.tensor_tensor(own[:, :, :], own[:, :, :], j[:, :, :], ALU.add))
            c.link(v.tensor_scalar(own[:, :, :], own[:, :, :], float(EXPERTS - 1), None, ALU.add))
            c.link(v.tensor_tensor(own[:, :, :], own[:, :, :], pos[:, :, :], ALU.subtract))
            c.link(v.tensor_tensor(own[:, :, :], own[:, :, :], more[:, :, :], ALU.mult))
            c.link(v.tensor_tensor(own[:, :, :], own[:, :, :], pos[:, :, :], ALU.add))
            c.link(v.tensor_tensor(own[:, :, :], own[:, :, :], j[:, :, :], ALU.subtract))
            c.link(v.scalar_tensor_tensor(out=slot[:, :, :], in0=own[:, :, :], scalar=float(P), in1=r[:, :, :],
                                          op0=ALU.mult, op1=ALU.add))
            v.tensor_copy(m.slot_u[:, :, :], slot[:, :, :]).then_inc(q["slots"], 1)
            c.link(v.tensor_tensor(cmpx[:, :, :], incl[:, :].unsqueeze(1).to_broadcast([P, EXTRA, EXPERTS]),
                                   iota[:, 0:EXTRA].unsqueeze(2).to_broadcast([P, EXTRA, EXPERTS]), ALU.is_le))
            c.link(v.tensor_reduce(bex[:, :], cmpx[:, :, :], axis=AX.X, op=ALU.add))
            c.link(v.tensor_scalar(bex[:, :], bex[:, :], float(EXPERTS - 1), None, ALU.min))
            c.link(v.tensor_copy(m.plan[:, 0:EXTRA], bex[:, :]))
            c.link(v.tensor_copy(m.plan[:, EXTRA:EXTRA + 1], incl[:, EXPERTS - 1:EXPERTS]))
            dve.wait_ge(q["rows_loaded"], 16)
            v.tensor_copy(rowsf[:, :], rows[:, :]).then_inc(q["rows_ready"], 1)
            dve.wait_ge(q["rows_turned"], 1)
            c.link(v.tensor_copy(m.slot_idx[:, :], m.ps[3][:, 0:BLOCKS]))


def experts(nc, m, name, further):
    KH = MOE_H // P
    wg, wu, wd = m.moe_w
    b = m.moe_buf
    q = {n: [m.sem(f"{name}_{n}{r}") for r in range(2)] for n in (
        "idx_ready", "x_gathered", "turned", "xT_ready", "gu_done", "silu_ready", "h_ready", "down_done", "out_ready",
        "stored", "pool_past")}
    if not further:
        q["w_loaded"], q["wd_loaded"] = m.moe_w_loaded
    else:
        q["w_loaded"], q["wd_loaded"] = ([m.sem(f"{name}_{n}{r}") for r in range(2)] for n in ("w_loaded", "wd_loaded"))
    act_past = m.sem(f"{name}_act_past")
    PASSES = (EXTRA if further else EXPERTS) // 2
    first_block = EXPERTS if further else 0
    out_banks = ((6, 7), (0, 1))

    def passes(eng, body, peel=False):
        if not further:
            with eng.Fori(0, PASSES - 1 if peel else PASSES) as i:
                body(i)
            return
        number = eng.value_load(m.plan[0:1, EXTRA:EXTRA + 1], min_val=0, max_val=EXTRA)
        with eng.Fori(0, PASSES) as i:
            with eng.If(number > 2 * i):
                body(i)
            eng.nop()

    with nc.Block() as block:
        @block.sync
        def _(sp):
            def load_gate_up(r, e):
                load_expert_gate_up(m, sp, r, e, q["w_loaded"][r])

            def load_down(r, e):
                load_expert_down(m, sp, r, e, q["wd_loaded"][r])

            if further:
                def body(i):
                    e = [sp.value_load(m.plan[0:1, bass.ds(2 * i + r, 1)], min_val=0, max_val=EXPERTS - 1)
                         for r in range(2)]
                    for r in range(2):
                        sp.wait_ge(q["gu_done"][r], i)
                        load_gate_up(r, e[r])
                        sp.wait_ge(q["down_done"][r], i)
                        load_down(r, e[r])
                passes(sp, body)
            else:
                def body(i):
                    sp.wait_ge(q["gu_done"][0], i + 1)
                    load_gate_up(0, 2 * i + 2)
                    sp.wait_ge(q["down_done"][1], i)
                    load_down(1, 2 * i + 1)
                    sp.wait_ge(q["gu_done"][1], i + 1)
                    load_gate_up(1, 2 * i + 3)
                    sp.wait_ge(q["down_done"][0], i + 1)
                    load_down(0, 2 * i + 2)
                passes(sp, body, peel=True)
                sp.dma_start(m.ple_wg[:, :, :], m.i["ple_w_gate"][0].rearrange("(p k) n -> p k n", k=KD))\
                    .then_inc(m.ple_loaded, 16)
                sp.wait_ge(q["down_done"][1], PASSES - 1)
                load_down(1, EXPERTS - 1)

        @block.gpsimd
        def _(pool):
            def body(i):
                for r in range(2):
                    pool.wait_ge(q["turned"][r], 2 * i)
                    nc.gpsimd.tensor_copy(b["idx"][:, r:r + 1], m.slot_idx[:, bass.ds(2 * i + r + first_block, 1)])\
                        .then_inc(q["idx_ready"][r], 1)
                    pool.wait_ge(q["idx_ready"][r], i + 1)
                    pool.sem_inc(q["pool_past"][r], 1)
                    nc.gpsimd.indirect_dma_start(b["x"][r][:, :], None, m.xn_dram,
                                                 bass.IndirectOffsetOnAxis(ap=b["idx"][:, r:r + 1], axis=0))\
                        .then_inc(q["x_gathered"][r], 16)
            passes(pool, body)

        @block.tensor
        def _(pe):
            def turn(r, i, outs=0):
                pe.wait_ge(q["x_gathered"][r], 16 * (i + 1))
                pe.wait_ge(q["xT_ready"][r], 2 * i)
                if r == 0:
                    pe.wait_ge(q["out_ready"][1], outs)
                for h in range(2):
                    for k in range(4):
                        mm = nc.tensor.transpose(m.ps[2 * r + h][:, k * P:(k + 1) * P],
                                                 b["x"][r][:, 4 * h + k:D:KD], m.ident[:, :])
                    mm.then_inc(q["turned"][r], 1)

            def gate_up(r, i):
                pe.wait_ge(q["w_loaded"][r], 32 * (i + 1))
                pe.wait_ge(q["xT_ready"][r], 2 * i + 2)
                pe.wait_ge(q["h_ready"][r], i)
                for n, w in enumerate((wg, wu)):
                    for c in range(KH):
                        for k in range(KD):
                            mm = nc.tensor.matmul(m.ps[4 + r][:, (KH * n + c) * P:(KH * n + c + 1) * P],
                                                  w[:, r, k, c * P:(c + 1) * P], b["xT"][:, r, k, :],
                                                  start=(k == 0), stop=(k == KD - 1))
                mm.then_inc(q["gu_done"][r], 1)

            def down(r, i, tokens=0):
                pe.wait_ge(q["wd_loaded"][r], 16 * (i + 1))
                pe.wait_ge(q["h_ready"][r], i + 1)
                pe.wait_ge(q["out_ready"][r], i)
                if r == 1:
                    pe.wait_ge(q["xT_ready"][0], tokens)
                for h in range(2):
                    for k in range(KH):
                        mm = nc.tensor.matmul(m.ps[out_banks[r][h]][:, :], b["h"][:, r, k, :],
                                              wd[:, r, k, h * HALF:(h + 1) * HALF],
                                              start=(k == 0), stop=(k == KH - 1))
                mm.then_inc(q["down_done"][r], 1)

            if further:
                def body(i):
                    turn(0, i, outs=i)
                    turn(1, i)
                    gate_up(0, i)
                    gate_up(1, i)
                    down(0, i)
                    down(1, i, tokens=2 * i + 2)
                passes(pe, body)
            else:
                turn(0, 0)
                gate_up(0, 0)
                turn(1, 0)

                def body(i):
                    gate_up(1, i)
                    turn(0, i + 1, outs=i)
                    down(0, i)
                    gate_up(0, i + 1)
                    turn(1, i + 1)
                    down(1, i, tokens=2 * i + 4)
                passes(pe, body, peel=True)
                gate_up(1, PASSES - 1)
                down(0, PASSES - 1)
                down(1, PASSES - 1, tokens=2 * PASSES)

        @block.scalar
        def _(act):
            def silu(r, i):
                act.wait_ge(q["gu_done"][r], i + 1)
                act.wait_ge(q["h_ready"][r], i)
                nc.scalar.activation(b["sg"][:, r, :], m.ps[4 + r][:, 0:MOE_H], ACT.Silu)\
                    .then_inc(q["silu_ready"][r], 1)

            def store(r, i):
                act.wait_ge(q["down_done"][r], i + 1)
                act.wait_ge(q["stored"][r], 16 * i)
                banks = m.psum[:, out_banks[r][0] * HALF:(out_banks[r][1] + 1) * HALF]
                nc.scalar.copy(b["out"][:, r, :], banks).then_inc(q["out_ready"][r], 1)
                act.wait_ge(q["out_ready"][r], i + 1)
                act.dma_start(m.y_slots[bass.ds((2 * i + r + first_block) * P, P), :], b["out"][:, r, :])\
                    .then_inc(q["stored"][r], 16)

            if further:
                def body(i):
                    silu(0, i)
                    silu(1, i)
                    store(0, i)
                    store(1, i)
                    for r in range(2):
                        act.wait_ge(q["stored"][r], 16 * (i + 1))
                    act.sem_inc(act_past, 1)
                passes(act, body)
            else:
                silu(0, 0)

                def body(i):
                    silu(1, i)
                    store(0, i)
                    silu(0, i + 1)
                    store(1, i)
                passes(act, body, peel=True)
                silu(1, PASSES - 1)
                store(0, PASSES - 1)
                store(1, PASSES - 1)
                for r in range(2):
                    act.wait_ge(q["stored"][r], 16 * PASSES)

        @block.vector
        def _(dve):
            def scale(r, i):
                for h in range(2):
                    dve.wait_ge(q["turned"][r], 2 * i + h + 1)
                    dve.wait_ge(q["gu_done"][r], i)
                    nc.vector.tensor_tensor(b["xT"][:, r, 4 * h:4 * h + 4, :],
                                            m.ps[2 * r + h][:, :].rearrange("p (k n) -> p k n", k=4),
                                            m.moe_gain[:, 4 * h:4 * h + 4].unsqueeze(2).to_broadcast([P, 4, P]),
                                            ALU.mult).then_inc(q["xT_ready"][r], 1)

            def hidden(r, i):
                dve.wait_ge(q["silu_ready"][r], i + 1)
                dve.wait_ge(q["down_done"][r], i)
                nc.vector.tensor_tensor(b["h"][:, r, :, :].rearrange("p k n -> p (k n)"), b["sg"][:, r, :],
                                        m.ps[4 + r][:, MOE_H:2 * MOE_H], ALU.mult).then_inc(q["h_ready"][r], 1)

            if further:
                def body(i):
                    scale(0, i)
                    scale(1, i)
                    hidden(0, i)
                    hidden(1, i)
                passes(dve, body)
            else:
                scale(0, 0)
                hidden(0, 0)
                scale(1, 0)

                def body(i):
                    hidden(1, i)
                    scale(0, i + 1)
                    hidden(0, i + 1)
                    scale(1, i + 1)
                passes(dve, body, peel=True)
                hidden(1, PASSES - 1)


def load_expert_gate_up(m, eng, r, e, loaded):
    wg, wu, _ = m.moe_w
    for w, name in ((wg, "moe_w_gate"), (wu, "moe_w_up")):
        eng.dma_start(w[:, r, :, :], m.i[name][0][e, :, :].rearrange("(p k) n -> p k n", k=KD)).then_inc(loaded, 16)


def load_expert_down(m, eng, r, e, loaded):
    eng.dma_start(m.moe_w[2][:, r, :, :], m.i["moe_w_down"][0][e, :, :].rearrange("(k p) n -> p k n", k=MOE_H // P))\
        .then_inc(loaded, 16)


def finish(nc, m):
    RING = 3
    rows = m.sb("finish_rows", [P, RING, 2, D])
    xn = m.sb("finish_xn", [P, D])
    hT = m.sb("finish_hT", [P, 2, KD, P])
    sg = m.sb("finish_sg", [P, D])
    res = m.sb("finish_res", [P, D])
    gathered = [m.sem(f"finish_gathered{r}{s}") for r in range(RING) for s in range(2)]
    stored = m.sem("finish_stored")
    q = {n: m.sem(f"finish_{n}") for n in ("added", "squared", "mean_made", "rooted", "normed", "turned", "hT_ready",
                                           "gate_done", "sig_ready", "summed")}
    ch = m.chains(nc, "finish")
    with nc.Block() as block:
        @block.gpsimd
        def _(pool):
            for t in range(NT):
                if t >= RING:
                    pool.wait_ge(q["added"], 2 * (t - RING + 1))
                for s in range(2):
                    nc.gpsimd.indirect_dma_start(rows[:, t % RING, s, :], None, m.y_slots,
                                                 bass.IndirectOffsetOnAxis(ap=m.slot_u[:, t, s:s + 1], axis=0))\
                        .then_inc(gathered[2 * (t % RING) + s], 16)

        @block.sync
        def _(sp):
            for t in range(NT):
                sp.wait_ge(q["summed"], t + 1)
                sp.dma_start(m.out[0, t * P:(t + 1) * P, :], res[:, :]).then_inc(stored, 16)
            sp.wait_ge(stored, 16 * NT)

        @block.tensor
        def _(pe):
            def turn(t):
                pe.wait_ge(q["normed"], t + 1)
                if t:
                    pe.wait_ge(q["hT_ready"], 2 * t)
                for n in range(2):
                    for k in range(4):
                        mm = nc.tensor.transpose(m.ps[n][:, k * P:(k + 1) * P], xn[:, 4 * n + k:D:KD], m.ident[:, :])
                    mm.then_inc(q["turned"], 1)

            turn(0)
            pe.wait_ge(m.ple_loaded, 16)
            for t in range(NT):
                pe.wait_ge(q["hT_ready"], 2 * t + 2)
                if t >= 2:
                    pe.wait_ge(q["sig_ready"], 2 * (t - 1))
                for n in range(2):
                    for k in range(KD):
                        mm = nc.tensor.matmul(m.ps[2 + 2 * (t % 2) + n][:, :], hT[:, t % 2, k, :],
                                              m.ple_wg[:, k, n * HALF:(n + 1) * HALF],
                                              start=(k == 0), stop=(k == KD - 1))
                    mm.then_inc(q["gate_done"], 1)
                    if n == 0 and t < NT - 1:
                        turn(t + 1)

        @block.scalar
        def _(act):
            def root(t):
                act.wait_ge(q["added"], 2 * t + 2)
                nc.scalar.activation(m.junk[:, t % 2, :], m.x2[:, t, :], ACT.Square,
                                     accum_out=m.sumsq[:, t:t + 1]).then_inc(q["squared"], 1)
                act.wait_ge(q["mean_made"], t + 1)
                nc.scalar.activation(m.rms[:, t:t + 1], m.rms[:, t:t + 1], ACT.Sqrt).then_inc(q["rooted"], 1)

            root(0)
            root(1)
            for t in range(NT):
                for n in range(2):
                    act.wait_ge(q["gate_done"], 2 * t + n + 1)
                    if t:
                        act.wait_ge(q["summed"], t)
                    nc.scalar.activation(sg[:, n * HALF:(n + 1) * HALF], m.ps[2 + 2 * (t % 2) + n][:, :],
                                         ACT.Sigmoid).then_inc(q["sig_ready"], 1)
                if t + 2 < NT:
                    root(t + 2)

        @block.vector
        def _(dve):
            c = Chain(dve, ch["dve"])

            def mean(t):
                for s in range(2):
                    dve.wait_ge(gathered[2 * (t % RING) + s], 16 * (t // RING + 1))
                    if s:
                        dve.wait_ge(q["added"], 2 * t + 1)
                    nc.vector.scalar_tensor_tensor(out=m.x2[:, t, :], in0=rows[:, t % RING, s, :],
                                                   scalar=m.weight[:, t, s:s + 1], in1=m.x2[:, t, :],
                                                   op0=ALU.mult, op1=ALU.add).then_inc(q["added"], 1)
                dve.wait_ge(q["squared"], t + 1)
                nc.vector.tensor_scalar(m.rms[:, t:t + 1], m.sumsq[:, t:t + 1], 1.0 / D, EPS, ALU.mult,
                                        ALU.add).then_inc(q["mean_made"], 1)
                dve.wait_ge(q["rooted"], t + 1)
                c.link(nc.vector.reciprocal(m.rstd[:, t:t + 1], m.rms[:, t:t + 1]))

            def norm(t):
                if t:
                    dve.wait_ge(q["turned"], 2 * t)
                nc.vector.tensor_scalar(xn[:, :], m.x2[:, t, :], m.rstd[:, t:t + 1], None,
                                        ALU.mult).then_inc(q["normed"], 1)

            def scale(t):
                for n in range(2):
                    dve.wait_ge(q["turned"], 2 * t + n + 1)
                    nc.vector.tensor_tensor(hT[:, t % 2, 4 * n:4 * n + 4, :],
                                            m.ps[n][:, :].rearrange("p (k n) -> p k n", k=4),
                                            m.ple_gain[:, 4 * n:4 * n + 4].unsqueeze(2).to_broadcast([P, 4, P]),
                                            ALU.mult).then_inc(q["hT_ready"], 1)

            mean(0)
            norm(0)
            scale(0)
            mean(1)
            norm(1)
            for t in range(NT):
                if t + 1 < NT:
                    scale(t + 1)
                dve.wait_ge(q["sig_ready"], 2 * t + 2)
                dve.wait_ge(stored, 16 * t)
                c.link(nc.vector.tensor_tensor(res[:, :], sg[:, :], m.proj[:, t, :], ALU.mult))
                nc.vector.tensor_tensor(res[:, :], res[:, :], m.x2[:, t, :], ALU.add).then_inc(q["summed"], 1)
                if t + 2 < NT:
                    mean(t + 2)
                    norm(t + 2)


def phase_constants(nc, m):
    m.slot_tok = nc.dram_tensor("slot_tok", [SLOTS, 1], I32).ap()
    m.xn_dram = nc.dram_tensor("xn_rows", [S, D], F32).ap()
    m.y_slots = nc.dram_tensor("y_slots", [SLOTS, D], F32).ap()
    constants(nc, m)


def phase_mix_norm(nc, m):
    m.xbc = m.sb("xbc", [P, MC, S])
    m.y = m.sb("y", [P, NT, INNER])
    m.dt = m.sb("dt", [P, NT, SSM_HEADS])
    m.adt = m.sb("adt", [P, NT + 1, SSM_HEADS])
    m.wz = m.sb("wz", [P, KD, INNER])
    m.ssd_base = m.top
    m.conv_ring = m.sb("conv_ring", [P, 3, KD, P])
    m.dt_w = m.sb("dt_w", [P, KD, SSM_HEADS])
    m.conv_w_loaded = [m.sem(f"conv_w_loaded{r}") for r in range(3)]
    m.dt_w_loaded, m.wz_loaded = m.sem("dt_w_loaded"), m.sem("wz_loaded")
    norm_transpose(nc, m, m.x_in, m.mix_gain, m.hT)


def phase_ssm(nc, m):
    project_conv(nc, m)
    m.top = m.ssd_base
    ssd(nc, m)
    m.nsa_w, m.nsa_w_at = m.sb_at_end("nsa_w", [P, KD, NSA_W])
    m.nsa_w_loaded = m.sem("nsa_w_loaded")
    m.top = m.base
    m.ybT = m.sb("ybT", [P, KD, S])
    keep, m.top = m.top, m.ssd_base - 4 * KD * INNER
    group_norm(nc, m, m.ybT)
    m.top = m.base = keep


def phase_nsa(nc, m):
    m.yaT = m.sb("yaT", [P, Q_W // P, S])
    m.top = m.base
    JP = CMP_BLOCK // 2
    m.cmp_w = (m.sb("cmp_w1", [P, 2, JP, CMP_HIDDEN]), None, None)
    m.base = m.top
    m.qT = m.sb("qT", [P, E, S])
    m.ksT, m.kwT = m.sb("ksT", [P, S]), m.sb("kwT", [P, S])
    m.v_sel, m.v_win = m.sb("v_sel", [P, NT, GROUPS, HD + 1]), m.sb("v_win", [P, NT, GROUPS, HD + 1])
    m.cT = m.sb("cT", [P, 2, S])
    m.kcT = m.sb("kcT", [P, NCMP])
    m.v_cmp = m.sb("v_cmp", [NCMP, GROUPS, HD + 1])
    keep = m.top
    m.cmp_w = (m.cmp_w[0], m.sb("cmp_w2", [P, 2, HD]), m.sb("cmp_pos", [JP, 2, P]))
    m.cmp_loaded = m.sem("cmp_loaded")
    nsa_base = m.top
    nsa_project(nc, m)
    assert m.top <= m.nsa_w_at
    m.top = nsa_base
    compress(nc, m)
    m.top = keep
    m.ya = m.sb("ya", [P, NT, HEADS, HD])
    RING = 2
    KW = sum(x[0] for x in merge_parts(m))
    m.merge_w, m.merge_w_at = m.sb_at_end("merge_w", [P, RING, KW, P])
    m.merge_w_loaded = [m.lasting_sem(f"merge_w_loaded{r}") for r in range(RING)]
    attention(nc, m)
    assert m.top <= m.merge_w_at
    turn_ya(nc, m)
    m.renew_semaphores()
    m.top = m.base


def phase_merge(nc, m):
    m.x2 = m.sb("x2", [P, NT, D])
    m.x_loaded = m.sem("x_loaded")
    m.weight = m.sb("weight", [P, NT, 2])
    m.slot_u = m.sb("slot_u", [P, NT, 2], U32)
    m.slot_idx = m.sb("slot_idx", [P, BLOCKS], U32)
    m.plan = m.sb("plan", [P, EXTRA + 1], I32)
    m.route_w = m.sb("route_w", [P, KD, ROUTES])
    m.above = m.top
    m.mergedT = m.sb("mergedT", [P, KD, S])
    keep = m.top
    merge(nc, m)
    assert m.top <= m.merge_w_at
    m.top = m.low
    m.xn = m.sb("xn", [P, 2, D])
    m.h2T = m.sb("h2T", [P, 2, KD, P])
    m.pin = m.sb("ple_in", [P, NT, PLE])
    m.pT = m.sb("ple_pT", [P, PLE // P, S])
    m.tail = m.top
    m.moe_w = (m.sb("moe_wg", [P, 2, KD, MOE_H]), m.sb("moe_wu", [P, 2, KD, MOE_H]),
               m.sb("moe_wd", [P, 2, MOE_H // P, D]))
    m.moe_w_loaded = [[m.sem(f"moe_first_{n}{r}") for r in range(2)] for n in ("w_loaded", "wd_loaded")]
    m.route_w_loaded, m.p_loaded = m.sem("route_w_loaded"), m.sem("p_loaded")
    m.logits = m.ps[4]
    m.top = keep
    project_out(nc, m)
    m.top = m.above


def phase_route(nc, m):
    m.proj = m.sb("proj", [P, NT, D])
    m.above = m.top
    m.ple_wp = m.sb("ple_wp", [P, PLE // P, D])
    route(nc, m)
    m.top = m.above


def phase_experts(nc, m):
    m.top = m.low
    m.ple_wg = m.sb("ple_wg", [P, KD, D])
    assert m.top == m.tail
    m.ple_loaded = m.sem("ple_loaded")
    m.top = m.above
    m.moe_buf = {"idx": m.sb("moe_idx", [P, 2], U32), "x": [m.sb(f"moe_x{r}", [P, D]) for r in range(2)],
                 "xT": m.sb("moe_xT", [P, 2, KD, P]), "sg": m.sb("moe_sg", [P, 2, MOE_H]),
                 "h": m.sb("moe_h", [P, 2, MOE_H // P, P]), "out": m.sb("moe_out", [P, 2, D])}
    experts(nc, m, "moe_first", False)
    experts(nc, m, "moe_more", True)


def phase_finish(nc, m):
    m.top = m.tail
    finish(nc, m)


PHASES = [phase_constants, phase_mix_norm, phase_ssm, phase_nsa, phase_merge, phase_route, phase_experts, phase_finish]


def program(nc, ins, out):
    m = Machine(nc, ins, out)
    for phase in PHASES:
        phase(nc, m)


def kernel(**inputs):
    import numpy as np
    from concourse import bacc
    from concourse.bass_utils import run_bass_kernel_spmd

    nc = bacc.Bacc("TRN2", target_bir_lowering=False, num_devices=1)
    arrays, ins = {}, {}
    for name, value in inputs.items():
        a = np.ascontiguousarray(value)
        arrays[f"in_{name}"] = a
        ins[name] = nc.dram_tensor(f"in_{name}", a.shape, mybir.dt.from_np(a.dtype), kind="ExternalInput").ap()
    out = nc.dram_tensor("out", (1, S, D), F32, kind="ExternalOutput").ap()
    program(nc, ins, out)
    r = run_bass_kernel_spmd(nc, [arrays], core_ids=[0])
    return r.results[0]["out"]
```

```python
import concourse.bass as bass
from concourse import mybir

F32 = mybir.dt.float32
F32R = mybir.dt.float32r
BF16 = mybir.dt.bfloat16
I32 = mybir.dt.int32
U32 = mybir.dt.uint32
ALU = mybir.AluOpType
ACT = mybir.ActivationFunctionType
AX = mybir.AxisListType

P = 128
D = 1024
S = 1024
KD = D // P
NT = S // P
HALF = 512
EPS = 1e-6
MASK = -1e30

HEADS, GROUPS, HD = 8, 2, 64
E = HEADS // GROUPS
Q_W, KV_W, GATE_W = HEADS * HD, GROUPS * HD, HEADS * 3
NSA_W = Q_W + 6 * KV_W + GATE_W
SSM_HEADS, SSM_P, SSM_G, SSM_N = 16, 64, 2, 128
INNER = SSM_HEADS * SSM_P
GW = INNER // SSM_G
CONV_DIM = INNER + 2 * SSM_G * SSM_N
CONV = 4
MC = CONV_DIM // P
Z0 = NSA_W
XBC0 = Z0 + INNER
DT0 = XBC0 + CONV_DIM
BR0 = DT0 + SSM_HEADS
CMP_STRIDE, CMP_BLOCK, CMP_HIDDEN = 16, 32, 128
NCMP = S // CMP_STRIDE - 1
WINDOW = 512
EXPERTS, MGROUPS, PER_GROUP, MOE_H = 32, 4, 8, 256
ROUTES = MGROUPS + EXPERTS
EXTRA = 2 * S // P
BLOCKS = EXPERTS + EXTRA
SLOTS = BLOCKS * P
PLE = 256


def high_part(engine, out, src):
    return engine.tensor_copy(out, src)


def low_part(engine, out, src, high):
    return engine.tensor_tensor(out, src, high.bitcast(F32), ALU.subtract)


def split_product(nc, dst, weights, moving, first, last):
    pairs = ((weights[0], moving[0]), (weights[0], moving[1]), (weights[1], moving[0]))
    for n, (w, x) in enumerate(pairs):
        mm = nc.tensor.matmul(dst, w, x, start=(first and n == 0), stop=(last and n == 2))
    return mm


class Chain:

    def __init__(self, eng, sem):
        self.eng, self.sem, self.start, self.base, self.n = eng, sem, 0, 0, 0

    def link(self, ins):
        ins.then_inc(self.sem, 1)
        self.n += 1
        self.eng.wait_ge(self.sem, self.base + self.n)

    def put(self, ins):
        ins.then_inc(self.sem, 1)
        self.n += 1
        return self.base + self.n

    def need(self, count):
        self.eng.wait_ge(self.sem, count)

    def enter(self, i, per):
        self.start += self.n
        self.n, self.base = 0, self.start + i * per

    def leave(self, passes, per):
        assert self.n == per, (self.n, per)
        self.start += passes * per
        self.base, self.n = self.start, 0


class Machine:

    def __init__(self, nc, ins, out):
        self.nc, self.i, self.out, self.sems = nc, ins, out, []
        self.psum = nc.alloc_psum_tensor("banks", [P, 8 * HALF], F32)
        self.ps = [self.psum[:, b * HALF:(b + 1) * HALF] for b in range(8)]
        self.top = nc.sbuf_base + (-nc.sbuf_base) % 64
        self.end = nc.sbuf_usable_end
        self.at = {}

    def sb(self, name, shape, dt=F32):
        size = 2 if dt == BF16 else 4
        for n in shape[1:]:
            size *= n
        t = self.nc.alloc_sbuf_tensor_at(name, shape, dt, offset=self.top)
        self.at[name] = self.top
        self.top += size + (-size) % 64
        assert self.top <= self.end, (name, self.top, self.end)
        return t

    def sb_at_end(self, name, shape):
        size = 4
        for n in shape[1:]:
            size *= n
        at = (self.end - size) // 64 * 64
        self.at[name] = at
        return self.nc.alloc_sbuf_tensor_at(name, shape, F32, offset=at), at

    def part(self, name, shape, place):
        return self.nc.alloc_sbuf_tensor_at(name, shape, F32R, offset=self.at[place])

    def lasting_sem(self, name):
        return self.nc.alloc_semaphore(name=name)

    def sem(self, name):
        self.sems.append(self.nc.alloc_semaphore(name=name))
        return self.sems[-1]

    def chains(self, nc, phase):
        return Steps(self, phase)

    def renew_semaphores(self):
        self.nc.clear_and_free_semaphores(self.sems)
        self.sems = []
        self.nc.all_engine_barrier()


class Steps(dict):

    def __init__(self, m, phase):
        super().__init__()
        self.m, self.phase = m, phase

    def __missing__(self, engine):
        self[engine] = self.m.sem(f"{self.phase}_{engine}_step")
        return self[engine]


def constants(nc, m):
    m.ident = m.sb("ident", [P, P])
    m.ones = m.sb("ones", [P, P])
    m.tri_le = m.sb("tri_le", [P, P])
    m.tri_lt = m.sb("tri_lt", [P, P], BF16)
    m.onesb = m.sb("onesb", [P, P], BF16)
    m.identb = m.sb("identb", [P, P], BF16)
    m.mask_future = m.sb("mask_future", [P, P], BF16)
    m.mask_far = m.sb("mask_far", [P, P], BF16)
    m.mask_past = m.sb("mask_past", [P, P], BF16)
    m.mask_cmp = m.sb("mask_cmp", [P, NT, NCMP + 1], BF16)
    m.any_cmp = m.sb("any_cmp", [P, 1])
    m.small = m.sb("small", [P, 2, P])
    m.mix_gain = m.sb("mix_gain", [P, KD])
    m.moe_gain = m.sb("moe_gain", [P, KD])
    m.ple_gain = m.sb("ple_gain", [P, KD])
    m.ssm_gain = m.sb("ssm_gain", [P, KD])
    m.qk_gain = m.sb("qk_gain", [P, 4])
    m.dt_bias = m.sb("dt_bias", [P, SSM_HEADS])
    m.neg_a = m.sb("neg_a", [P, SSM_HEADS])
    m.d_skip = m.sb("d_skip", [P, SSM_HEADS])
    m.route_bias = m.sb("route_bias", [P, ROUTES])
    m.gate_scale = m.sb("gate_scale", [P, NT, GATE_W])
    m.junk = m.sb("junk", [P, 2, D])
    m.sumsq = m.sb("sumsq", [P, NT])
    m.rms = m.sb("rms", [P, NT])
    m.rstd = m.sb("rstd", [P, NT])
    m.low = m.top
    m.hT = m.sb("hT", [P, KD, S])
    m.base = m.top
    m.x_in = m.sb("x_in", [P, NT, D])
    m.mix_x_loaded = [m.sem(f"mix_x_loaded{t}") for t in range(NT)]
    m.top = m.base
    made, loaded, turned = m.sem("const_made"), m.sem("const_loaded"), m.sem("const_turned")
    ch = m.chains(nc, "const")
    i = m.i
    m.const_dmas = 0
    with nc.Block() as block:
        @block.gpsimd
        def _(pool):
            c = Chain(pool, ch["pool"])

            def tri(t, op, cm, step, base, inside, outside, shape=(P,)):
                c.link(nc.gpsimd.memset(t, inside))
                c.link(nc.gpsimd.affine_select(out=t, in_=t, compare_op=op, fill=outside, base=base,
                                               pattern=[[step, P]], channel_multiplier=cm))
            tri(m.ident[:, :], ALU.not_equal, 1, -1, 0, 0.0, 1.0)
            tri(m.identb[:, :], ALU.not_equal, 1, -1, 0, 0.0, 1.0)
            tri(m.tri_le[:, :], ALU.is_ge, -1, 1, 0, 1.0, 0.0)
            tri(m.tri_lt[:, :], ALU.is_gt, -1, 1, 0, 1.0, 0.0)
            tri(m.mask_future[:, :], ALU.is_ge, 1, -1, 0, 0.0, MASK)
            tri(m.mask_far[:, :], ALU.is_gt, -1, 1, 0, 0.0, MASK)
            tri(m.mask_past[:, :], ALU.is_ge, -1, 1, 0, 0.0, MASK)
            c.link(nc.gpsimd.memset(m.ones[:, :], 1.0))
            c.link(nc.gpsimd.memset(m.onesb[:, :], 1.0))
            c.link(nc.gpsimd.memset(m.mask_cmp[:, :, :], 0.0))
            c.link(nc.gpsimd.affine_select(out=m.mask_cmp[:, :, :], in_=m.mask_cmp[:, :, :], compare_op=ALU.is_ge,
                                           fill=MASK, base=-(CMP_BLOCK - 1), channel_multiplier=1,
                                           pattern=[[P, NT], [-CMP_STRIDE, NCMP + 1]]))
            c.link(nc.gpsimd.memset(m.any_cmp[:, :], 1.0))
            nc.gpsimd.affine_select(out=m.any_cmp[:, :], in_=m.any_cmp[:, :], compare_op=ALU.is_ge, fill=0.0,
                                    base=-(CMP_BLOCK - 1), channel_multiplier=1, pattern=[[0, 1]]).then_inc(made, 1)

        @block.sync
        def _(sp):
            def load(dst, src):
                sp.dma_start(dst, src).then_inc(loaded, 16)
                m.const_dmas += 1
            load(m.small[0:CONV * MC, 0, :], i["ssm_conv_w"][0].rearrange("j (m p) -> (j m) p", p=P))
            load(m.small[CONV * MC:(CONV + 1) * MC, 0, :], i["ssm_conv_b"][0].rearrange("(m p) -> m p", p=P))
            load(m.mix_gain[:, :], i["mix_norm"][0].rearrange("(p k) -> p k", k=KD))

        @block.tensor
        def _(pe):
            pe.wait_ge(made, 1)
            pe.wait_ge(loaded, 16 * m.const_dmas)
            n = (CONV + 1) * MC
            nc.tensor.transpose(m.ps[0][:, 0:n], m.small[0:n, 0, :], m.ident[0:n, 0:n]).then_inc(turned, 1)

        @block.scalar
        def _(act):
            for t in range(NT):
                act.dma_start(m.x_in[:, t, :], m.i["x"][0][t * P:(t + 1) * P, :]).then_inc(m.mix_x_loaded[t], 16)

        @block.vector
        def _(dve):
            dve.wait_ge(turned, 1)
            n = (CONV + 1) * MC
            nc.vector.tensor_copy(m.small[:, 1, 0:n], m.ps[0][:, 0:n]).then_inc(turned, 1)
    m.conv_w = m.small[:, 1, 0:CONV * MC].rearrange("p (j m) -> p j m", j=CONV)
    m.conv_b = m.small[:, 1, CONV * MC:(CONV + 1) * MC]


def norm_transpose(nc, m, x, gain, hT):
    here = m.mix_x_loaded
    squared, mean_made, rooted, normed, turned = (m.sem(f"mix_{n}") for n in
                                                  ("squared", "mean_made", "rooted", "normed", "turned"))
    read = [m.sem("mix_act_read"), m.sem("mix_dve_read")]
    params_loaded = m.sem("params_loaded")
    ch = m.chains(nc, "mix")
    NG = 2 * KD
    with nc.Block() as block:
        @block.sync
        def _(sp):
            load_conv_weights(m, sp, range(len(m.conv_w_loaded)))
            load_params(m, sp, params_loaded)
            sp.dma_start(m.dt_w[:, :, :], m.i["w_in"][0][:, DT0:DT0 + SSM_HEADS].rearrange("(p k) n -> p k n", k=KD))\
                .then_inc(m.dt_w_loaded, 16)
            sp.wait_ge(params_loaded, 16 * PARAMS)

        @block.scalar
        def _(act):
            def square(t):
                act.wait_ge(here[t], 16)
                nc.scalar.activation(m.junk[:, t % 2, :], x[:, t, :], ACT.Square,
                                     accum_out=m.sumsq[:, t:t + 1]).then_inc(squared, 1)

            def root(t):
                act.wait_ge(mean_made, t + 1)
                nc.scalar.activation(m.rms[:, t:t + 1], m.rms[:, t:t + 1], ACT.Sqrt).then_inc(rooted, 1)

            square(0)
            for t in range(NT):
                if t + 1 < NT:
                    if t >= 1:
                        act.wait_ge(squared, t)
                    square(t + 1)
                root(t)
            for n in range(0, NG, 2):
                act.wait_ge(turned, n + 1)
                k = n % KD
                h = n // KD
                nc.scalar.activation(hT[:, k, h * HALF:(h + 1) * HALF], m.ps[n % 4][:, :], ACT.Copy,
                                     scale=gain[:, k:k + 1]).then_inc(read[0], 1)
            c = Chain(act, ch["act"])
            act.wait_ge(params_loaded, 16 * PARAMS)
            c.link(nc.scalar.activation(m.neg_a[:, :], m.neg_a[:, :], ACT.Exp))
            c.link(nc.scalar.mul(m.qk_gain[:, 0:1], m.qk_gain[:, 0:1], HD ** -0.5))
            c.link(nc.scalar.mul(m.neg_a[:, :], m.neg_a[:, :], -1.0))

        @block.vector
        def _(dve):
            c = Chain(dve, ch["dve"])

            def mean(t):
                dve.wait_ge(squared, t + 1)
                nc.vector.tensor_scalar(m.rms[:, t:t + 1], m.sumsq[:, t:t + 1], 1.0 / D, EPS, ALU.mult,
                                        ALU.add).then_inc(mean_made, 1)

            mean(0)
            for t in range(NT):
                if t + 1 < NT:
                    mean(t + 1)
                dve.wait_ge(rooted, t + 1)
                c.link(nc.vector.reciprocal(m.rstd[:, t:t + 1], m.rms[:, t:t + 1]))
                nc.vector.tensor_scalar(x[:, t, :], x[:, t, :], m.rstd[:, t:t + 1], None,
                                        ALU.mult).then_inc(normed, 1)
            for n in range(1, NG, 2):
                dve.wait_ge(turned, n + 1)
                k = n % KD
                h = n // KD
                nc.vector.tensor_scalar(hT[:, k, h * HALF:(h + 1) * HALF], m.ps[n % 4][:, :], gain[:, k:k + 1],
                                        None, ALU.mult).then_inc(read[1], 1)

        @block.tensor
        def _(pe):
            for n in range(NG):
                k, h = n % KD, n // KD
                pe.wait_ge(normed, 4 * (h + 1))
                if n >= 4:
                    pe.wait_ge(read[n % 2], (n - 4) // 2 + 1)
                for j in range(4):
                    t = 4 * h + j
                    mm = nc.tensor.transpose(m.ps[n % 4][:, j * P:(j + 1) * P], x[:, t, k:D:KD], m.ident[:, :])
                mm.then_inc(turned, 1)


PARAMS = 3 + 4 * GROUPS + 3 + 2


def load_params(m, eng, loaded):
    i = m.i
    for t, name in ((m.moe_gain, "moe_norm"), (m.ple_gain, "ple_norm"), (m.ssm_gain, "ssm_norm")):
        eng.dma_start(t[:, :], i[name][0].rearrange("(p k) -> p k", k=KD)).then_inc(loaded, 16)
    for n, name in enumerate(("nsa_q_gain", "nsa_kc_gain", "nsa_ks_gain", "nsa_kw_gain")):
        for g in range(GROUPS):
            eng.dma_start(m.qk_gain[g * HD:(g + 1) * HD, n:n + 1], i[name][0].rearrange("(d a) -> d a", a=1))\
                .then_inc(loaded, 16)
    for t, name in ((m.dt_bias[:, :], "ssm_dt_bias"), (m.neg_a[:, :], "ssm_a_log"), (m.d_skip[:, :], "ssm_d"),
                    (m.route_bias[:, 0:MGROUPS], "moe_b_group"), (m.route_bias[:, MGROUPS:], "moe_b_expert")):
        eng.dma_start(t, i[name].partition_broadcast(P).rearrange("p a h -> p (a h)")).then_inc(loaded, 16)


def load_conv_weights(m, eng, slots, it=0):
    wv = m.i["w_in"][0][:, XBC0:XBC0 + CONV_DIM].rearrange("(p k) (m c) -> m p k c", k=KD, c=P)
    ring = len(m.conv_w_loaded)
    for r in slots:
        eng.dma_start(m.conv_ring[:, r, :, :], wv[ring * it + r, :, :, :]).then_inc(m.conv_w_loaded[r], 16)


def project_conv(nc, m):
    RING, BODY = 3, 6
    LOOPS = MC // BODY
    W, here = m.conv_ring, m.conv_w_loaded
    high, low = m.part("conv_hT_high", [P, KD, S], "y"), m.part("conv_hT_low", [P, KD, S], "wz")
    high_w = m.sb("conv_w_high", [P, 2, KD, P], F32R)
    low_w = m.part("conv_w_low", [P, RING, KD, P], "conv_ring")
    w_split, high_made = m.sem("conv_w_split"), m.sem("conv_high_made")
    low_made = [m.sem(f"conv_low_made_{e}") for e in ("pool", "dve")]
    pre = m.sb("conv_pre", [P, 2, CONV - 1 + S])
    raw, mag, ln = (m.sb(f"dt_{n}", [P, NT, SSM_HEADS]) for n in ("raw", "mag", "ln"))
    dt_done, sized, logged = (m.sem(f"dt_{n}") for n in ("products_done", "sized", "logged"))
    per_head = [P, NT, SSM_HEADS]
    done, used, free, pre_free = (m.sem(f"conv_{n}") for n in
                                          ("products_done", "w_free", "bank_free", "pre_free"))
    ch = m.chains(nc, "conv")
    with nc.Block() as block:
        @block.sync
        def _(sp):
            with sp.Fori(0, MC // RING - 1) as it:
                for r in range(RING):
                    sp.wait_ge(used, RING * it + r + 2)
                    load_conv_weights(m, sp, (r,), it + 1)

        @block.gpsimd
        def _(pool):
            def split_w(n, r):
                pool.wait_ge(here[r % RING], 16 * (n // RING + 1) if isinstance(n, int) else
                             16 * (2 * it + r // RING + 1))
                pool.wait_ge(used, n)
                high_part(nc.gpsimd, high_w[:, r % 2, :, :], W[:, r % RING, :, :]).then_inc(w_split, 1)
                pool.wait_ge(w_split, 2 * n + 1)
                low_part(nc.gpsimd, low_w[:, r % RING, :, :], W[:, r % RING, :, :], high_w[:, r % 2, :, :])\
                    .then_inc(w_split, 1)

            split_w(0, 0)
            for n in range(0, 2 * KD, 2):
                pool.wait_ge(high_made, n + 1)
                h, k = divmod(n, KD)
                cols = slice(h * HALF, (h + 1) * HALF)
                low_part(nc.gpsimd, low[:, k, cols], m.hT[:, k, cols], high[:, k, cols]).then_inc(low_made[0], 1)
            for r in range(1, BODY):
                split_w(r, r)
            with pool.Fori(1, LOOPS) as it:
                for r in range(BODY):
                    split_w(BODY * it + r, r)

        @block.tensor
        def _(pe):
            pe.wait_ge(m.dt_w_loaded, 16)
            for t in range(NT):
                for k in range(KD):
                    mm = nc.tensor.matmul(m.ps[6][:, t * SSM_HEADS:(t + 1) * SSM_HEADS],
                                          m.hT[:, k, t * P:(t + 1) * P], m.dt_w[:, k, :],
                                          start=(k == 0), stop=(k == KD - 1))
            mm.then_inc(dt_done, 1)
            pe.sem_inc(free, 4)
            pe.sem_inc(used, 1)
            with pe.Fori(0, LOOPS) as it:
                for r in range(BODY):
                    pe.wait_ge(w_split, 2 * (BODY * it + r) + 2)
                    for h in range(2):
                        pe.wait_ge(free, 2 * BODY * it + 2 * r + h + 1)
                        b = (2 * r + h) % 4
                        cols = slice(h * HALF, (h + 1) * HALF)
                        for k in range(KD):
                            if r == 0:
                                pe.wait_ge(low_made[k % 2], (h * KD + k) // 2 + 1)
                            mm = split_product(nc, m.ps[b][:, :], (high_w[:, r % 2, k, :], low_w[:, r % RING, k, :]),
                                               (high[:, k, cols], low[:, k, cols]), k == 0, k == KD - 1)
                        mm.then_inc(done, 1)
                    nc.tensor.matmul(m.ps[7][0:1, 0:1], m.ident[:, 0:1], m.ident[:, 0:1], start=True,
                                     stop=True).then_inc(used, 1)

        @block.scalar
        def _(act):
            a = Chain(act, ch["act"])
            act.wait_ge(sized, 1)
            a.link(nc.scalar.activation(mag[:, :, :], mag[:, :, :], ACT.Exp, scale=-1.0))
            nc.scalar.activation(ln[:, :, :], mag[:, :, :], ACT.Ln, bias=1.0).then_inc(logged, 1)
            with act.Fori(0, LOOPS) as it:
                for r in range(BODY):
                    act.wait_ge(pre_free, BODY * it + r + 1)
                    for h in range(2):
                        act.wait_ge(done, 2 * BODY * it + 2 * r + h + 1)
                        nc.scalar.copy(pre[:, r % 2, CONV - 1 + h * HALF:CONV - 1 + (h + 1) * HALF],
                                       m.ps[(2 * r + h) % 4][:, :]).then_inc(free, 1)

        @block.vector
        def _(dve):
            c = Chain(dve, ch["dve"])
            for r in range(2):
                c.link(dve.memset(pre[:, r, 0:CONV - 1], 0.0))
            for n in range(2 * KD):
                h, k = divmod(n, KD)
                cols = slice(h * HALF, (h + 1) * HALF)
                high_part(nc.vector, high[:, k, cols], m.hT[:, k, cols]).then_inc(high_made, 1)
                if n % 2:
                    dve.wait_ge(high_made, n + 1)
                    low_part(nc.vector, low[:, k, cols], m.hT[:, k, cols], high[:, k, cols])\
                        .then_inc(low_made[1], 1)
            dve.wait_ge(dt_done, 1)
            c.link(nc.vector.tensor_tensor(raw[:, :, :], m.ps[6][:, 0:NT * SSM_HEADS].rearrange("p (t h) -> p t h", t=NT),
                                           m.dt_bias[:, :].unsqueeze(1).to_broadcast(per_head), ALU.add))
            nc.vector.scalar_tensor_tensor(out=mag[:, :, :], in0=raw[:, :, :], scalar=-1.0, in1=raw[:, :, :],
                                           op0=ALU.mult, op1=ALU.max).then_inc(sized, 1)
            dve.wait_ge(logged, 1)
            c.link(nc.vector.scalar_tensor_tensor(out=m.dt[:, :, :], in0=raw[:, :, :], scalar=0.0,
                                                  in1=ln[:, :, :], op0=ALU.max, op1=ALU.add))
            c.link(dve.memset(m.adt[:, NT, :], 0.0))
            c.link(nc.vector.tensor_tensor(m.adt[:, 0:NT, :], m.dt[:, :, :],
                                           m.neg_a[:, :].unsqueeze(1).to_broadcast(per_head), ALU.mult))
            dve.sem_inc(pre_free, 2)
            with dve.Fori(0, LOOPS) as it:
                c.enter(it, BODY * (CONV - 1))
                for r in range(BODY):
                    dve.wait_ge(free, 2 * BODY * it + 2 * r + 2 + 4)
                    out = m.xbc[:, BODY * it + r, :]
                    for j in range(CONV):
                        src = pre[:, r % 2, j:j + S]
                        w = m.conv_w[:, j, bass.ds(BODY * it + r, 1)]
                        if j == 0:
                            ins = nc.vector.tensor_scalar(out, src, w, None, ALU.mult)
                        else:
                            ins = nc.vector.scalar_tensor_tensor(out=out, in0=src, scalar=w, in1=out,
                                                                 op0=ALU.mult, op1=ALU.add)
                        if j < CONV - 1:
                            c.link(ins)
                        else:
                            ins.then_inc(pre_free, 1)
                c.leave(LOOPS, BODY * (CONV - 1))


def ssd(nc, m):
    xc = m.sb("ssd_xc", [P, MC, P])
    hc = m.sb("ssd_hc", [P, KD, P])
    adt_c = m.sb("ssd_adt_c", [P, SSM_HEADS])
    xtok = m.sb("ssd_xtok", [P, INNER])
    btok = m.sb("ssd_btok", [P, SSM_G * SSM_N])
    xd, xdd, xskip, y1, zs = (m.sb(f"ssd_{n}", [P, INNER]) for n in ("xd", "xdd", "xskip", "y1", "zs"))
    seg = m.sb("ssd_seg", [P, SSM_HEADS, P])
    state = m.sb("ssd_state", [P, INNER])
    sums = m.sb("ssd_sums", [P, 3, SSM_HEADS])
    exps = m.sb("ssd_exps", [P, 3, SSM_HEADS])
    neg = m.sb("ssd_neg", [P, SSM_HEADS])
    dtin = m.sb("ssd_dtin", [P, SSM_HEADS])
    names = ("xc_ready", "x_turned", "xtok_ready", "xtok_used", "small_done", "cb_done", "sums_ready",
             "exps_ready", "adt_ready", "seg_done", "seg_exp", "mt_ready", "z_done", "z_ready", "hc_ready",
             "yoff_done", "yoff_read", "ydiag_done", "ydiag_read", "dtin_ready",
             "st_done", "st_read", "decayed", "gated")
    q = {n: m.sem(f"ssd_{n}") for n in names}
    ch = m.chains(nc, "ssd")
    CB0 = INNER // P
    HG = SSM_HEADS // SSM_G

    def heads(ap):
        return ap.rearrange("p (h d) -> p h d", d=SSM_P)

    def spread(ap, n):
        return ap.unsqueeze(2).to_broadcast([P, n, SSM_P])

    with nc.Block() as block:
        @block.sync
        def _(sp):
            sp.dma_start(m.wz[:, :, :], m.i["w_in"][0][:, Z0:Z0 + INNER].rearrange("(p k) n -> p k n", k=KD))\
                .then_inc(m.wz_loaded, 16)

        @block.scalar
        def _(act):
            c = Chain(act, ch["act"])
            with act.Fori(0, NT) as i:
                act.wait_ge(q["yoff_done"], i)
                for j in range(MC):
                    nc.scalar.activation(xc[:, j, :], m.xbc[:, j, bass.ds(i * P, P)], ACT.Silu,
                                         bias=m.conv_b[:, j:j + 1]).then_inc(q["xc_ready"], 1)
                act.wait_ge(q["xtok_used"], 3 * i)
                for h in range(2):
                    act.wait_ge(q["x_turned"], 2 * i + h + 1)
                    nc.scalar.copy(xtok[:, h * HALF:(h + 1) * HALF], m.ps[h][:, :]).then_inc(q["xtok_ready"], 1)
                act.wait_ge(q["sums_ready"], i + 1)
                act.wait_ge(q["yoff_read"], 2 * i)
                act.wait_ge(q["decayed"], i)
                nc.scalar.activation(exps[:, :, :], sums[:, :, :], ACT.Exp).then_inc(q["exps_ready"], 1)
                act.wait_ge(q["ydiag_done"], 2 * i)
                for r in range(4):
                    act.wait_ge(q["seg_done"], 4 * i + r + 1)
                    for hh in range(4):
                        h = 4 * r + hh
                        ins = nc.scalar.activation(seg[:, h, :], m.ps[4 + r % 2][:, hh * P:(hh + 1) * P], ACT.Exp,
                                                   bias=neg[:, h:h + 1])
                    ins.then_inc(q["seg_exp"], 1)
                act.wait_ge(q["gated"], i)
                for h in range(2):
                    act.wait_ge(q["z_done"], 2 * i + h + 1)
                    nc.scalar.activation(zs[:, h * HALF:(h + 1) * HALF], m.ps[h][:, :],
                                         ACT.Silu).then_inc(q["z_ready"], 1)

        @block.gpsimd
        def _(pool):
            c = Chain(pool, ch["pool"])
            nc.gpsimd.memset(state[:, :], 0.0).then_inc(q["st_read"], 2)
            with pool.Fori(0, NT) as i:
                pool.wait_ge(q["z_done"], 2 * i)
                nc.gpsimd.tensor_copy(hc[:, :, :], m.hT[:, :, bass.ds(i * P, P)]).then_inc(q["hc_ready"], 1)
                pool.wait_ge(q["xtok_ready"], 2 * i + 2)
                pool.wait_ge(q["gated"], i)
                nc.gpsimd.tensor_tensor(heads(xskip[:, :]), heads(xtok[:, :]), spread(m.d_skip[:, :], SSM_HEADS),
                                        ALU.mult).then_inc(q["xtok_used"], 1)
                pool.wait_ge(q["dtin_ready"], i + 1)
                pool.wait_ge(q["st_done"], 2 * i)
                nc.gpsimd.tensor_tensor(heads(xdd[:, :]), heads(xtok[:, :]), spread(dtin[:, :], SSM_HEADS),
                                        ALU.mult).then_inc(q["xtok_used"], 1)
                pool.wait_ge(q["yoff_done"], i + 1)
                nc.gpsimd.tensor_tensor(heads(state[:, :]), heads(state[:, :]),
                                        spread(exps[:, 1, :], SSM_HEADS), ALU.mult).then_inc(q["decayed"], 1)

        @block.vector
        def _(dve):
            c = Chain(dve, ch["dve"])
            PER = 4
            def next_adt(i):
                nc.vector.tensor_copy(adt_c[:, :], m.adt[:, bass.ds(i, 1), :].rearrange("p a h -> p (a h)"))\
                    .then_inc(q["adt_ready"], 1)

            next_adt(0)
            with dve.Fori(0, NT) as i:
                c.enter(i, PER)
                dve.wait_ge(q["small_done"], i + 1)
                dve.wait_ge(q["st_done"], 2 * i)
                c.link(nc.vector.tensor_copy(btok[:, :], m.ps[2][:, 0:256]))
                c.link(nc.vector.tensor_copy(sums[:, 0:2, :], m.ps[2][:, 256:288].rearrange("p (a h) -> p a h", a=2)))
                c.link(nc.vector.tensor_scalar(neg[:, :], sums[:, 0, :], -1.0, None, ALU.mult))
                nc.vector.tensor_tensor(sums[:, 2, :], sums[:, 1, :], sums[:, 0, :],
                                        ALU.subtract).then_inc(q["sums_ready"], 1)
                dve.wait_ge(q["exps_ready"], i + 1)
                dt_c = m.dt[:, bass.ds(i, 1), :].rearrange("p a h -> p (a h)")
                dve.wait_ge(q["xtok_used"], 3 * i + 1)
                nc.vector.tensor_tensor(dtin[:, :], dt_c, exps[:, 2, :], ALU.mult).then_inc(q["dtin_ready"], 1)
                dve.wait_ge(q["xtok_ready"], 2 * i + 2)
                dve.wait_ge(q["ydiag_done"], 2 * i)
                nc.vector.tensor_tensor(heads(xd[:, :]), heads(xtok[:, :]), spread(dt_c, SSM_HEADS),
                                        ALU.mult).then_inc(q["xtok_used"], 1)
                dve.wait_ge(q["cb_done"], i + 1)
                for r in range(4):
                    g = r // 2
                    dve.wait_ge(q["seg_exp"], 4 * i + r + 1)
                    part = seg[:, 4 * r:4 * r + 4, :]
                    nc.vector.tensor_tensor(part, part, m.ps[3][:, g * P:(g + 1) * P].unsqueeze(1)
                                            .to_broadcast([P, 4, P]), ALU.mult).then_inc(q["mt_ready"], 1)
                dve.wait_ge(q["seg_done"], 4 * i + 4)
                next_adt(i + 1)
                for g in range(2):
                    part = slice(g * HALF, (g + 1) * HALF)
                    dve.wait_ge(q["yoff_done"], i + 1)
                    ins = nc.vector.tensor_tensor(heads(y1[:, part]), heads(m.ps[6 + g][:, :]),
                                                  spread(exps[:, 0, g * HG:(g + 1) * HG], HG), ALU.mult)
                    ins.then_inc(q["yoff_read"], 1)
                dve.wait_ge(q["decayed"], i + 1)
                for g in range(2):
                    part = slice(g * HALF, (g + 1) * HALF)
                    dve.wait_ge(q["st_done"], 2 * i + g + 1)
                    nc.vector.tensor_tensor(state[:, part], state[:, part], m.ps[2 + g][:, :],
                                            ALU.add).then_inc(q["st_read"], 1)
                dve.wait_ge(q["yoff_read"], 2 * i + 2)
                dve.wait_ge(q["xtok_used"], 3 * i + 3)
                c.link(nc.vector.tensor_tensor(y1[:, :], y1[:, :], xskip[:, :], ALU.add))
                for g in range(2):
                    part = slice(g * HALF, (g + 1) * HALF)
                    dve.wait_ge(q["ydiag_done"], 2 * i + g + 1)
                    nc.vector.tensor_tensor(y1[:, part], y1[:, part], m.ps[4 + g][:, :],
                                            ALU.add).then_inc(q["ydiag_read"], 1)
                dve.wait_ge(q["ydiag_read"], 2 * i + 2)
                dve.wait_ge(q["z_ready"], 2 * i + 2)
                nc.vector.tensor_tensor(m.y[:, bass.ds(i, 1), :].rearrange("p a n -> p (a n)"), y1[:, :], zs[:, :],
                                        ALU.mult).then_inc(q["gated"], 1)
                c.leave(NT, PER)

        @block.tensor
        def _(pe):
            with pe.Fori(0, NT) as i:
                pe.wait_ge(q["z_ready"], 2 * i)
                for h in range(2):
                    pe.wait_ge(q["xc_ready"], MC * i + 4 * h + 4)
                    for j in range(4):
                        mm = nc.tensor.transpose(m.ps[h][:, j * P:(j + 1) * P], xc[:, 4 * h + j, :], m.ident[:, :])
                    mm.then_inc(q["x_turned"], 1)
                pe.wait_ge(q["st_read"], 2 * i + 2)
                pe.wait_ge(q["xc_ready"], MC * i + MC)
                for g in range(SSM_G):
                    nc.tensor.transpose(m.ps[2][:, g * P:(g + 1) * P], xc[:, CB0 + g, :], m.ident[:, :])
                pe.wait_ge(q["adt_ready"], i + 1)
                nc.tensor.matmul(m.ps[2][:, 256:272], m.tri_le[:, :], adt_c[:, :], start=True, stop=True)
                nc.tensor.matmul(m.ps[2][:, 272:288], m.ones[:, :], adt_c[:, :], start=True,
                                 stop=True).then_inc(q["small_done"], 1)
                for g in range(SSM_G):
                    mm = nc.tensor.matmul(m.ps[3][:, g * P:(g + 1) * P], xc[:, CB0 + g, :], xc[:, CB0 + 2 + g, :],
                                          start=True, stop=True)
                mm.then_inc(q["cb_done"], 1)
                for r in range(4):
                    if r < 2:
                        pe.wait_ge(q["ydiag_read"], 2 * i)
                    else:
                        pe.wait_ge(q["seg_exp"], 4 * i + r - 1)
                    bank = m.ps[4 + r % 2]
                    nc.tensor.matmul(bank[:, :].rearrange("p (h l) -> p h l", l=P), m.identb[:, :],
                                     m.mask_past[:, :].unsqueeze(1).to_broadcast([P, 4, P]), start=True, stop=False)
                    for hh in range(4):
                        h = 4 * r + hh
                        mm = nc.tensor.matmul(bank[:, hh * P:(hh + 1) * P], adt_c[:, h:h + 1].to_broadcast([P, P]),
                                              m.tri_le[:, :], start=False, stop=(hh == 3))
                    mm.then_inc(q["seg_done"], 1)
                pe.wait_ge(q["hc_ready"], i + 1)
                pe.wait_ge(m.wz_loaded, 16)
                for h in range(2):
                    pe.wait_ge(q["xtok_ready"], 2 * i + h + 1)
                    for k in range(KD):
                        mm = nc.tensor.matmul(m.ps[h][:, :], hc[:, k, :], m.wz[:, k, h * HALF:(h + 1) * HALF],
                                              start=(k == 0), stop=(k == KD - 1))
                    mm.then_inc(q["z_done"], 1)
                pe.wait_ge(q["yoff_read"], 2 * i)
                for g in range(SSM_G):
                    mm = nc.tensor.matmul(m.ps[6 + g][:, :], xc[:, CB0 + 2 + g, :],
                                          state[:, g * HALF:(g + 1) * HALF], start=True, stop=True)
                mm.then_inc(q["yoff_done"], 1)
                pe.wait_ge(q["xtok_used"], 3 * i + 3)
                pe.wait_ge(q["mt_ready"], 4 * i + 4)
                for g in range(SSM_G):
                    nc.tensor.matmul(m.ps[2 + g][:, :], btok[:, g * P:(g + 1) * P], xdd[:, g * HALF:(g + 1) * HALF],
                                     start=True, stop=True).then_inc(q["st_done"], 1)
                for h in range(SSM_HEADS):
                    mm = nc.tensor.matmul(m.ps[4 + h // HG][:, (h % HG) * SSM_P:(h % HG + 1) * SSM_P], seg[:, h, :],
                                          xd[:, h * SSM_P:(h + 1) * SSM_P], start=True, stop=True)
                    if h % HG == HG - 1:
                        mm.then_inc(q["ydiag_done"], 1)


def group_norm(nc, m, ybT):
    squared, mean, root, normed, turned = (m.sem(f"gn_{n}") for n in
                                           ("squared", "mean_made", "rooted", "normed", "turned"))
    read = [m.sem("gn_act_read"), m.sem("gn_dve_read")]
    ch = m.chains(nc, "gn")
    ss = m.sb("gn_ss", [P, NT * SSM_G])
    rs = m.sb("gn_rs", [P, NT * SSM_G])
    NG = 2 * KD
    with nc.Block() as block:
        @block.sync
        def _(sp):
            sp.dma_start(m.nsa_w[:, :, :], m.i["w_in"][0][:, 0:NSA_W].rearrange("(p k) n -> p k n", k=KD))\
                .then_inc(m.nsa_w_loaded, 16)

        @block.gpsimd
        def _(pool):
            for b in range(2):
                nc.gpsimd.tensor_copy(m.nsa_hc[:, b, :, :], m.hT[:, :, b * P:(b + 1) * P])\
                    .then_inc(m.nsa_hc_ready, 1)

        @block.scalar
        def _(act):
            def square(t):
                for g in range(SSM_G):
                    n = SSM_G * t + g
                    if n >= 2:
                        act.wait_ge(squared, n - 1)
                    nc.scalar.activation(m.junk[:, g, 0:GW], m.y[:, t, g * GW:(g + 1) * GW], ACT.Square,
                                         accum_out=ss[:, n:n + 1]).then_inc(squared, 1)

            def rooted(t):
                act.wait_ge(mean, t + 1)
                part = ss[:, SSM_G * t:SSM_G * (t + 1)]
                nc.scalar.activation(part, part, ACT.Sqrt).then_inc(root, 1)

            square(0)
            for t in range(NT):
                if t + 1 < NT:
                    square(t + 1)
                rooted(t)
            for n in range(0, NG, 2):
                act.wait_ge(turned, n + 1)
                k, h = n % KD, n // KD
                nc.scalar.activation(ybT[:, k, h * HALF:(h + 1) * HALF], m.ps[n % 4][:, :], ACT.Copy,
                                     scale=m.ssm_gain[:, k:k + 1]).then_inc(read[0], 1)

        @block.vector
        def _(dve):
            c = Chain(dve, ch["dve"])

            def means(t):
                dve.wait_ge(squared, SSM_G * (t + 1))
                part = ss[:, SSM_G * t:SSM_G * (t + 1)]
                nc.vector.tensor_scalar(part, part, 1.0 / GW, EPS, ALU.mult, ALU.add).then_inc(mean, 1)

            means(0)
            for t in range(NT):
                if t + 1 < NT:
                    means(t + 1)
                dve.wait_ge(root, t + 1)
                tile = slice(SSM_G * t, SSM_G * (t + 1))
                c.link(nc.vector.reciprocal(rs[:, tile], ss[:, tile]))
                part = m.y[:, t, :].rearrange("p (g n) -> p g n", g=SSM_G)
                nc.vector.tensor_tensor(part, part, rs[:, tile].unsqueeze(2).to_broadcast([P, SSM_G, GW]),
                                        ALU.mult).then_inc(normed, 1)
            for n in range(1, NG, 2):
                dve.wait_ge(turned, n + 1)
                k, h = n % KD, n // KD
                nc.vector.tensor_scalar(ybT[:, k, h * HALF:(h + 1) * HALF], m.ps[n % 4][:, :],
                                        m.ssm_gain[:, k:k + 1], None, ALU.mult).then_inc(read[1], 1)

        @block.tensor
        def _(pe):
            for n in range(NG):
                k, h = n % KD, n // KD
                pe.wait_ge(normed, 4 * (h + 1))
                if n >= 4:
                    pe.wait_ge(read[n % 2], (n - 4) // 2 + 1)
                for j in range(4):
                    mm = nc.tensor.transpose(m.ps[n % 4][:, j * P:(j + 1) * P], m.y[:, 4 * h + j, k:D:KD],
                                             m.ident[:, :])
                mm.then_inc(turned, 1)


def nsa_project(nc, m):
    W = m.nsa_w
    hc = m.nsa_hc
    NH = HEADS + 2 * GROUPS
    nb = m.sb("nsa_norm_in", [P, 2, NH, HD])
    cv = m.sb("nsa_cmp_in", [P, 2, 2 * KV_W])
    sq = m.sb("nsa_sq", [P, NH, HD])
    ss, rs = m.sb("nsa_ss", [P, NH]), m.sb("nsa_rs", [P, NH])
    q = {n: m.sem(f"nsa_{n}") for n in ("proj_done", "copied", "squared", "mean", "rooted",
                                        "normed", "turned", "spread", "ones", "gates")}
    ch = m.chains(nc, "nsa")
    LOOPS = NT // 2
    KS0, KW0 = HEADS * HD, HEADS * HD + KV_W
    nbf = nb[:, :, :, :].rearrange("p b h d -> p b (h d)")
    with nc.Block() as block:
        @block.sync
        def _(sp):
            load_compress(m, sp)

        @block.gpsimd
        def _(pool):
            nc.gpsimd.memset(m.v_sel[:, :, :, HD:HD + 1], 1.0).then_inc(q["ones"], 1)
            nc.gpsimd.memset(m.v_win[:, :, :, HD:HD + 1], 1.0).then_inc(q["ones"], 1)
            with pool.Fori(0, LOOPS - 1) as i:
                for b in range(2):
                    pool.wait_ge(q["proj_done"], 3 * (2 * i + b) + 3)
                    nc.gpsimd.tensor_copy(hc[:, b, :, :], m.hT[:, :, bass.ds((2 * i + b + 2) * P, P)])\
                        .then_inc(m.nsa_hc_ready, 1)

        @block.tensor
        def _(pe):
            def project(t, b):
                pe.wait_ge(m.nsa_hc_ready, t + 1)
                pe.wait_ge(q["copied"], 6 * t)
                for n in range(3):
                    c0, c1 = n * HALF, min((n + 1) * HALF, NSA_W)
                    for k in range(KD):
                        mm = nc.tensor.matmul(m.ps[n][:, 0:c1 - c0], hc[:, b, k, :], W[:, k, c0:c1],
                                              start=(k == 0), stop=(k == KD - 1))
                    mm.then_inc(q["proj_done"], 1)

            def turn(t, b):
                pe.wait_ge(q["spread"], 4 * t)
                pe.wait_ge(q["normed"], t + 1)
                for n in range(E + 2):
                    nc.tensor.transpose(m.ps[3 + n // 4][:, n % 4 * P:(n % 4 + 1) * P],
                                        nbf[:, b, n * P:(n + 1) * P], m.ident[:, :])
                for n in range(2):
                    mm = nc.tensor.transpose(m.ps[4][:, (2 + n) * P:(3 + n) * P], cv[:, b, n * P:(n + 1) * P],
                                             m.ident[:, :])
                mm.then_inc(q["turned"], 1)

            pe.sem_inc(q["turned"], 1)
            pe.wait_ge(m.nsa_w_loaded, 16)
            project(0, 0)
            with pe.Fori(0, LOOPS - 1) as i:
                project(2 * i + 1, 1)
                turn(2 * i, 0)
                project(2 * i + 2, 0)
                turn(2 * i + 1, 1)
            project(NT - 1, 1)
            turn(NT - 2, 0)
            turn(NT - 1, 1)

        @block.scalar
        def _(act):
            act.wait_ge(q["ones"], 2)
            c = Chain(act, ch["act"])
            with act.Fori(0, LOOPS) as i:
                c.enter(i, 2)
                for b in range(2):
                    t = 2 * i + b
                    act.wait_ge(q["turned"], t)
                    act.wait_ge(q["proj_done"], 3 * t + 1)
                    nc.scalar.copy(nb[:, b, 0:HEADS, :].rearrange("p (e g) d -> p g e d", g=GROUPS),
                                   m.ps[0][:, :].rearrange("p (g e d) -> p g e d", g=GROUPS, e=E))\
                        .then_inc(q["copied"], 1)
                    act.wait_ge(q["proj_done"], 3 * t + 2)
                    nc.scalar.copy(cv[:, b, :], m.ps[1][:, 0:2 * KV_W]).then_inc(q["copied"], 1)
                    nc.scalar.copy(nbf[:, b, KS0:KS0 + KV_W], m.ps[1][:, 2 * KV_W:3 * KV_W]).then_inc(q["copied"], 1)
                    nc.scalar.copy(m.v_sel[:, bass.ds(t, 1), :, 0:HD].rearrange("p a g d -> p (a g) d"),
                                   m.ps[1][:, 3 * KV_W:4 * KV_W].rearrange("p (g d) -> p g d", d=HD))\
                        .then_inc(q["copied"], 1)
                    act.wait_ge(q["proj_done"], 3 * t + 3)
                    nc.scalar.copy(nbf[:, b, KW0:KW0 + KV_W], m.ps[2][:, 0:KV_W]).then_inc(q["copied"], 1)
                    nc.scalar.copy(m.v_win[:, bass.ds(t, 1), :, 0:HD].rearrange("p a g d -> p (a g) d"),
                                   m.ps[2][:, KV_W:2 * KV_W].rearrange("p (g d) -> p g d", d=HD))
                    c.link(nc.scalar.copy(m.gate_scale[:, bass.ds(t, 1), :].rearrange("p a g -> p (a g)"),
                                          m.ps[2][:, 2 * KV_W:2 * KV_W + GATE_W]))
                    nc.scalar.copy(m.junk[:, 0, 0:1], m.ones[:, 0:1]).then_inc(q["copied"], 1)
                    act.wait_ge(q["copied"], 6 * t + 6)
                    nc.scalar.activation(sq[:, :, :], nb[:, b, :, :], ACT.Square).then_inc(q["squared"], 1)
                    act.wait_ge(q["mean"], t + 1)
                    nc.scalar.activation(ss[:, :], ss[:, :], ACT.Sqrt).then_inc(q["rooted"], 1)
                c.leave(LOOPS, 2)
            g = m.gate_scale[:, :, :].rearrange("p t n -> p (t n)")
            nc.scalar.activation(g, g, ACT.Sigmoid).then_inc(q["gates"], 1)

        @block.vector
        def _(dve):
            c = Chain(dve, ch["dve"])
            PER = 2 * 2
            with dve.Fori(0, LOOPS) as i:
                c.enter(i, PER)
                for b in range(2):
                    t = 2 * i + b
                    cols = bass.ds(t * P, P)
                    dve.wait_ge(q["squared"], t + 1)
                    c.link(nc.vector.tensor_reduce(ss[:, :], sq[:, :, :], axis=AX.X, op=ALU.add))
                    nc.vector.tensor_scalar(ss[:, :], ss[:, :], 1.0 / HD, EPS, ALU.mult, ALU.add)\
                        .then_inc(q["mean"], 1)
                    dve.wait_ge(q["rooted"], t + 1)
                    c.link(nc.vector.reciprocal(rs[:, :], ss[:, :]))
                    nc.vector.tensor_tensor(nb[:, b, :, :], nb[:, b, :, :],
                                            rs[:, :].unsqueeze(2).to_broadcast([P, NH, HD]), ALU.mult)\
                        .then_inc(q["normed"], 1)
                    dve.wait_ge(q["turned"], t + 2)
                    nc.vector.tensor_scalar(m.qT[:, :, cols], m.ps[3][:, :].rearrange("p (e q) -> p e q", e=E),
                                            m.qk_gain[:, 0:1], None, ALU.mult).then_inc(q["spread"], 1)
                    nc.vector.tensor_scalar(m.ksT[:, cols], m.ps[4][:, 0:P], m.qk_gain[:, 2:3], None,
                                            ALU.mult).then_inc(q["spread"], 1)
                    nc.vector.tensor_scalar(m.kwT[:, cols], m.ps[4][:, P:2 * P], m.qk_gain[:, 3:4], None,
                                            ALU.mult).then_inc(q["spread"], 1)
                    nc.vector.tensor_copy(m.cT[:, :, cols], m.ps[4][:, 2 * P:].rearrange("p (a q) -> p a q", a=2))\
                        .then_inc(q["spread"], 1)
                c.leave(LOOPS, PER)
            dve.wait_ge(q["gates"], 1)
            first = m.gate_scale[:, 0, 0:GATE_W:3]
            c.link(nc.vector.tensor_scalar(first, first, m.any_cmp[:, 0:1], None, ALU.mult))


def load_compress(m, eng):
    W1, W2, pos = m.cmp_w
    for n, kv in enumerate("kv"):
        eng.dma_start(pos[:, n, :], m.i[f"cmp_pos_{kv}"][0].rearrange("(j a) d -> j (a d)", a=2))\
            .then_inc(m.cmp_loaded, 16)
        for part in range(2):
            js = slice(part * CMP_BLOCK // 4, (part + 1) * CMP_BLOCK // 4)
            eng.dma_start(W1[:, n, js, :], m.i[f"cmp_w1_{kv}"][0].rearrange("(j p) h -> p j h", p=P)[:, js, :])\
                .then_inc(m.cmp_loaded, 16)
        eng.dma_start(W2[:, n, :], m.i[f"cmp_w2_{kv}"][0]).then_inc(m.cmp_loaded, 16)


def compress(nc, m):
    JP = CMP_BLOCK // 2
    W1, W2, pos = m.cmp_w
    pairs = m.sb("cmp_pairs", [P, 2, GROUPS, S])
    posT = m.sb("cmp_posT", [P, 2, JP])
    bias = m.sb("cmp_bias", [P, 2])
    hid = m.sb("cmp_hid", [P, 2, GROUPS, NCMP])
    kc = m.sb("cmp_k", [NCMP, GROUPS, HD])
    sq = m.sb("cmp_sq", [NCMP, GROUPS, HD])
    ss, rs = m.sb("cmp_ss", [NCMP, GROUPS]), m.sb("cmp_rs", [NCMP, GROUPS])
    q = {n: m.sem(f"cmp_{n}") for n in ("paired", "pos_turned", "pos_ready", "bias_done", "bias_ready", "hid_done",
                                        "hid_ready", "kv_done", "squared", "mean", "rooted", "normed", "k_turned",
                                        "ones")}
    ch = m.chains(nc, "cmp")
    with nc.Block() as block:
        @block.sync
        def _(sp):
            for n in range(2):
                for g in range(GROUPS):
                    own = slice(g * HD, (g + 1) * HD)
                    sp.dma_start(pairs[0:HD, n, g, :], m.cT[own, n, :]).then_inc(q["paired"], 16)
                    sp.dma_start(pairs[HD:P, n, g, 0:S - 1], m.cT[own, n, 1:S]).then_inc(q["paired"], 16)

        @block.tensor
        def _(pe):
            pe.wait_ge(m.cmp_loaded, 16 * 2 * 4)
            for n in range(2):
                mm = nc.tensor.transpose(m.ps[0][:, n * JP:(n + 1) * JP], pos[:, n, :], m.ident[0:JP, 0:JP])
            mm.then_inc(q["pos_turned"], 1)
            pe.wait_ge(q["pos_ready"], 1)
            for n in range(2):
                for j in range(JP):
                    mm = nc.tensor.matmul(m.ps[1][:, n:n + 1], W1[:, n, j, :], posT[:, n, j:j + 1],
                                          start=(j == 0), stop=(j == JP - 1))
            mm.then_inc(q["bias_done"], 1)
            pe.wait_ge(q["paired"], 16 * 4 * GROUPS)
            for n in range(2):
                dst = m.ps[2 + n][:, 0:GROUPS * NCMP].rearrange("h (g c) -> h g c", g=GROUPS)
                for j in range(JP):
                    last = CMP_STRIDE * (NCMP - 1) + 2 * j + 1
                    mm = nc.tensor.matmul(dst, W1[:, n, j, :], pairs[:, n, :, 2 * j:last:CMP_STRIDE],
                                          start=(j == 0), stop=(j == JP - 1))
                mm.then_inc(q["hid_done"], 1)
            pe.wait_ge(q["hid_ready"], 2)
            for n in range(2):
                for g in range(GROUPS):
                    mm = nc.tensor.matmul(m.ps[4][0:NCMP, (2 * n + g) * HD:(2 * n + g + 1) * HD], hid[:, n, g, :],
                                          W2[:, n, :], start=True, stop=True)
            mm.then_inc(q["kv_done"], 1)
            pe.wait_ge(q["normed"], 1)
            nc.tensor.transpose(m.ps[5][:, 0:NCMP], kc[:, :, :].rearrange("c g d -> c (g d)"),
                                m.ident[0:NCMP, 0:NCMP]).then_inc(q["k_turned"], 1)

        @block.scalar
        def _(act):
            act.wait_ge(q["bias_ready"], 1)
            for n in range(2):
                act.wait_ge(q["hid_done"], n + 1)
                nc.scalar.activation(hid[:, n, :, :], m.ps[2 + n][:, 0:GROUPS * NCMP]
                                     .rearrange("h (g c) -> h g c", g=GROUPS), ACT.Silu,
                                     bias=bias[:, n:n + 1]).then_inc(q["hid_ready"], 1)
            act.wait_ge(q["kv_done"], 1)
            nc.scalar.activation(sq[:, :, :], m.ps[4][0:NCMP, 0:2 * HD].rearrange("c (g d) -> c g d", d=HD),
                                 ACT.Square).then_inc(q["squared"], 1)
            act.wait_ge(q["mean"], 1)
            nc.scalar.activation(ss[:, :], ss[:, :], ACT.Sqrt).then_inc(q["rooted"], 1)

        @block.gpsimd
        def _(pool):
            nc.gpsimd.memset(m.v_cmp[:, :, HD:HD + 1], 1.0).then_inc(q["ones"], 1)

        @block.vector
        def _(dve):
            c = Chain(dve, ch["dve"])
            dve.wait_ge(q["pos_turned"], 1)
            nc.vector.tensor_copy(posT[:, :, :], m.ps[0][:, 0:2 * JP].rearrange("p (n j) -> p n j", n=2))\
                .then_inc(q["pos_ready"], 1)
            dve.wait_ge(q["bias_done"], 1)
            nc.vector.tensor_copy(bias[:, :], m.ps[1][:, 0:2]).then_inc(q["bias_ready"], 1)
            dve.wait_ge(q["squared"], 1)
            c.link(nc.vector.tensor_reduce(ss[:, :], sq[:, :, :], axis=AX.X, op=ALU.add))
            nc.vector.tensor_scalar(ss[:, :], ss[:, :], 1.0 / HD, EPS, ALU.mult, ALU.add).then_inc(q["mean"], 1)
            dve.wait_ge(q["ones"], 1)
            kv = m.ps[4][0:NCMP, 0:4 * HD].rearrange("c (n g d) -> c n g d", n=2, g=GROUPS)
            c.link(nc.vector.tensor_copy(m.v_cmp[:, :, 0:HD], kv[:, 1, :, :]))
            dve.wait_ge(q["rooted"], 1)
            c.link(nc.vector.reciprocal(rs[:, :], ss[:, :]))
            nc.vector.tensor_tensor(kc[:, :, :], kv[:, 0, :, :], rs[:, :].unsqueeze(2).to_broadcast([NCMP, GROUPS, HD]),
                                    ALU.mult).then_inc(q["normed"], 1)
            dve.wait_ge(q["k_turned"], 1)
            c.link(nc.vector.tensor_scalar(m.kcT[:, :], m.ps[5][:, 0:NCMP], m.qk_gain[:, 1:2], None, ALU.mult))


def attention(nc, m):
    qz = m.sb("att_q", [P, GROUPS, S])
    prob = m.sb("att_prob", [P, 2, S])
    probT = m.sb("att_probT", [P, 2, S])
    nmax = m.sb("att_nmax", [P, 2, 2])
    rec = m.sb("att_rec", [P, 2, 3])
    acc = m.sb("att_acc", [P, 2, 2, HD])
    names = ("row_zeroed", "rows_cleared", "zeroed", "q_ready", "scored", "maxed", "exped", "turned", "act_copied",
             "dve_copied", "summed", "mixed")
    q = {n: m.sem(f"att_{n}") for n in names}
    copied = [q["act_copied"], q["dve_copied"]]
    ch = m.chains(nc, "att")
    WT = WINDOW // P
    CMP0 = (WT + 1) * P
    TURN = HALF // P
    units = [(i, g, kind) for i in range(NT) for g in range(GROUPS) for kind in ("sel", "win")]
    U = len(units)

    def pair(u):
        return m.psum[:, 2 * HALF * (u % 2):2 * HALF * (u % 2 + 1)]

    def tiles(u):
        i, _, kind = units[u]
        return range(0 if kind == "sel" else max(0, i - WT), i + 1)

    def pieces(u):
        at = [x * P for x in range(len(tiles(u)))] + ([CMP0] if units[u][2] == "win" else [])
        return [at[x:x + TURN] for x in range(0, len(at), TURN)]

    start = [0]
    for u in range(U):
        start.append(start[-1] + len(pieces(u)))
    TURNS = start[-1]
    assert TURNS % 2 == 0

    def at(e, u):
        return (e, u) if u < U else (e + 1, u - U)

    def wait_past(eng, sem, n):
        if not isinstance(n, int) or n > 0:
            eng.wait_ge(sem, n)

    def wait_turns(eng, e, n):
        eng.wait_ge(copied[0], TURNS // 2 * e + (n + 1) // 2)
        eng.wait_ge(copied[1], TURNS // 2 * e + n // 2)

    def copies(eng, which, e, u):
        for x, at in enumerate(pieces(u)):
            n = start[u] + x
            if n % 2 == which:
                if x < 2:
                    wait_past(eng, q["summed"], U * e + u - 1)
                eng.wait_ge(q["turned"], TURNS * e + n + 1)
                dst = probT[:, u % 2, x * HALF:x * HALF + len(at) * P]
                src = m.ps[4 + n % 2][:, 0:len(at) * P]
                ins = nc.scalar.copy(dst, src) if which == 0 else nc.vector.tensor_copy(dst, src)
                ins.then_inc(copied[which], 1)

    with nc.Block() as block:
        @block.gpsimd
        def _(pool):
            nc.gpsimd.memset(m.junk[:, 0, :], 0.0).then_inc(q["row_zeroed"], 1)
            pool.wait_ge(q["row_zeroed"], 1)
            for g in range(GROUPS):
                other = slice((1 - g) * HD, (2 - g) * HD)
                nc.gpsimd.memset(qz[other, g, :], 0.0).then_inc(q["zeroed"], 1)
            pool.wait_ge(q["zeroed"], 2)
            nc.gpsimd.memset(prob[:, :, CMP0:CMP0 + P], 0.0).then_inc(q["zeroed"], 1)
            pool.wait_ge(q["zeroed"], 3)
            def q_tile(e, i, g):
                own = slice(g * HD, (g + 1) * HD)
                cols = slice(i * P, (i + 1) * P)
                nc.gpsimd.tensor_copy(qz[own, g, cols], m.qT[own, bass.ds(e, 1), cols].rearrange("p a q -> p (a q)"))\
                    .then_inc(q["q_ready"], 1)

            for i in range(NT):
                for g in range(GROUPS):
                    q_tile(0, i, g)
            with pool.Fori(0, E - 1) as e:
                for i in range(NT):
                    for g in range(GROUPS):
                        pool.wait_ge(q["scored"], U * e + 2 * (GROUPS * i + g) + 2)
                        q_tile(e + 1, i, g)

        @block.sync
        def _(sp):
            sp.wait_ge(q["row_zeroed"], 1)
            for b in range(EXPERTS, BLOCKS):
                sp.dma_start(m.y_slots[b * P:(b + 1) * P, :], m.junk[:, 0, :]).then_inc(q["rows_cleared"], 16)
            sp.wait_ge(q["rows_cleared"], 16 * EXTRA)
            for part in range(len(m.merge_w)):
                load_merge(m, sp, part, 0)

        @block.tensor
        def _(pe):
            pe.wait_ge(q["zeroed"], 3)

            def scores(e, u):
                i, g, kind = units[u]
                ps = pair(u)
                wait_past(pe, q["exped"], U * e + u - 1)
                if kind == "sel":
                    pe.wait_ge(q["q_ready"], GROUPS * (NT * e + i) + g + 1)
                keys = m.ksT if kind == "sel" else m.kwT
                qs = qz[:, g, i * P:(i + 1) * P]
                k0, n = tiles(u)[0] * P, len(tiles(u)) * P
                for c0 in range(0, n, HALF):
                    c1 = min(c0 + HALF, n)
                    masks = []
                    if c1 == n:
                        masks.append((n - P, m.mask_future))
                    if kind == "win" and i >= WT and c0 == 0:
                        masks.append((0, m.mask_far))
                    mm = nc.tensor.matmul(ps[:, c0:c1], qs, keys[:, k0 + c0:k0 + c1], start=True, stop=not masks)
                    for x, (at, mask) in enumerate(masks):
                        mm = nc.tensor.matmul(ps[:, at:at + P], m.identb[:, :], mask[:, :], start=False,
                                              stop=(x == len(masks) - 1))
                if kind == "win":
                    nc.tensor.matmul(ps[:, CMP0:CMP0 + NCMP], qs, m.kcT[:, :], start=True, stop=False)
                    mm = nc.tensor.matmul(ps[:, CMP0:CMP0 + NCMP], m.identb[:, :], m.mask_cmp[:, i, 0:NCMP],
                                          start=False, stop=True)
                mm.then_inc(q["scored"], 1)

            def turn(e, u):
                pe.wait_ge(q["exped"], U * e + u + 1)
                for x, at in enumerate(pieces(u)):
                    n = start[u] + x
                    wait_past(pe, copied[n % 2], TURNS // 2 * e + n // 2)
                    for y, c in enumerate(at):
                        mm = nc.tensor.transpose(m.ps[4 + n % 2][:, y * P:(y + 1) * P], prob[:, u % 2, c:c + P],
                                                 m.ident[:, :])
                    mm.then_inc(q["turned"], 1)

            def sums(e, u):
                i, g, kind = units[u]
                dst, pt = m.ps[6 + (u // 2) % 2], probT[:, u % 2, :]
                if kind == "sel":
                    pe.wait_ge(q["mixed"], U // 2 * e + u // 2)
                wait_turns(pe, e, start[u + 1])
                v, at = (m.v_sel, HD + 1) if kind == "sel" else (m.v_win, 2 * (HD + 1))
                ts = tiles(u)
                for x, t in enumerate(ts):
                    mm = nc.tensor.matmul(dst[:, at:at + HD + 1], pt[:, x * P:(x + 1) * P], v[:, t, g, :],
                                          start=(x == 0), stop=(x == len(ts) - 1))
                if kind == "win":
                    mm = nc.tensor.matmul(dst[:, 0:HD + 1], pt[0:NCMP, len(ts) * P:(len(ts) + 1) * P],
                                          m.v_cmp[:, g, :], start=True, stop=True)
                mm.then_inc(q["summed"], 1)

            def one_pass(e, last):
                for u in range(2, U + 2):
                    if u < U or not last:
                        scores(*at(e, u))
                    sums(e, u - 2)
                    if u - 1 < U or not last:
                        turn(*at(e, u - 1))

            scores(0, 0)
            scores(0, 1)
            turn(0, 0)
            with pe.Fori(0, E - 1) as e:
                one_pass(e, False)
            one_pass(E - 1, True)

        @block.scalar
        def _(act):
            def exponentials(e, u, before):
                ps, pr, nm = pair(u), prob[:, u % 2, :], nmax[:, u % 2, :]
                n = len(tiles(u)) * P
                act.wait_ge(q["maxed"], U * e + u + 1)
                wait_past(act, q["turned"], before)
                ins = nc.scalar.activation(pr[:, 0:n], ps[:, 0:n], ACT.Exp, bias=nm[:, 0:1])
                if units[u][2] == "win":
                    ins = nc.scalar.activation(pr[:, CMP0:CMP0 + NCMP], ps[:, CMP0:CMP0 + NCMP], ACT.Exp,
                                               bias=nm[:, 1:2])
                ins.then_inc(q["exped"], 1)

            def one_pass(e, last):
                for u in range(2, U + 2):
                    if u < U or not last:
                        exponentials(*at(e, u), TURNS * e + start[u - 1])
                    if u - 1 < U or not last:
                        copies(act, 0, *at(e, u - 1))

            exponentials(0, 0, 0)
            exponentials(0, 1, 0)
            copies(act, 0, 0, 0)
            with act.Fori(0, E - 1) as e:
                one_pass(e, False)
            one_pass(E - 1, True)

        @block.vector
        def _(dve):
            c = Chain(dve, ch["dve"])
            PER = (U // 2) * 4

            dve.sem_inc(q["mixed"], 1)

            def maxima(e, u):
                ps, nm = pair(u), nmax[:, u % 2, :]
                n = len(tiles(u)) * P
                dve.wait_ge(q["scored"], U * e + u + 1)
                ins = nc.vector.tensor_reduce(nm[:, 0:1], ps[:, 0:n], axis=AX.X, op=ALU.max, negate=True)
                if units[u][2] == "win":
                    ins = nc.vector.tensor_reduce(nm[:, 1:2], ps[:, CMP0:CMP0 + NCMP], axis=AX.X, op=ALU.max,
                                                  negate=True)
                ins.then_inc(q["maxed"], 1)

            def mix(e, w):
                i, g, _ = units[2 * w]
                o = m.ps[6 + w % 2][:, 0:3 * (HD + 1)].rearrange("p (b d) -> p b d", b=3)
                r, a = rec[:, w % 2, :], acc[:, w % 2, :, :]
                head = g * E + e
                dve.wait_ge(q["summed"], U * e + 2 * w + 2)
                done = c.put(nc.vector.reciprocal(r, o[:, :, HD:HD + 1].rearrange("p b a -> p (b a)")))
                yield
                c.need(done)
                done = c.put(nc.vector.tensor_tensor(r, r, m.gate_scale[:, i, bass.ds(3 * head, 3)], ALU.mult))
                yield
                c.need(done)
                done = c.put(nc.vector.tensor_scalar(a[:, 0, :], o[:, 0, 0:HD], r[:, 0:1], None, ALU.mult))
                yield
                c.need(done)
                done = c.put(nc.vector.scalar_tensor_tensor(out=a[:, 1, :], in0=o[:, 1, 0:HD], scalar=r[:, 1:2],
                                                            in1=a[:, 0, :], op0=ALU.mult, op1=ALU.add))
                yield
                c.need(done)
                nc.vector.scalar_tensor_tensor(out=m.ya[:, i, bass.ds(head, 1), :].rearrange("p a d -> p (a d)"),
                                               in0=o[:, 2, 0:HD], scalar=r[:, 2:3], in1=a[:, 1, :],
                                               op0=ALU.mult, op1=ALU.add).then_inc(q["mixed"], 1)

            def one_pass(e, last):
                for u in range(4, U + 4):
                    if u % 2 == 0:
                        steps = mix(e, u // 2 - 2)
                    if u < U or not last:
                        maxima(*at(e, u))
                    next(steps, None)
                    if u - 1 < U or not last:
                        copies(dve, 1, *at(e, u - 1))
                    next(steps, None)
                    if u % 2 == 1:
                        next(steps, None)

            for u in range(4):
                maxima(0, u)
                if u:
                    copies(dve, 1, 0, u - 1)
            with dve.Fori(0, E - 1) as e:
                c.enter(e, PER)
                one_pass(e, False)
                c.leave(E - 1, PER)
            one_pass(E - 1, True)


def turn_ya(nc, m):
    KA = Q_W // P
    turned = m.sem("ya_turned")
    read = [m.sem("ya_act_read"), m.sem("ya_dve_read")]
    src = m.ya[:, :, :, :].rearrange("p t h d -> p t (h d)")
    with nc.Block() as block:
        @block.tensor
        def _(pe):
            for n in range(2 * KA):
                k, h = n % KA, n // KA
                if n >= 4:
                    pe.wait_ge(read[n % 2], (n - 4) // 2 + 1)
                for j in range(4):
                    mm = nc.tensor.transpose(m.ps[n % 4][:, j * P:(j + 1) * P], src[:, 4 * h + j, k:Q_W:KA],
                                             m.ident[:, :])
                mm.then_inc(turned, 1)

        @block.scalar
        def _(act):
            for n in range(0, 2 * KA, 2):
                k, h = n % KA, n // KA
                act.wait_ge(turned, n + 1)
                nc.scalar.copy(m.yaT[:, k, h * HALF:(h + 1) * HALF], m.ps[n % 4][:, :]).then_inc(read[0], 1)

        @block.vector
        def _(dve):
            for n in range(1, 2 * KA, 2):
                k, h = n % KA, n // KA
                dve.wait_ge(turned, n + 1)
                nc.vector.tensor_copy(m.yaT[:, k, h * HALF:(h + 1) * HALF], m.ps[n % 4][:, :]).then_inc(read[1], 1)


def merge_parts(m):
    return ((KD, BR0, "w_in"), (KD, BR0 + D, "w_in"), (Q_W // P, 0, "w_branch_a"), (KD, 0, "w_branch_b"))


def load_merge(m, eng, part, c):
    kk, c0, name = merge_parts(m)[part]
    src = m.i[name][0][:, c0:c0 + D].rearrange("(p k) (m c) -> m p k c", k=kk, c=P)
    eng.dma_start(m.merge_w[part][:, :, :], src[c, :, :, :]).then_inc(m.merge_w_loaded[part], 16)


def merge(nc, m):
    parts = merge_parts(m)
    PARTS = len(parts)
    W, here = m.merge_w, m.merge_w_loaded
    high_w = [m.sb(f"merge_w_high{n}", [P, kk, P], F32R) for n, (kk, _, _) in enumerate(parts)]
    low_w = [m.part(f"merge_w_low{n}", [P, kk, P], f"merge_w{n}") for n, (kk, _, _) in enumerate(parts)]
    whole = (m.hT, m.yaT, m.ybT)
    low = tuple(m.part(f"{n}_low", x.shape, n) for n, x in zip(("hT", "yaT", "ybT"), whole))
    high = (m.hT_high, m.yaT_high, m.ybT_high)
    source = (0, 0, 1, 2)
    steps = [x.shape[1] for x in whole]
    base = [sum(steps[:x]) for x in range(3)]
    STEPS = sum(steps)
    sg = m.sb("merge_sg", [P, 2, HALF])
    q = {n: m.sem(f"merge_{n}") for n in ("w_split", "high_made", "low_made", "done", "sig_ready", "a_gated",
                                          "b_gated", "merged", "sp_past")}

    def tiles(eng, tile):
        for h in range(2):
            tile(h, 0, True, False)
            with eng.Fori(0, KD - 2) as i:
                tile(h, i + 1, False, False)
            tile(h, KD - 1, False, True)

    with nc.Block() as block:
        @block.sync
        def _(sp):
            def tile(h, c, first, last):
                if h == 1 and last:
                    return
                coming = 0 if last else c + 1
                for part in range(PARTS):
                    sp.wait_ge(q["done"], PARTS * (KD * h + c) + part + 1)
                    sp.sem_inc(q["sp_past"], 1)
                    load_merge(m, sp, part, coming)
            tiles(sp, tile)

        @block.gpsimd
        def _(pool):
            for h in range(2):
                cols = slice(h * HALF, (h + 1) * HALF)
                for x in range(3):
                    for k in range(steps[x]):
                        pool.wait_ge(q["high_made"], STEPS * h + base[x] + k + 1)
                        low_part(nc.gpsimd, low[x][:, k, cols], whole[x][:, k, cols], high[x][:, k, :])\
                            .then_inc(q["low_made"], 1)

        @block.tensor
        def _(pe):
            def tile(h, c, first, last):
                n = KD * h + c
                cols = slice(h * HALF, (h + 1) * HALF)
                for part in range(PARTS):
                    x, kk = source[part], parts[part][0]
                    pe.wait_ge(q["w_split"], 2 * (PARTS * n + part) + 2)
                    if part < 2:
                        pe.wait_ge(q["sig_ready"], 2 * n)
                    else:
                        pe.wait_ge(q["a_gated" if part == 2 else "b_gated"], n)
                    for k in range(kk):
                        if first:
                            pe.wait_ge(q["low_made"], STEPS * h + base[x] + k + 1)
                        mm = split_product(nc, m.ps[part][:, :], (high_w[part][:, k, :], low_w[part][:, k, :]),
                                           (high[x][:, k, :], low[x][:, k, cols]), k == 0, k == kk - 1)
                    mm.then_inc(q["done"], 1)
            tiles(pe, tile)

        @block.scalar
        def _(act):
            def tile(h, c, first, last):
                n = KD * h + c
                for b in range(2):
                    act.wait_ge(q["done"], PARTS * n + b + 1)
                    act.wait_ge(q["merged"], n)
                    nc.scalar.activation(sg[:, b, :], m.ps[b][:, :], ACT.Sigmoid).then_inc(q["sig_ready"], 1)
            tiles(act, tile)

        @block.vector
        def _(dve):
            def split_w(n, part):
                dve.wait_ge(here[part], 16 * (n + 1))
                if not isinstance(n, int) or n > 0:
                    dve.wait_ge(q["done"], PARTS * (n - 1) + part + 1)
                w, hi = W[part][:, :, :], high_w[part][:, :, :]
                high_part(nc.vector, hi, w).then_inc(q["w_split"], 1)
                dve.wait_ge(q["w_split"], 2 * (PARTS * n + part) + 1)
                low_part(nc.vector, low_w[part][:, :, :], w, hi).then_inc(q["w_split"], 1)

            def split_source(h, x):
                if h == 1:
                    dve.wait_ge(q["done"], PARTS * (KD - 1) + {0: 2, 1: 3, 2: 4}[x])
                for k in range(steps[x]):
                    high_part(nc.vector, high[x][:, k, :], whole[x][:, k, h * HALF:(h + 1) * HALF])\
                        .then_inc(q["high_made"], 1)

            def tile(h, c, first, last):
                n = KD * h + c
                at_end = h == 1 and last
                turn = h == 0 and last
                if not at_end:
                    split_w(n + 1, 0)
                    if turn:
                        split_source(1, 0)
                    split_w(n + 1, 1)
                    split_w(n + 1, 2)
                    if turn:
                        split_source(1, 1)
                dve.wait_ge(q["sig_ready"], 2 * n + 1)
                dve.wait_ge(q["done"], PARTS * n + 3)
                nc.vector.tensor_tensor(sg[:, 0, :], sg[:, 0, :], m.ps[2][:, :], ALU.mult).then_inc(q["a_gated"], 1)
                dve.wait_ge(q["sig_ready"], 2 * n + 2)
                dve.wait_ge(q["done"], PARTS * n + 4)
                nc.vector.tensor_tensor(sg[:, 1, :], sg[:, 1, :], m.ps[3][:, :], ALU.mult).then_inc(q["b_gated"], 1)
                dve.wait_ge(q["a_gated"], n + 1)
                dve.wait_ge(q["b_gated"], n + 1)
                dst = m.mergedT[:, c, h * HALF:(h + 1) * HALF] if isinstance(c, int) else \
                    m.mergedT[:, bass.ds(c, 1), h * HALF:(h + 1) * HALF].rearrange("p a n -> p (a n)")
                nc.vector.tensor_tensor(dst, sg[:, 0, :], sg[:, 1, :], ALU.add).then_inc(q["merged"], 1)
                if turn:
                    split_source(1, 2)
                if not at_end:
                    split_w(n + 1, 3)

            split_w(0, 0)
            split_source(0, 0)
            split_w(0, 1)
            split_source(0, 1)
            split_w(0, 2)
            split_source(0, 2)
            split_w(0, 3)
            tiles(dve, tile)


def project_out(nc, m):
    FIRST = 3
    W = m.sb("out_w", [P, KD, D])
    W_low, merged_low = m.part("out_w_low", [P, KD, D], "out_w"), m.part("merged_low", [P, KD, S], "mergedT")
    merged_high = m.part("merged_high", [P, KD, S], "moe_wg")
    W_high = (m.part("out_w_high0", [P, KD // 2, D], "moe_wd"), m.sb("out_w_high1", [P, KD // 2, D], F32R))
    q = {n: m.sem(f"out_{n}") for n in ("high", "low", "done", "read", "squared", "mean_made", "rooted", "normed", "turned",
                                        "hT_ready", "logits")}
    w_here = [m.sem(f"out_w_loaded{k}") for k in range(KD)]
    stored = [m.sem(f"xn_stored{r}") for r in range(2)]
    ch = m.chains(nc, "out")
    with nc.Block() as block:
        @block.sync
        def _(sp):
            for k in range(KD):
                sp.dma_start(W[:, k, :], m.i["w_out"][0][k * P:(k + 1) * P, :]).then_inc(w_here[k], 16)
            for t in range(NT):
                sp.dma_start(m.x2[:, t, :], m.i["x"][0][t * P:(t + 1) * P, :]).then_inc(m.x_loaded, 16)
            sp.dma_start(m.route_w[:, :, 0:MGROUPS], m.i["moe_w_group"][0].rearrange("(p k) n -> p k n", k=KD))\
                .then_inc(m.route_w_loaded, 16)
            sp.dma_start(m.route_w[:, :, MGROUPS:], m.i["moe_w_expert"][0].rearrange("(p k) n -> p k n", k=KD))\
                .then_inc(m.route_w_loaded, 16)
            sp.dma_start(m.pin[:, :, :], m.i["p"][0, 0].rearrange("(t p) n -> p t n", p=P)).then_inc(m.p_loaded, 16)
            for t in range(NT):
                sp.wait_ge(q["normed"], t + 1)
                sp.dma_start(m.xn_dram[t * P:(t + 1) * P, :], m.xn[:, t % 2, :]).then_inc(stored[t % 2], 16)
            for r in range(2):
                sp.wait_ge(stored[r], 16 * NT // 2)

        @block.tensor
        def _(pe):
            def product(t, n, k, bank):
                rows, cols = slice(t * P, (t + 1) * P), slice(n * HALF, (n + 1) * HALF)
                return split_product(nc, m.ps[bank][:, :], (merged_high[:, k, rows], merged_low[:, k, rows]),
                                     (W_high[2 * k // KD][:, k % (KD // 2), cols], W_low[:, k, cols]),
                                     k == 0, k == KD - 1)

            def turn(t):
                pe.wait_ge(q["normed"], t + 1)
                if t:
                    pe.wait_ge(q["hT_ready"], 2 * t)
                for n in range(2):
                    for k in range(4):
                        mm = nc.tensor.transpose(m.ps[6 + n][:, k * P:(k + 1) * P],
                                                 m.xn[:, t % 2, 4 * n + k:D:KD], m.ident[:, :])
                    mm.then_inc(q["turned"], 1)

            def logits(t):
                pe.wait_ge(q["hT_ready"], 2 * t + 2)
                for k in range(KD):
                    nc.tensor.matmul(m.logits[:, t * ROUTES:(t + 1) * ROUTES], m.h2T[:, t % 2, k, :],
                                     m.route_w[:, k, :], start=(k == 0), stop=(k == KD - 1))

            for k in range(KD):
                pe.wait_ge(q["low"], 2 * k + 2)
                for t in range(FIRST):
                    for n in range(2):
                        mm = product(t, n, k, 2 * t + n)
                        if k == KD - 1:
                            mm.then_inc(q["done"], 1)
            turns = {3: (0,), 4: (1, 2), 5: (3, 4), 6: (5,), 7: (6, 7)}
            for t in range(FIRST, NT):
                last = {3: 1, 4: 0}.get(t, t - 2)
                for n in range(2):
                    pe.wait_ge(q["read"], 2 * last + n + 1)
                    for k in range(KD):
                        mm = product(t, n, k, 2 * (t % 2) + n)
                    mm.then_inc(q["done"], 1)
                for u in turns[t]:
                    if u == 1:
                        pe.wait_ge(m.route_w_loaded, 32)
                        pe.wait_ge(q["read"], 2 * FIRST)
                    if u:
                        logits(u - 1)
                    turn(u)
            logits(NT - 1)

        @block.scalar
        def _(act):
            for k in range(KD):
                act.wait_ge(w_here[k], 16)
                nc.scalar.copy(W_high[2 * k // KD][:, k % (KD // 2), :], W[:, k, :]).then_inc(q["high"], 1)
                nc.scalar.copy(merged_high[:, k, :], m.mergedT[:, k, :]).then_inc(q["high"], 1)
            for t in range(NT):
                act.wait_ge(q["read"], 2 * t + 2)
                nc.scalar.activation(m.junk[:, t % 2, :], m.x2[:, t, :], ACT.Square,
                                     accum_out=m.sumsq[:, t:t + 1]).then_inc(q["squared"], 1)
                act.wait_ge(q["mean_made"], t + 1)
                nc.scalar.activation(m.rms[:, t:t + 1], m.rms[:, t:t + 1], ACT.Sqrt).then_inc(q["rooted"], 1)

        @block.vector
        def _(dve):
            c = Chain(dve, ch["dve"])

            def add(t):
                for n in range(2):
                    bank = 2 * t + n if t < FIRST else 2 * (t % 2) + n
                    dve.wait_ge(q["done"], 2 * t + n + 1)
                    part = m.x2[:, t, n * HALF:(n + 1) * HALF]
                    nc.vector.tensor_tensor(part, part, m.ps[bank][:, :], ALU.add).then_inc(q["read"], 1)

            def norm(t):
                dve.wait_ge(q["squared"], t + 1)
                nc.vector.tensor_scalar(m.rms[:, t:t + 1], m.sumsq[:, t:t + 1], 1.0 / D, EPS, ALU.mult,
                                        ALU.add).then_inc(q["mean_made"], 1)
                dve.wait_ge(q["rooted"], t + 1)
                c.link(nc.vector.reciprocal(m.rstd[:, t:t + 1], m.rms[:, t:t + 1]))
                if t >= 2:
                    dve.wait_ge(q["turned"], 2 * (t - 1))
                    dve.wait_ge(stored[t % 2], 16 * (t // 2))
                nc.vector.tensor_scalar(m.xn[:, t % 2, :], m.x2[:, t, :], m.rstd[:, t:t + 1], None,
                                        ALU.mult).then_inc(q["normed"], 1)

            def scale(t):
                for n in range(2):
                    dve.wait_ge(q["turned"], 2 * t + n + 1)
                    nc.vector.tensor_tensor(m.h2T[:, t % 2, 4 * n:4 * n + 4, :],
                                            m.ps[6 + n][:, :].rearrange("p (k n) -> p k n", k=4),
                                            m.moe_gain[:, 4 * n:4 * n + 4].unsqueeze(2).to_broadcast([P, 4, P]),
                                            ALU.mult).then_inc(q["hT_ready"], 1)

            for k in range(KD):
                dve.wait_ge(q["high"], 2 * k + 1)
                low_part(nc.vector, W_low[:, k, :], W[:, k, :], W_high[2 * k // KD][:, k % (KD // 2), :])\
                    .then_inc(q["low"], 1)
                dve.wait_ge(q["high"], 2 * k + 2)
                low_part(nc.vector, merged_low[:, k, :], m.mergedT[:, k, :], merged_high[:, k, :])\
                    .then_inc(q["low"], 1)
            dve.wait_ge(m.x_loaded, 16 * NT)
            for t in range(FIRST):
                add(t)
            norm(0)
            norm(1)
            add(3)
            scale(0)
            norm(2)
            add(4)
            scale(1)
            norm(3)
            scale(2)
            norm(4)
            add(5)
            scale(3)
            norm(5)
            scale(4)
            add(6)
            norm(6)
            scale(5)
            add(7)
            scale(6)
            norm(7)
            scale(7)


def route(nc, m):
    KP = PLE // P
    EARLY = 5
    lg = m.sb("route_logits", [P, NT, ROUTES])
    f = {n: m.sb(f"route_{n}", [P, NT]) for n in ("gmax", "gsum", "grp", "m1", "i1", "m2", "i2", "e2", "den")}
    eg, gm = m.sb("route_eg", [P, NT, MGROUPS]), m.sb("route_gm", [P, NT, MGROUPS])
    el, eq, ex = (m.sb(f"route_{n}", [P, NT, PER_GROUP]) for n in ("el", "eq", "ex"))
    sel = m.sb("route_sel", [P, NT, PER_GROUP, MGROUPS])
    M1, M2, rank, tmp = (m.sb(f"route_{n}", [P, NT, EXPERTS]) for n in ("M1", "M2", "rank", "tmp"))
    M = m.sb("route_M", [P, NT, EXPERTS], BF16)
    bound = m.sb("route_bound", [P, NT - 1])
    past, pastr = m.sb("route_past", [P, EXPERTS, NT - 1]), m.sb("route_pastr", [P, NT, 2, NT - 1])
    iota, iotai = m.sb("route_iota", [P, P]), m.sb("route_iotai", [P, P], I32)
    tok, toki = m.sb("route_tok", [P, NT]), m.sb("route_toki", [P, NT], I32)
    cnt, carry, extra, incl = (m.sb(f"route_{n}", [P, EXPERTS]) for n in ("cnt", "carry", "extra", "incl"))
    r, j, own, pos, slot, more = (m.sb(f"route_{n}", [P, NT, 2]) for n in ("r", "j", "own", "pos", "slot", "more"))
    cmpx = m.sb("route_cmpx", [P, EXTRA, EXPERTS])
    bex = m.sb("route_bex", [P, EXTRA])
    at_row, at_block = m.sb("route_at_row", [P, NT, 2, P], F32R), m.sb("route_at_block", [P, NT, 2, BLOCKS], F32R)
    in_block = m.sb("route_in_block", [P, NT, 2, BLOCKS])
    q = {n: m.sem(f"route_{n}") for n in ("iota", "maxed", "exped", "masks",
                                          "ranked", "placed", "slots_filled",
                                          "proj_w_loaded", "p_turned", "pT_ready", "proj_done", "proj_read")}
    ch = m.chains(nc, "route")
    with nc.Block() as block:
        @block.sync
        def _(sp):
            sp.dma_start(m.ple_wp[:, :, :], m.i["ple_w_proj"][0].rearrange("(p k) n -> p k n", k=KP))\
                .then_inc(q["proj_w_loaded"], 16)
            for r in range(2):
                load_expert_gate_up(m, sp, r, r, m.moe_w_loaded[0][r])
            load_expert_down(m, sp, 0, 0, m.moe_w_loaded[1][0])
            load_ple_gate(m, sp, slice(0, KD // 2))
            sp.wait_ge(q["proj_done"], 2 * NT)
            load_ple_gate(m, sp, slice(KD // 2, KD))

        @block.gpsimd
        def _(pool):
            nc.gpsimd.iota(toki[:, :], pattern=[[P, NT]], base=0, channel_multiplier=1).then_inc(q["iota"], 1)
            nc.gpsimd.iota(iotai[:, :], pattern=[[1, P]], base=0, channel_multiplier=0).then_inc(q["iota"], 1)

        @block.tensor
        def _(pe):
            def turn_p():
                pe.wait_ge(m.p_loaded, 16)
                for n in range(4):
                    k, h = n % KP, n // KP
                    if n >= 2:
                        pe.wait_ge(q["pT_ready"], n - 1)
                    for j in range(4):
                        mm = nc.tensor.transpose(m.ps[6 + n % 2][:, j * P:(j + 1) * P],
                                                 m.pin[:, 4 * h + j, k:PLE:KP], m.ident[:, :])
                    mm.then_inc(q["p_turned"], 1)

            def project_p(t0, t1):
                for t in range(t0, t1):
                    for n in range(2):
                        if t:
                            pe.wait_ge(q["proj_read"], 2 * t + n - 1)
                        for k in range(KP):
                            mm = nc.tensor.matmul(m.ps[6 + n][:, :], m.pT[:, k, t * P:(t + 1) * P],
                                                  m.ple_wp[:, k, n * HALF:(n + 1) * HALF],
                                                  start=(k == 0), stop=(k == KP - 1))
                        mm.then_inc(q["proj_done"], 1)

            turn_p()
            pe.wait_ge(q["pT_ready"], 4)
            pe.wait_ge(q["proj_w_loaded"], 16)
            project_p(0, EARLY)
            pe.wait_ge(q["masks"], 1)
            ranks = m.ps[1][:, 0:NT * EXPERTS].rearrange("p (t e) -> p t e", t=NT)
            nc.tensor.matmul(ranks, m.tri_lt[:, :], M[:, :, :], start=True, stop=False)
            for t in range(NT - 1):
                nc.tensor.matmul(ranks[:, t + 1:, :], m.onesb[:, :],
                                 M[:, t:t + 1, :].to_broadcast([P, NT - 1 - t, EXPERTS]), start=False, stop=(t == NT - 2))
            for t in range(NT):
                mm = nc.tensor.matmul(m.ps[2][:, 0:EXPERTS], m.onesb[:, :], M[:, t, :], start=(t == 0),
                                      stop=(t == NT - 1))
            mm.then_inc(q["ranked"], 1)
            project_p(EARLY, NT)
            pe.wait_ge(q["placed"], 1)
            for t in range(NT):
                for s in range(2):
                    mm = nc.tensor.matmul(m.ps[3][:, 0:BLOCKS], at_row[:, t, s, :], at_block[:, t, s, :],
                                          start=(t == 0 and s == 0), stop=(t == NT - 1 and s == 1))
            mm.then_inc(q["slots_filled"], 1)

        @block.scalar
        def _(act):
            c = Chain(act, ch["act"])
            for n in range(4):
                k, h = n % KP, n // KP
                act.wait_ge(q["p_turned"], n + 1)
                nc.scalar.copy(m.pT[:, k, h * HALF:(h + 1) * HALF], m.ps[6 + n % 2][:, :]).then_inc(q["pT_ready"], 1)
            for t in range(NT):
                if t == EARLY:
                    act.wait_ge(q["maxed"], 2)
                    c.link(nc.scalar.activation(eg[:, :, :], gm[:, :, :], ACT.Exp))
                    nc.scalar.activation(f["e2"][:, :], f["e2"][:, :], ACT.Exp).then_inc(q["exped"], 1)
                for n in range(2):
                    act.wait_ge(q["proj_done"], 2 * t + n + 1)
                    nc.scalar.copy(m.proj[:, t, n * HALF:(n + 1) * HALF], m.ps[6 + n][:, :])\
                        .then_inc(q["proj_read"], 1)

        @block.vector
        def _(dve):
            c = Chain(dve, ch["dve"])
            v = nc.vector

            def wide(ap, n):
                return ap.unsqueeze(2).to_broadcast([P, NT, n])

            def row(ap, n):
                return ap.unsqueeze(1).to_broadcast([P, NT, n])

            def first(out, hit, n):
                c.link(v.scalar_tensor_tensor(out=hit, in0=hit, scalar=-64.0, in1=row(iota[:, 0:n], n),
                                              op0=ALU.mult, op1=ALU.add))
                c.link(v.tensor_reduce(out, hit, axis=AX.X, op=ALU.min))
                c.link(v.tensor_scalar(out, out, 64.0, None, ALU.add))

            dve.wait_ge(q["iota"], 2)
            c.link(v.tensor_copy(iota[:, :], iotai[:, :]))
            c.link(v.tensor_copy(tok[:, :], toki[:, :]))
            c.link(v.tensor_scalar(bound[:, :], iota[:, 1:NT], float(P), None, ALU.mult))
            c.link(v.tensor_tensor(lg[:, :, :], m.logits[:, 0:NT * ROUTES].rearrange("p (t n) -> p t n", t=NT),
                                   row(m.route_bias[:, :], ROUTES), ALU.add))
            g = lg[:, :, 0:MGROUPS]
            c.link(v.tensor_reduce(f["gmax"][:, :], g, axis=AX.X, op=ALU.max))
            v.tensor_tensor(gm[:, :, :], g, wide(f["gmax"][:, :], MGROUPS), ALU.subtract).then_inc(q["maxed"], 1)
            hit = sel[:, :, 0, :]
            c.link(v.tensor_tensor(hit, g, wide(f["gmax"][:, :], MGROUPS), ALU.is_equal))
            first(f["grp"][:, :], hit, MGROUPS)
            c.link(v.tensor_tensor(eq[:, :, 0:MGROUPS], row(iota[:, 0:MGROUPS], MGROUPS),
                                   wide(f["grp"][:, :], MGROUPS), ALU.is_equal))
            c.link(v.tensor_tensor(sel[:, :, :, :],
                                   lg[:, :, MGROUPS:].rearrange("p t (g e) -> p t e g", g=MGROUPS),
                                   eq[:, :, 0:MGROUPS].unsqueeze(2).to_broadcast([P, NT, PER_GROUP, MGROUPS]), ALU.mult))
            c.link(v.tensor_reduce(el[:, :, :], sel[:, :, :, :], axis=AX.X, op=ALU.add))
            c.link(v.tensor_reduce(f["m1"][:, :], el[:, :, :], axis=AX.X, op=ALU.max))
            c.link(v.tensor_tensor(eq[:, :, :], el[:, :, :], wide(f["m1"][:, :], PER_GROUP), ALU.is_equal))
            first(f["i1"][:, :], eq[:, :, :], PER_GROUP)
            c.link(v.tensor_tensor(eq[:, :, :], row(iota[:, 0:PER_GROUP], PER_GROUP), wide(f["i1"][:, :], PER_GROUP),
                                   ALU.is_equal))
            c.link(v.scalar_tensor_tensor(out=ex[:, :, :], in0=eq[:, :, :], scalar=MASK, in1=el[:, :, :],
                                          op0=ALU.mult, op1=ALU.add))
            c.link(v.tensor_reduce(f["m2"][:, :], ex[:, :, :], axis=AX.X, op=ALU.max))
            c.link(v.tensor_tensor(eq[:, :, :], ex[:, :, :], wide(f["m2"][:, :], PER_GROUP), ALU.is_equal))
            first(f["i2"][:, :], eq[:, :, :], PER_GROUP)
            v.tensor_tensor(f["e2"][:, :], f["m2"][:, :], f["m1"][:, :], ALU.subtract).then_inc(q["maxed"], 1)
            for i in ("i1", "i2"):
                c.link(v.scalar_tensor_tensor(out=f[i][:, :], in0=f["grp"][:, :], scalar=float(PER_GROUP), in1=f[i][:, :],
                                              op0=ALU.mult, op1=ALU.add))
            for mask, i in ((M1, "i1"), (M2, "i2")):
                c.link(v.tensor_tensor(mask[:, :, :], row(iota[:, 0:EXPERTS], EXPERTS), wide(f[i][:, :], EXPERTS), ALU.is_equal))
            v.tensor_tensor(M[:, :, :], M1[:, :, :], M2[:, :, :], ALU.add).then_inc(q["masks"], 1)
            dve.wait_ge(q["exped"], 1)
            c.link(v.tensor_reduce(f["gsum"][:, :], eg[:, :, :], axis=AX.X, op=ALU.add))
            c.link(v.scalar_tensor_tensor(out=f["den"][:, :], in0=f["e2"][:, :], scalar=1.0, in1=f["gsum"][:, :],
                                          op0=ALU.add, op1=ALU.mult))
            c.link(v.reciprocal(m.weight[:, :, 0], f["den"][:, :]))
            c.link(v.tensor_tensor(m.weight[:, :, 1], m.weight[:, :, 0], f["e2"][:, :], ALU.mult))
            dve.wait_ge(q["ranked"], 1)
            c.link(v.tensor_copy(rank[:, :, :], m.ps[1][:, 0:NT * EXPERTS].rearrange("p (t e) -> p t e", t=NT)))
            c.link(v.tensor_copy(cnt[:, :], m.ps[2][:, 0:EXPERTS]))
            c.link(v.tensor_tensor(past[:, :, :], cnt[:, :].unsqueeze(2).to_broadcast([P, EXPERTS, NT - 1]),
                                   bound[:, :].unsqueeze(1).to_broadcast([P, EXPERTS, NT - 1]), ALU.is_gt))
            c.link(v.tensor_reduce(extra[:, :], past[:, :, :], axis=AX.X, op=ALU.add))
            c.link(v.tensor_tensor_scan(incl[:, :], m.ones[:, 0:EXPERTS], extra[:, :], 0.0, ALU.mult, ALU.add))
            c.link(v.tensor_tensor(carry[:, :], incl[:, :], extra[:, :], ALU.subtract))
            for s, mask in ((0, M1), (1, M2)):
                c.link(v.tensor_tensor(tmp[:, :, :], mask[:, :, :], rank[:, :, :], ALU.mult))
                c.link(v.tensor_reduce(r[:, :, s], tmp[:, :, :], axis=AX.X, op=ALU.add))
                c.link(v.tensor_tensor(tmp[:, :, :], mask[:, :, :], row(carry[:, :], EXPERTS), ALU.mult))
                c.link(v.tensor_reduce(own[:, :, s], tmp[:, :, :], axis=AX.X, op=ALU.add))
                c.link(v.tensor_copy(pos[:, :, s], f["i1" if s == 0 else "i2"][:, :]))
            c.link(v.tensor_tensor(pastr[:, :, :, :], r[:, :, :].unsqueeze(3).to_broadcast([P, NT, 2, NT - 1]),
                                   bound[:, :].unsqueeze(1).unsqueeze(1).to_broadcast([P, NT, 2, NT - 1]), ALU.is_ge))
            c.link(v.tensor_reduce(j[:, :, :], pastr[:, :, :, :], axis=AX.X, op=ALU.add))
            c.link(v.tensor_scalar(more[:, :, :], r[:, :, :], float(P), None, ALU.is_ge))
            c.link(v.scalar_tensor_tensor(out=r[:, :, :], in0=j[:, :, :], scalar=-float(P), in1=r[:, :, :],
                                          op0=ALU.mult, op1=ALU.add))
            c.link(v.tensor_tensor(own[:, :, :], own[:, :, :], j[:, :, :], ALU.add))
            c.link(v.tensor_scalar(own[:, :, :], own[:, :, :], float(EXPERTS - 1), None, ALU.add))
            c.link(v.tensor_tensor(own[:, :, :], own[:, :, :], pos[:, :, :], ALU.subtract))
            c.link(v.tensor_tensor(own[:, :, :], own[:, :, :], more[:, :, :], ALU.mult))
            c.link(v.tensor_tensor(own[:, :, :], own[:, :, :], pos[:, :, :], ALU.add))
            c.link(v.tensor_tensor(in_block[:, :, :, :], iota[:, 0:BLOCKS].unsqueeze(1).unsqueeze(1)
                                   .to_broadcast([P, NT, 2, BLOCKS]),
                                   own[:, :, :].unsqueeze(3).to_broadcast([P, NT, 2, BLOCKS]), ALU.is_equal))
            c.link(v.tensor_tensor(at_block[:, :, :, :].rearrange("p t s b -> p t (s b)"),
                                   in_block[:, :, :, :].rearrange("p t s b -> p t (s b)"),
                                   wide(tok[:, :], 2 * BLOCKS), ALU.mult))
            v.tensor_tensor(at_row[:, :, :, :], iota[:, :].unsqueeze(1).unsqueeze(1).to_broadcast([P, NT, 2, P]),
                            r[:, :, :].unsqueeze(3).to_broadcast([P, NT, 2, P]), ALU.is_equal).then_inc(q["placed"], 1)
            c.link(v.scalar_tensor_tensor(out=slot[:, :, :], in0=own[:, :, :], scalar=float(P), in1=r[:, :, :],
                                          op0=ALU.mult, op1=ALU.add))
            c.link(v.tensor_copy(m.slot_u[:, :, :], slot[:, :, :]))
            c.link(v.tensor_tensor(cmpx[:, :, :], incl[:, :].unsqueeze(1).to_broadcast([P, EXTRA, EXPERTS]),
                                   iota[:, 0:EXTRA].unsqueeze(2).to_broadcast([P, EXTRA, EXPERTS]), ALU.is_le))
            c.link(v.tensor_reduce(bex[:, :], cmpx[:, :, :], axis=AX.X, op=ALU.add))
            c.link(v.tensor_scalar(bex[:, :], bex[:, :], float(EXPERTS - 1), None, ALU.min))
            c.link(v.tensor_copy(m.plan[:, 0:EXTRA], bex[:, :]))
            c.link(v.tensor_copy(m.plan[:, EXTRA:EXTRA + 1], incl[:, EXPERTS - 1:EXPERTS]))
            dve.wait_ge(q["slots_filled"], 1)
            c.link(v.tensor_copy(m.slot_idx[:, :], m.ps[3][:, 0:BLOCKS]))


def experts(nc, m, name, further):
    KH = MOE_H // P
    wg, wu, wd = m.moe_w
    b = m.moe_buf
    q = {n: [m.sem(f"{name}_{n}{r}") for r in range(2)] for n in (
        "idx_ready", "x_gathered", "turned", "xT_ready", "gu_done", "silu_ready", "h_ready", "down_done", "out_ready",
        "stored", "pool_past")}
    if not further:
        q["w_loaded"], q["wd_loaded"] = m.moe_w_loaded
    else:
        q["w_loaded"], q["wd_loaded"] = ([m.sem(f"{name}_{n}{r}") for r in range(2)] for n in ("w_loaded", "wd_loaded"))
    act_past = m.sem(f"{name}_act_past")
    PASSES = (EXTRA if further else EXPERTS) // 2
    first_block = EXPERTS if further else 0
    out_banks = ((6, 7), (0, 1))

    def passes(eng, body, peel=False):
        if not further:
            with eng.Fori(0, PASSES - 1 if peel else PASSES) as i:
                body(i)
            return
        number = eng.value_load(m.plan[0:1, EXTRA:EXTRA + 1], min_val=0, max_val=EXTRA)
        with eng.Fori(0, PASSES) as i:
            with eng.If(number > 2 * i):
                body(i)
            eng.nop()

    with nc.Block() as block:
        @block.sync
        def _(sp):
            def load_gate_up(r, e):
                load_expert_gate_up(m, sp, r, e, q["w_loaded"][r])

            def load_down(r, e):
                load_expert_down(m, sp, r, e, q["wd_loaded"][r])

            if further:
                def body(i):
                    e = [sp.value_load(m.plan[0:1, bass.ds(2 * i + r, 1)], min_val=0, max_val=EXPERTS - 1)
                         for r in range(2)]
                    for r in range(2):
                        sp.wait_ge(q["gu_done"][r], i)
                        load_gate_up(r, e[r])
                        sp.wait_ge(q["down_done"][r], i)
                        load_down(r, e[r])
                passes(sp, body)
            else:
                def body(i):
                    sp.wait_ge(q["gu_done"][0], i + 1)
                    load_gate_up(0, 2 * i + 2)
                    sp.wait_ge(q["down_done"][1], i)
                    load_down(1, 2 * i + 1)
                    sp.wait_ge(q["gu_done"][1], i + 1)
                    load_gate_up(1, 2 * i + 3)
                    sp.wait_ge(q["down_done"][0], i + 1)
                    load_down(0, 2 * i + 2)
                passes(sp, body, peel=True)
                sp.wait_ge(q["down_done"][1], PASSES - 1)
                load_down(1, EXPERTS - 1)

        @block.gpsimd
        def _(pool):
            def body(i):
                for r in range(2):
                    pool.wait_ge(q["turned"][r], 2 * i)
                    nc.gpsimd.tensor_copy(b["idx"][:, r:r + 1], m.slot_idx[:, bass.ds(2 * i + r + first_block, 1)])\
                        .then_inc(q["idx_ready"][r], 1)
                    pool.wait_ge(q["idx_ready"][r], i + 1)
                    pool.sem_inc(q["pool_past"][r], 1)
                    nc.gpsimd.indirect_dma_start(b["x"][r][:, :], None, m.xn_dram,
                                                 bass.IndirectOffsetOnAxis(ap=b["idx"][:, r:r + 1], axis=0))\
                        .then_inc(q["x_gathered"][r], 16)
            passes(pool, body)

        @block.tensor
        def _(pe):
            def turn(r, i, outs=0):
                pe.wait_ge(q["x_gathered"][r], 16 * (i + 1))
                pe.wait_ge(q["xT_ready"][r], 2 * i)
                if r == 0:
                    pe.wait_ge(q["out_ready"][1], outs)
                for h in range(2):
                    for k in range(4):
                        mm = nc.tensor.transpose(m.ps[2 * r + h][:, k * P:(k + 1) * P],
                                                 b["x"][r][:, 4 * h + k:D:KD], m.ident[:, :])
                    mm.then_inc(q["turned"][r], 1)

            def gate_up(r, i):
                pe.wait_ge(q["w_loaded"][r], 32 * (i + 1))
                pe.wait_ge(q["xT_ready"][r], 2 * i + 2)
                pe.wait_ge(q["h_ready"][r], i)
                for n, w in enumerate((wg, wu)):
                    for c in range(KH):
                        for k in range(KD):
                            mm = nc.tensor.matmul(m.ps[4 + r][:, (KH * n + c) * P:(KH * n + c + 1) * P],
                                                  w[:, r, k, c * P:(c + 1) * P], b["xT"][:, r, k, :],
                                                  start=(k == 0), stop=(k == KD - 1))
                mm.then_inc(q["gu_done"][r], 1)

            def down(r, i, tokens=0):
                pe.wait_ge(q["wd_loaded"][r], 16 * (i + 1))
                pe.wait_ge(q["h_ready"][r], i + 1)
                pe.wait_ge(q["out_ready"][r], i)
                if r == 1:
                    pe.wait_ge(q["xT_ready"][0], tokens)
                for h in range(2):
                    for k in range(KH):
                        mm = nc.tensor.matmul(m.ps[out_banks[r][h]][:, :], b["h"][:, r, k, :],
                                              wd[:, r, k, h * HALF:(h + 1) * HALF],
                                              start=(k == 0), stop=(k == KH - 1))
                mm.then_inc(q["down_done"][r], 1)

            if further:
                def body(i):
                    turn(0, i, outs=i)
                    turn(1, i)
                    gate_up(0, i)
                    gate_up(1, i)
                    down(0, i)
                    down(1, i, tokens=2 * i + 2)
                passes(pe, body)
            else:
                turn(0, 0)
                gate_up(0, 0)
                turn(1, 0)

                def body(i):
                    gate_up(1, i)
                    turn(0, i + 1, outs=i)
                    down(0, i)
                    gate_up(0, i + 1)
                    turn(1, i + 1)
                    down(1, i, tokens=2 * i + 4)
                passes(pe, body, peel=True)
                gate_up(1, PASSES - 1)
                down(0, PASSES - 1)
                down(1, PASSES - 1, tokens=2 * PASSES)

        @block.scalar
        def _(act):
            def silu(r, i):
                act.wait_ge(q["gu_done"][r], i + 1)
                act.wait_ge(q["h_ready"][r], i)
                nc.scalar.activation(b["sg"][:, r, :], m.ps[4 + r][:, 0:MOE_H], ACT.Silu)\
                    .then_inc(q["silu_ready"][r], 1)

            def store(r, i):
                act.wait_ge(q["down_done"][r], i + 1)
                act.wait_ge(q["stored"][r], 16 * i)
                banks = m.psum[:, out_banks[r][0] * HALF:(out_banks[r][1] + 1) * HALF]
                nc.scalar.copy(b["out"][:, r, :], banks).then_inc(q["out_ready"][r], 1)
                act.wait_ge(q["out_ready"][r], i + 1)
                act.dma_start(m.y_slots[bass.ds((2 * i + r + first_block) * P, P), :], b["out"][:, r, :])\
                    .then_inc(q["stored"][r], 16)

            if further:
                def body(i):
                    silu(0, i)
                    silu(1, i)
                    store(0, i)
                    store(1, i)
                    for r in range(2):
                        act.wait_ge(q["stored"][r], 16 * (i + 1))
                    act.sem_inc(act_past, 1)
                passes(act, body)
            else:
                silu(0, 0)

                def body(i):
                    silu(1, i)
                    store(0, i)
                    silu(0, i + 1)
                    store(1, i)
                passes(act, body, peel=True)
                silu(1, PASSES - 1)
                store(0, PASSES - 1)
                store(1, PASSES - 1)
                for r in range(2):
                    act.wait_ge(q["stored"][r], 16 * PASSES)

        @block.vector
        def _(dve):
            def scale(r, i):
                for h in range(2):
                    dve.wait_ge(q["turned"][r], 2 * i + h + 1)
                    dve.wait_ge(q["gu_done"][r], i)
                    nc.vector.tensor_tensor(b["xT"][:, r, 4 * h:4 * h + 4, :],
                                            m.ps[2 * r + h][:, :].rearrange("p (k n) -> p k n", k=4),
                                            m.moe_gain[:, 4 * h:4 * h + 4].unsqueeze(2).to_broadcast([P, 4, P]),
                                            ALU.mult).then_inc(q["xT_ready"][r], 1)

            def hidden(r, i):
                dve.wait_ge(q["silu_ready"][r], i + 1)
                dve.wait_ge(q["down_done"][r], i)
                nc.vector.tensor_tensor(b["h"][:, r, :, :].rearrange("p k n -> p (k n)"), b["sg"][:, r, :],
                                        m.ps[4 + r][:, MOE_H:2 * MOE_H], ALU.mult).then_inc(q["h_ready"][r], 1)

            if further:
                def body(i):
                    scale(0, i)
                    scale(1, i)
                    hidden(0, i)
                    hidden(1, i)
                passes(dve, body)
            else:
                scale(0, 0)
                hidden(0, 0)
                scale(1, 0)

                def body(i):
                    hidden(1, i)
                    scale(0, i + 1)
                    hidden(0, i + 1)
                    scale(1, i + 1)
                passes(dve, body, peel=True)
                hidden(1, PASSES - 1)


def load_expert_gate_up(m, eng, r, e, loaded):
    wg, wu, _ = m.moe_w
    for w, name in ((wg, "moe_w_gate"), (wu, "moe_w_up")):
        eng.dma_start(w[:, r, :, :], m.i[name][0][e, :, :].rearrange("(p k) n -> p k n", k=KD)).then_inc(loaded, 16)


def load_ple_gate(m, eng, ks):
    eng.dma_start(m.ple_wg[:, ks, :], m.i["ple_w_gate"][0].rearrange("(p k) n -> p k n", k=KD)[:, ks, :])\
        .then_inc(m.ple_loaded, 16)


def load_expert_down(m, eng, r, e, loaded):
    eng.dma_start(m.moe_w[2][:, r, :, :], m.i["moe_w_down"][0][e, :, :].rearrange("(k p) n -> p k n", k=MOE_H // P))\
        .then_inc(loaded, 16)


def finish(nc, m):
    RING = 3
    rows = m.sb("finish_rows", [P, RING, 2, D])
    xn = m.sb("finish_xn", [P, D])
    hT = m.sb("finish_hT", [P, 2, KD, P])
    sg = m.sb("finish_sg", [P, D])
    res = m.sb("finish_res", [P, D])
    m.top = m.above
    wg_high, hT_high = m.sb("finish_wg_high", [P, KD, D], F32R), m.sb("finish_hT_high", [P, 2, KD, P], F32R)
    wg_low, hT_low = m.part("finish_wg_low", [P, KD, D], "ple_wg"), m.part("finish_hT_low", [P, 2, KD, P], "finish_hT")
    gathered = [m.sem(f"finish_gathered{r}{s}") for r in range(RING) for s in range(2)]
    stored = m.sem("finish_stored")
    q = {n: m.sem(f"finish_{n}") for n in ("added", "squared", "mean_made", "rooted", "normed", "turned", "hT_ready",
                                           "gate_done", "sig_ready", "summed", "w_high", "w_low", "hT_high", "hT_low")}
    ch = m.chains(nc, "finish")
    with nc.Block() as block:
        @block.gpsimd
        def _(pool):
            for t in range(NT):
                if t >= RING:
                    pool.wait_ge(q["added"], 2 * (t - RING + 1))
                for s in range(2):
                    nc.gpsimd.indirect_dma_start(rows[:, t % RING, s, :], None, m.y_slots,
                                                 bass.IndirectOffsetOnAxis(ap=m.slot_u[:, t, s:s + 1], axis=0))\
                        .then_inc(gathered[2 * (t % RING) + s], 16)

        @block.sync
        def _(sp):
            for t in range(NT):
                sp.wait_ge(q["summed"], t + 1)
                sp.dma_start(m.out[0, t * P:(t + 1) * P, :], res[:, :]).then_inc(stored, 16)
            sp.wait_ge(stored, 16 * NT)

        @block.tensor
        def _(pe):
            def turn(t):
                pe.wait_ge(q["normed"], t + 1)
                if t:
                    pe.wait_ge(q["hT_ready"], 2 * t)
                for n in range(2):
                    for k in range(4):
                        mm = nc.tensor.transpose(m.ps[n][:, k * P:(k + 1) * P], xn[:, 4 * n + k:D:KD], m.ident[:, :])
                    mm.then_inc(q["turned"], 1)

            turn(0)
            for t in range(NT):
                pe.wait_ge(q["hT_low"], t + 1)
                if t >= 2:
                    pe.wait_ge(q["sig_ready"], 2 * (t - 1))
                for n in range(2):
                    cols = slice(n * HALF, (n + 1) * HALF)
                    for k in range(KD):
                        if t == 0 and n == 0:
                            pe.wait_ge(q["w_low"], k + 1)
                        mm = split_product(nc, m.ps[2 + 2 * (t % 2) + n][:, :],
                                           (hT_high[:, t % 2, k, :], hT_low[:, t % 2, k, :]),
                                           (wg_high[:, k, cols], wg_low[:, k, cols]), k == 0, k == KD - 1)
                    mm.then_inc(q["gate_done"], 1)
                    if n == 0 and t < NT - 1:
                        turn(t + 1)

        @block.scalar
        def _(act):
            def root(t):
                act.wait_ge(q["added"], 2 * t + 2)
                nc.scalar.activation(m.junk[:, t % 2, :], m.x2[:, t, :], ACT.Square,
                                     accum_out=m.sumsq[:, t:t + 1]).then_inc(q["squared"], 1)
                act.wait_ge(q["mean_made"], t + 1)
                nc.scalar.activation(m.rms[:, t:t + 1], m.rms[:, t:t + 1], ACT.Sqrt).then_inc(q["rooted"], 1)

            def split_w(k0, k1):
                for k in range(k0, k1):
                    nc.scalar.copy(wg_high[:, k, :], m.ple_wg[:, k, :]).then_inc(q["w_high"], 1)

            def split_hT(t):
                if t >= 2:
                    act.wait_ge(q["gate_done"], 2 * (t - 1))
                act.wait_ge(q["hT_ready"], 2 * t + 2)
                nc.scalar.copy(hT_high[:, t % 2, :, :], hT[:, t % 2, :, :]).then_inc(q["hT_high"], 1)

            act.wait_ge(m.ple_loaded, 32)
            split_w(0, KD // 2)
            root(0)
            split_w(KD // 2, KD)
            split_hT(0)
            root(1)
            for t in range(NT):
                for n in range(2):
                    if n == 1 and t + 1 < NT:
                        split_hT(t + 1)
                    if n == 1 and t + 2 < NT:
                        root(t + 2)
                    act.wait_ge(q["gate_done"], 2 * t + n + 1)
                    if t:
                        act.wait_ge(q["summed"], t)
                    nc.scalar.activation(sg[:, n * HALF:(n + 1) * HALF], m.ps[2 + 2 * (t % 2) + n][:, :],
                                         ACT.Sigmoid).then_inc(q["sig_ready"], 1)

        @block.vector
        def _(dve):
            c = Chain(dve, ch["dve"])

            def mean(t):
                for s in range(2):
                    dve.wait_ge(gathered[2 * (t % RING) + s], 16 * (t // RING + 1))
                    if s:
                        dve.wait_ge(q["added"], 2 * t + 1)
                    nc.vector.scalar_tensor_tensor(out=m.x2[:, t, :], in0=rows[:, t % RING, s, :],
                                                   scalar=m.weight[:, t, s:s + 1], in1=m.x2[:, t, :],
                                                   op0=ALU.mult, op1=ALU.add).then_inc(q["added"], 1)
                dve.wait_ge(q["squared"], t + 1)
                nc.vector.tensor_scalar(m.rms[:, t:t + 1], m.sumsq[:, t:t + 1], 1.0 / D, EPS, ALU.mult,
                                        ALU.add).then_inc(q["mean_made"], 1)
                dve.wait_ge(q["rooted"], t + 1)
                c.link(nc.vector.reciprocal(m.rstd[:, t:t + 1], m.rms[:, t:t + 1]))

            def norm(t):
                if t:
                    dve.wait_ge(q["turned"], 2 * t)
                nc.vector.tensor_scalar(xn[:, :], m.x2[:, t, :], m.rstd[:, t:t + 1], None,
                                        ALU.mult).then_inc(q["normed"], 1)

            def split_w(k0, k1):
                for k in range(k0, k1):
                    dve.wait_ge(q["w_high"], k + 1)
                    low_part(nc.vector, wg_low[:, k, :], m.ple_wg[:, k, :], wg_high[:, k, :]).then_inc(q["w_low"], 1)

            def scale(t):
                if t >= 2:
                    dve.wait_ge(q["gate_done"], 2 * (t - 1))
                for n in range(2):
                    dve.wait_ge(q["turned"], 2 * t + n + 1)
                    nc.vector.tensor_tensor(hT[:, t % 2, 4 * n:4 * n + 4, :],
                                            m.ps[n][:, :].rearrange("p (k n) -> p k n", k=4),
                                            m.ple_gain[:, 4 * n:4 * n + 4].unsqueeze(2).to_broadcast([P, 4, P]),
                                            ALU.mult).then_inc(q["hT_ready"], 1)
                dve.wait_ge(q["hT_high"], t + 1)
                low_part(nc.vector, hT_low[:, t % 2, :, :], hT[:, t % 2, :, :], hT_high[:, t % 2, :, :])\
                    .then_inc(q["hT_low"], 1)

            split_w(0, KD // 2)
            mean(0)
            norm(0)
            scale(0)
            split_w(KD // 2, KD)
            mean(1)
            norm(1)
            for t in range(NT):
                if t + 1 < NT:
                    scale(t + 1)
                if t + 2 < NT:
                    mean(t + 2)
                    norm(t + 2)
                dve.wait_ge(q["sig_ready"], 2 * t + 2)
                dve.wait_ge(stored, 16 * t)
                c.link(nc.vector.tensor_tensor(res[:, :], sg[:, :], m.proj[:, t, :], ALU.mult))
                nc.vector.tensor_tensor(res[:, :], res[:, :], m.x2[:, t, :], ALU.add).then_inc(q["summed"], 1)


def phase_constants(nc, m):
    m.xn_dram = nc.dram_tensor("xn_rows", [S, D], F32).ap()
    m.y_slots = nc.dram_tensor("y_slots", [SLOTS, D], F32).ap()
    constants(nc, m)


def phase_mix_norm(nc, m):
    m.xbc = m.sb("xbc", [P, MC, S])
    m.y = m.sb("y", [P, NT, INNER])
    m.dt = m.sb("dt", [P, NT, SSM_HEADS])
    m.adt = m.sb("adt", [P, NT + 1, SSM_HEADS])
    m.wz = m.sb("wz", [P, KD, INNER])
    m.ssd_base = m.top
    m.conv_ring = m.sb("conv_ring", [P, 3, KD, P])
    m.dt_w = m.sb("dt_w", [P, KD, SSM_HEADS])
    m.conv_w_loaded = [m.sem(f"conv_w_loaded{r}") for r in range(3)]
    m.dt_w_loaded, m.wz_loaded = m.sem("dt_w_loaded"), m.sem("wz_loaded")
    norm_transpose(nc, m, m.x_in, m.mix_gain, m.hT)


def phase_ssm(nc, m):
    project_conv(nc, m)
    m.top = m.ssd_base
    ssd(nc, m)
    m.nsa_w, m.nsa_w_at = m.sb_at_end("nsa_w", [P, KD, NSA_W])
    end, m.end = m.end, m.nsa_w_at
    m.nsa_hc, m.nsa_hc_at = m.sb_at_end("nsa_hc", [P, 2, KD, P])
    m.end = end
    m.nsa_w_loaded, m.nsa_hc_ready = m.sem("nsa_w_loaded"), m.sem("nsa_hc_ready")
    m.top = m.base
    m.ybT = m.sb("ybT", [P, KD, S])
    keep, m.top = m.top, m.ssd_base - 4 * KD * INNER
    group_norm(nc, m, m.ybT)
    m.top = m.base = keep


def phase_nsa(nc, m):
    m.yaT = m.sb("yaT", [P, Q_W // P, S])
    m.top = m.base
    JP = CMP_BLOCK // 2
    m.cmp_w = (m.sb("cmp_w1", [P, 2, JP, CMP_HIDDEN]), None, None)
    m.base = m.top
    m.qT = m.sb("qT", [P, E, S])
    m.ksT, m.kwT = m.sb("ksT", [P, S]), m.sb("kwT", [P, S])
    m.v_sel, m.v_win = m.sb("v_sel", [P, NT, GROUPS, HD + 1]), m.sb("v_win", [P, NT, GROUPS, HD + 1])
    m.cT = m.sb("cT", [P, 2, S])
    m.kcT = m.sb("kcT", [P, NCMP])
    m.v_cmp = m.sb("v_cmp", [NCMP, GROUPS, HD + 1])
    keep = m.top
    m.cmp_w = (m.cmp_w[0], m.sb("cmp_w2", [P, 2, HD]), m.sb("cmp_pos", [JP, 2, P]))
    m.cmp_loaded = m.sem("cmp_loaded")
    nsa_base = m.top
    nsa_project(nc, m)
    assert m.top <= m.nsa_hc_at
    m.top = nsa_base
    compress(nc, m)
    m.top = keep
    m.ya = m.sb("ya", [P, NT, HEADS, HD])
    m.merge_w, end = [], m.end
    for n, (kk, _, _) in enumerate(merge_parts(m)):
        w, m.end = m.sb_at_end(f"merge_w{n}", [P, kk, P])
        m.merge_w.append(w)
    m.merge_w_at, m.end = m.end, end
    m.merge_w_loaded = [m.lasting_sem(f"merge_w_loaded{n}") for n in range(len(m.merge_w))]
    attention(nc, m)
    assert m.top <= m.merge_w_at
    turn_ya(nc, m)
    m.renew_semaphores()
    m.top = m.base


def phase_merge(nc, m):
    x2_at = m.top
    m.x2 = m.sb("x2", [P, NT, D])
    m.x_loaded = m.sem("x_loaded")
    m.weight = m.sb("weight", [P, NT, 2])
    m.slot_u = m.sb("slot_u", [P, NT, 2], U32)
    m.slot_idx = m.sb("slot_idx", [P, BLOCKS], U32)
    m.plan = m.sb("plan", [P, EXTRA + 1], I32)
    m.above = m.top
    m.mergedT = m.sb("mergedT", [P, KD, S])
    keep = m.top
    m.top = x2_at
    m.hT_high, m.ybT_high = (m.sb(f"{n}_high", [P, KD, HALF], F32R) for n in ("hT", "ybT"))
    m.top = keep
    m.yaT_high = m.sb("yaT_high", [P, Q_W // P, HALF], F32R)
    merge(nc, m)
    assert m.top <= m.merge_w_at
    m.top = m.low
    m.xn = m.sb("xn", [P, 2, D])
    m.h2T = m.sb("h2T", [P, 2, KD, P])
    m.pin = m.sb("ple_in", [P, NT, PLE])
    pT_at = m.top
    m.route_w = m.sb("route_w", [P, KD, ROUTES])
    m.top = pT_at
    m.pT = m.sb("ple_pT", [P, PLE // P, S])
    m.tail = m.top
    m.moe_w = (m.sb("moe_wg", [P, 2, KD, MOE_H]), m.sb("moe_wu", [P, 2, KD, MOE_H]),
               m.sb("moe_wd", [P, 2, MOE_H // P, D]))
    m.moe_w_loaded = [[m.sem(f"moe_first_{n}{r}") for r in range(2)] for n in ("w_loaded", "wd_loaded")]
    m.route_w_loaded, m.p_loaded = m.sem("route_w_loaded"), m.sem("p_loaded")
    m.logits = m.ps[4]
    m.top = keep
    project_out(nc, m)
    m.top = m.above


def phase_route(nc, m):
    m.proj = m.sb("proj", [P, NT, D])
    m.above = m.top
    keep, m.top = m.top, m.low
    m.ple_wg = m.sb("ple_wg", [P, KD, D])
    assert m.top == m.tail
    m.ple_loaded = m.sem("ple_loaded")
    m.top = keep
    m.ple_wp = m.sb("ple_wp", [P, PLE // P, D])
    route(nc, m)
    m.top = m.above


def phase_experts(nc, m):
    m.top = m.above
    m.moe_buf = {"idx": m.sb("moe_idx", [P, 2], U32), "x": [m.sb(f"moe_x{r}", [P, D]) for r in range(2)],
                 "xT": m.sb("moe_xT", [P, 2, KD, P]), "sg": m.sb("moe_sg", [P, 2, MOE_H]),
                 "h": m.sb("moe_h", [P, 2, MOE_H // P, P]), "out": m.sb("moe_out", [P, 2, D])}
    experts(nc, m, "moe_first", False)
    experts(nc, m, "moe_more", True)


def phase_finish(nc, m):
    m.top = m.tail
    finish(nc, m)


PHASES = [phase_constants, phase_mix_norm, phase_ssm, phase_nsa, phase_merge, phase_route, phase_experts, phase_finish]


def program(nc, ins, out):
    m = Machine(nc, ins, out)
    for phase in PHASES:
        phase(nc, m)


def kernel(**inputs):
    import numpy as np
    from concourse import bacc
    from concourse.bass_utils import run_bass_kernel_spmd

    nc = bacc.Bacc("TRN2", target_bir_lowering=False, num_devices=1)
    arrays, ins = {}, {}
    for name, value in inputs.items():
        a = np.ascontiguousarray(value)
        arrays[f"in_{name}"] = a
        ins[name] = nc.dram_tensor(f"in_{name}", a.shape, mybir.dt.from_np(a.dtype), kind="ExternalInput").ap()
    out = nc.dram_tensor("out", (1, S, D), F32, kind="ExternalOutput").ap()
    program(nc, ins, out)
    r = run_bass_kernel_spmd(nc, [arrays], core_ids=[0])
    return r.results[0]["out"]
```
